# Optimizing a Trainium2 kernel written in Bass

```python
import math
import jax, jax.numpy as jnp
from jax import lax
import numpy as np

D_MODEL = 1024
BATCH = 1
SEQ = 256
DEPTH = 2

D_MIX = D_MODEL
CONV_CH = D_MIX // 4
CONV_WIDTH = 31
MLA_HEADS = 6
MLA_NOPE = 64
MLA_ROPE = 32
MLA_V = 64
MLA_Q_RANK = 256
MLA_KV_RANK = 128
DIFF_HEADS = 6
DIFF_HD = 32
DIFF_V = 2 * DIFF_HD
IN_COLS = 2 * CONV_CH + MLA_Q_RANK + MLA_KV_RANK + MLA_ROPE + 3 * DIFF_HEADS * DIFF_V
D_FF = 2816
N_EXPERTS = 8
TOP_K = 2
N_DENSE = (DEPTH + 1) // 2
N_MOE = DEPTH // 2
Q_BLOCK = 128
ROPE_THETA = 10000.0
RMS_EPS = 1e-6
LN_EPS = 1e-5

kernel_name = 'hybrid_conv_mla_diffattn_moe'

def rms_norm(x, g, eps=RMS_EPS):
    xf = x.astype(jnp.float32)
    y = xf * lax.rsqrt(jnp.mean(xf * xf, axis=-1, keepdims=True) + eps)
    return (y * g.astype(jnp.float32)).astype(x.dtype)

def layer_norm(x, g, b, eps=LN_EPS):
    xf = x.astype(jnp.float32)
    mu = jnp.mean(xf, axis=-1, keepdims=True)
    var = jnp.mean(jnp.square(xf - mu), axis=-1, keepdims=True)
    y = (xf - mu) * lax.rsqrt(var + eps)
    return (y * g.astype(jnp.float32) + b.astype(jnp.float32)).astype(x.dtype)

def apply_rope(x, pos):
    half = x.shape[-1] // 2
    freq = ROPE_THETA ** (-jnp.arange(half, dtype=jnp.float32) / half)
    ang = pos.astype(jnp.float32)[:, None] * freq[None, :]
    cos = jnp.cos(ang).astype(x.dtype)
    sin = jnp.sin(ang).astype(x.dtype)
    x1, x2 = x[..., :half], x[..., half:]
    return jnp.concatenate([x1 * cos - x2 * sin, x1 * sin + x2 * cos], axis=-1)

def alibi_slopes(n_heads):
    return 2.0 ** (-8.0 * jnp.arange(1, n_heads + 1, dtype=jnp.float32) / n_heads)

def causal_block_scores(q_blk, k_ctx, q_start, scale, slopes=None):
    s = jnp.einsum('bhqd,bhkd->bhqk', q_blk, k_ctx).astype(jnp.float32) * scale
    q_pos = q_start + jnp.arange(q_blk.shape[2])
    k_pos = jnp.arange(k_ctx.shape[2])
    dist = q_pos[:, None] - k_pos[None, :]
    if slopes is not None:
        s = s - slopes[:, None, None] * dist.astype(jnp.float32)[None]
    return jnp.where(dist >= 0, s, -jnp.inf)

def mla_attention(q, k, v):
    S = q.shape[2]
    scale = (MLA_NOPE + MLA_ROPE) ** -0.5
    outs = []
    for i in range(S // Q_BLOCK):
        start, end = i * Q_BLOCK, (i + 1) * Q_BLOCK
        p = jax.nn.softmax(causal_block_scores(q[:, :, start:end], k[:, :, :end], start, scale), axis=-1)
        outs.append(jnp.einsum('bhqk,bhkd->bhqd', p.astype(v.dtype), v[:, :, :end]))
    return jnp.concatenate(outs, axis=2)

def diff_attention(q1, q2, k1, k2, v, lam):
    S = q1.shape[2]
    scale = DIFF_HD ** -0.5
    slopes = alibi_slopes(DIFF_HEADS)
    outs = []
    for i in range(S // Q_BLOCK):
        start, end = i * Q_BLOCK, (i + 1) * Q_BLOCK
        p1 = jax.nn.softmax(causal_block_scores(q1[:, :, start:end], k1[:, :, :end], start, scale, slopes), axis=-1)
        p2 = jax.nn.softmax(causal_block_scores(q2[:, :, start:end], k2[:, :, :end], start, scale, slopes), axis=-1)
        a = p1 - lam * p2
        outs.append(jnp.einsum('bhqk,bhkd->bhqd', a.astype(v.dtype), v[:, :, :end]))
    return jnp.concatenate(outs, axis=2)

def conv_module(a, b_glu, w_dw, b_dw, ln_g, ln_b, w_pw, b_pw):
    a = a + b_glu
    u = a[..., :CONV_CH] * jax.nn.sigmoid(a[..., CONV_CH:])
    c = lax.conv_general_dilated(
        u, w_dw[:, None, :].astype(u.dtype), window_strides=(1,),
        padding=[(CONV_WIDTH - 1, 0)], dimension_numbers=('NWC', 'WIO', 'NWC'),
        feature_group_count=CONV_CH) + b_dw
    c = jax.nn.silu(layer_norm(c, ln_g, ln_b))
    return c @ w_pw + b_pw

def swiglu(h, w_gate, w_up, w_down):
    return (jax.nn.silu(h @ w_gate) * (h @ w_up)) @ w_down

def moe_ffn(h, w_router, w_gate, w_up, w_down):
    B, S, D = h.shape
    hf = h.reshape(B * S, D)
    logits = (hf @ w_router).astype(jnp.float32)
    top_vals, top_idx = lax.top_k(logits, TOP_K)
    top_w = jax.nn.softmax(top_vals, axis=-1)
    gates = jnp.einsum('nk,nke->ne', top_w, jax.nn.one_hot(top_idx, N_EXPERTS, dtype=jnp.float32))
    out = jnp.zeros_like(hf)
    for e in range(N_EXPERTS):
        out = out + gates[:, e:e + 1].astype(hf.dtype) * swiglu(hf, w_gate[e], w_up[e], w_down[e])
    return out.reshape(B, S, D)

def hybrid_mixer(h, layer_idx, w_in, b_glu, w_dw, b_dw, conv_ln_g, conv_ln_b, w_pw, b_pw,
                 q_norm, w_uq, kv_norm, w_ukv, lambda_q1, lambda_k1, lambda_q2, lambda_k2,
                 diff_subln, w_out):
    B, S, _ = h.shape
    pos = jnp.arange(S)
    proj = h @ w_in
    cuts = [int(c) for c in np.cumsum([2 * CONV_CH, MLA_Q_RANK, MLA_KV_RANK, MLA_ROPE,
                                        DIFF_HEADS * DIFF_V, DIFF_HEADS * DIFF_V])]
    conv_in, c_q, c_kv, k_r, d_q, d_k, d_v = jnp.split(proj, cuts, axis=-1)

    y_conv = conv_module(conv_in, b_glu, w_dw, b_dw, conv_ln_g, conv_ln_b, w_pw, b_pw)

    q = (rms_norm(c_q, q_norm) @ w_uq).reshape(B, S, MLA_HEADS, MLA_NOPE + MLA_ROPE).transpose(0, 2, 1, 3)
    q = jnp.concatenate([q[..., :MLA_NOPE], apply_rope(q[..., MLA_NOPE:], pos)], axis=-1)
    kv = (rms_norm(c_kv, kv_norm) @ w_ukv).reshape(B, S, MLA_HEADS, MLA_NOPE + MLA_V).transpose(0, 2, 1, 3)
    k_rope = apply_rope(k_r[:, None], pos)
    k = jnp.concatenate([kv[..., :MLA_NOPE], jnp.broadcast_to(k_rope, (B, MLA_HEADS, S, MLA_ROPE))], axis=-1)
    v = kv[..., MLA_NOPE:]
    y_mla = mla_attention(q, k, v).transpose(0, 2, 1, 3).reshape(B, S, MLA_HEADS * MLA_V)

    def heads(t):
        return t.reshape(B, S, DIFF_HEADS, DIFF_V).transpose(0, 2, 1, 3)
    dq, dk, dv = heads(d_q), heads(d_k), heads(d_v)
    lam_init = 0.8 - 0.6 * math.exp(-0.3 * layer_idx)
    lam = (jnp.exp(jnp.sum(lambda_q1.astype(jnp.float32) * lambda_k1.astype(jnp.float32)))
           - jnp.exp(jnp.sum(lambda_q2.astype(jnp.float32) * lambda_k2.astype(jnp.float32)))
           + lam_init)
    o = diff_attention(dq[..., :DIFF_HD], dq[..., DIFF_HD:], dk[..., :DIFF_HD], dk[..., DIFF_HD:], dv, lam)
    o = rms_norm(o, diff_subln, LN_EPS) * (1.0 - lam_init)
    y_diff = o.transpose(0, 2, 1, 3).reshape(B, S, DIFF_HEADS * DIFF_V)

    return jnp.concatenate([y_conv, y_mla, y_diff], axis=-1) @ w_out

def setup_inputs(seed: int = 0) -> dict:
    key = jax.random.key(seed)
    ks = list(jax.random.split(key, 32))

    def nrm(shape, scale):
        return scale * jax.random.normal(ks.pop(), shape, jnp.float32)

    def gain(shape):
        return 1.0 + nrm(shape, 0.02)

    D, C, L = D_MODEL, CONV_CH, DEPTH
    return {
        'x': nrm((BATCH, SEQ, D), 1.0),
        'attn_norm': gain((L, D)),
        'w_in': nrm((L, D, IN_COLS), D ** -0.5),
        'b_glu': nrm((L, 2 * C), 0.02),
        'w_dw': nrm((L, CONV_WIDTH, C), CONV_WIDTH ** -0.5),
        'b_dw': nrm((L, C), 0.02),
        'conv_ln_g': gain((L, C)),
        'conv_ln_b': nrm((L, C), 0.02),
        'w_pw': nrm((L, C, C), C ** -0.5),
        'b_pw': nrm((L, C), 0.02),
        'q_norm': gain((L, MLA_Q_RANK)),
        'w_uq': nrm((L, MLA_Q_RANK, MLA_HEADS * (MLA_NOPE + MLA_ROPE)), MLA_Q_RANK ** -0.5),
        'kv_norm': gain((L, MLA_KV_RANK)),
        'w_ukv': nrm((L, MLA_KV_RANK, MLA_HEADS * (MLA_NOPE + MLA_V)), MLA_KV_RANK ** -0.5),
        'lambda_q1': nrm((L, DIFF_HD), 0.1),
        'lambda_k1': nrm((L, DIFF_HD), 0.1),
        'lambda_q2': nrm((L, DIFF_HD), 0.1),
        'lambda_k2': nrm((L, DIFF_HD), 0.1),
        'diff_subln': gain((L, DIFF_V)),
        'w_out': nrm((L, D_MIX, D), D_MIX ** -0.5),
        'ffn_norm': gain((L, D)),
        'w_gate_dense': nrm((N_DENSE, D, D_FF), D ** -0.5),
        'w_up_dense': nrm((N_DENSE, D, D_FF), D ** -0.5),
        'w_down_dense': nrm((N_DENSE, D_FF, D), D_FF ** -0.5),
        'w_router': nrm((N_MOE, D, N_EXPERTS), D ** -0.5),
        'w_gate_exp': nrm((N_MOE, N_EXPERTS, D, D_FF), D ** -0.5),
        'w_up_exp': nrm((N_MOE, N_EXPERTS, D, D_FF), D ** -0.5),
        'w_down_exp': nrm((N_MOE, N_EXPERTS, D_FF, D), D_FF ** -0.5),
        'final_norm': gain((D,)),
    }

def reference(x, attn_norm, w_in, b_glu, w_dw, b_dw, conv_ln_g, conv_ln_b, w_pw, b_pw,
              q_norm, w_uq, kv_norm, w_ukv, lambda_q1, lambda_k1, lambda_q2, lambda_k2,
              diff_subln, w_out, ffn_norm, w_gate_dense, w_up_dense, w_down_dense,
              w_router, w_gate_exp, w_up_exp, w_down_exp, final_norm):
    for l in range(DEPTH):
        h = rms_norm(x, attn_norm[l])
        x = x + hybrid_mixer(h, l, w_in[l], b_glu[l], w_dw[l], b_dw[l], conv_ln_g[l], conv_ln_b[l],
                             w_pw[l], b_pw[l], q_norm[l], w_uq[l], kv_norm[l], w_ukv[l],
                             lambda_q1[l], lambda_k1[l], lambda_q2[l], lambda_k2[l],
                             diff_subln[l], w_out[l])
        h = rms_norm(x, ffn_norm[l])
        j = l // 2
        if l % 2 == 0:
            x = x + swiglu(h, w_gate_dense[j], w_up_dense[j], w_down_dense[j])
        else:
            x = x + moe_ffn(h, w_router[j], w_gate_exp[j], w_up_exp[j], w_down_exp[j])
    return rms_norm(x, final_norm)


_drawn_inputs = setup_inputs


def setup_inputs(seed=0):
    import zlib

    import numpy as np

    out = dict(_drawn_inputs(seed))
    spreads = {}
    factors = {'b_glu': 3.384,
     'conv_ln_g': 3.262,
     'conv_ln_b': 9.226,
     'q_norm': 8.0,
     'kv_norm': 7.732,
     'final_norm': 26.765,
     'b_pw': 6.217,
     'diff_subln': 4.838,
     'ffn_norm': 3.218}
    for name, (base, spread) in spreads.items():
        noise = np.random.default_rng([zlib.crc32(name.encode()), seed]).standard_normal(out[name].shape)
        drawn = base * np.exp(spread * noise) if base else spread * noise
        out[name] = __import__('jax').numpy.asarray(drawn.astype(out[name].dtype))
    for name, factor in factors.items():
        out[name] = (out[name] * factor).astype(out[name].dtype)
    return out
```

```python
import math
from contextlib import ExitStack

import numpy as np

import concourse.bass as bass
from concourse import mybir

ALU = mybir.AluOpType
ACT = mybir.ActivationFunctionType
AX = mybir.AxisListType
F32 = mybir.dt.float32
F32R = mybir.dt.float32r
I32 = mybir.dt.int32
U32 = mybir.dt.uint32

P = 128
D = 1024
T = 256
TT = T // P
KT = D // P
LAYERS = 2
CONV = 256
TAPS = 31
NOPE, ROPE, MV = 64, 32, 64
QR, KR = 256, 128
HEADS = 6
QD = NOPE + ROPE
KVD = NOPE + MV
HD, DV = 32, 64
FF = 2816
NE = 8
RMS_EPS, LN_EPS = 1e-6, 1e-5
MASKED = -1e30

C_CQ = 2 * CONV
C_CKV = C_CQ + QR
C_KR = C_CKV + KR
C_DQ = C_KR + ROPE
C_DV = C_DQ + 2 * HEADS * DV
IN_COLS = C_DV + HEADS * DV
IN_PIECES = [(0, 256), (256, 256), (C_CQ, 256), (C_CKV, KR + ROPE), (C_DQ, 256), (C_DQ + 256, 256),
             (C_DQ + 512, 256), (C_DV, 192), (C_DV + 192, 192)]
NIN = len(IN_PIECES)
NOUT = 4
FC = 256
NCH = FF // FC
NFF = 3 * NCH
PIECE = 2048
RAW_A, RAW_M, SPLIT = 4, 11, 3
NA = 2 * (NIN + NOUT) + NFF
ITEMS_MAX = NE + 3
LAYER_PIECE0 = [0, NIN + NOUT + NFF]


N_EARLY = 10
N_PARAMS = 8
MID = 16
OD_STEPS = 7

MID_BANK = [0, 1, 2, 3, 0, 1, 2, 3, 0, 1, 2, 3, 0, 7, 7, 7]
MID_ACT = {0: 1, 1: 2, 2: 3, 3: 4, 5: 5, 6: 6, 7: 7, 8: 8, 9: 9}
ACT_MID_STEPS = 10
DVE_MID_STEPS = 15
MID_DVE = {4: 5, 10: 8, 11: 11, 12: 14}

UNITS = 3 * HEADS
CA = 5
CS_U = 5
CS_TAPS = CS_U - 1 + TAPS * 2
CS_CENTRED = CS_TAPS + 1
CS_NORMED = CS_CENTRED + 1
CS = CS_NORMED + 3
RV_GAP, RV_CHOSEN = 4, 12
GU0 = 2 * NCH
XU0 = 12

CR = 8
SETUP_V = 5 + 2 * LAYERS + HEADS


def ff_order():
    order = [("G", 0), ("U", 0)]
    for c in range(1, NCH):
        order += [("G", c), ("U", c), ("D", c - 1)]
    return order + [("D", NCH - 1)]


ORDER = ff_order()

V_ATTN, V_BGLU, V_BDW, V_LNG, V_LNB, V_BPW, V_QN, V_KVN, V_FFN, V_END = 0, 16, 24, 28, 32, 36, 40, 44, 46, 62

K_ID = 0
K_U = K_ID + P
K_IOTA = K_U + P
K_R = K_IOTA + P
K_END1 = K_R + QD
K_MASK = 0
K_DIST = K_MASK + 3 * P
K_COS = K_DIST + 3 * P
K_SIN = K_COS + T
K_END2 = K_SIN + T


def tables():
    one = np.zeros((P, K_END1), np.float32)
    one[:, K_ID:K_ID + P] = np.eye(P)
    one[:, K_U:K_U + P] = np.triu(np.ones((P, P)), 1)
    one[:, K_IOTA:K_IOTA + P] = np.arange(P)
    half = ROPE // 2
    for a in range(half):
        one[NOPE + half + a, K_R + NOPE + a] = -1.0
        one[NOPE + a, K_R + NOPE + half + a] = 1.0
    two = np.zeros((P, K_END2), np.float32)
    q = np.arange(P)[:, None]
    dist = np.concatenate([q - np.arange(P)[None], q + P - np.arange(T)[None]], 1)
    two[:, K_MASK:K_MASK + 3 * P] = np.where(dist < 0, MASKED, 0.0)
    two[:, K_DIST:K_DIST + 3 * P] = np.maximum(dist, 0)
    freq = np.float32(10000.0) ** (-np.arange(half, dtype=np.float32) / np.float32(half))
    ang = np.arange(T, dtype=np.float32)[None, :] * freq[:, None].astype(np.float32)
    two[:NOPE, K_COS:K_COS + T] = 1.0
    for r in range(2):
        lo = NOPE + r * half
        two[lo:lo + half, K_COS:K_COS + T] = np.cos(ang)
        two[lo:lo + half, K_SIN:K_SIN + T] = np.sin(ang)
    return one, two


def build(nc, a, out):
    with ExitStack() as ctx:
        region = [ctx]

        def sb(name, shape, dt=F32):
            return region[0].enter_context(nc.sbuf_tensor(name, shape, dt))

        def sem(name):
            return ctx.enter_context(nc.semaphore(name))

        bank = [ctx.enter_context(nc.psum_tensor(f"bank{i}", [P, 512], F32)) for i in range(8)]

        hi_ring = sb("hi_ring", [P, SPLIT, PIECE], F32R)
        lo_ring = sb("lo_ring", [P, SPLIT, PIECE], F32R)
        raw_a = sb("raw_a", [P, RAW_A, PIECE])
        x = sb("x", [P, TT, D])
        xn = sb("xn", [P, TT, D])
        hT_hi = sb("hT_hi", [P, KT, T], F32R)
        hT_lo = sb("hT_lo", [P, KT, T], F32R)
        consts = sb("consts", [P, K_END1])
        ones = sb("ones", [P, P])
        vecs = sb("vecs", [P, V_END])
        neg_vecs = sb("neg_vecs", [P, V_END])
        ss = sb("ss", [P, TT])
        ms = sb("ms", [P, TT])
        rstd = sb("rstd", [P, TT])
        half_neg = sb("half_neg", [P, 2 * HEADS])
        eps_rms = sb("eps_rms", [P, 1])
        eps_ln = sb("eps_ln", [P, 1])
        wr = sb("wr", [P, KT, NE])
        wr_hi = sb("wr_hi", [P, KT, NE], F32R)
        wr_lo = sb("wr_lo", [P, KT, NE], F32R)

        mixers = ExitStack()
        region[0] = mixers
        w_pw = sb("w_pw", [P, 2, CONV])
        w_uq = sb("w_uq", [P, 2, HEADS * QD])
        w_ukv = sb("w_ukv", [P, HEADS * KVD])
        tabs = sb("tabs", [P, K_END2])
        bias = sb("bias", [P, HEADS, 3 * P])
        vec_rows = sb("vec_rows", [V_END, P])
        dw_rows = sb("dw_rows", [LAYERS * TAPS, CONV])
        dw = sb("dw", [P, 2, LAYERS * TAPS])
        subln = sb("subln", [P, LAYERS, DV])
        lam_in = sb("lam_in", [P, 4, LAYERS, HD])
        lam_prod = sb("lam_prod", [P, 2, LAYERS, HD])
        lam_dot = sb("lam_dot", [P, 2, LAYERS])
        lam_exp = sb("lam_exp", [P, 2, LAYERS])
        neg_lam = sb("neg_lam", [P, LAYERS])
        temps = ExitStack()
        region[0] = temps
        cq = sb("cq", [P, 2, T])
        ckv = sb("ckv", [P, T])
        kr = sb("kr", [QD, T])
        sq_q = sb("sq_q", [P, 2, T])
        sq_kv = sb("sq_kv", [P, T])
        rs = sb("rs", [P, 2, T])
        dqk = sb("dqk", [P, 6, T])
        dv = sb("dv", [P, TT, HEADS * DV])
        q_m = sb("q_m", [QD, HEADS, T])
        rot = sb("rot", [QD, 2, T])
        k_m = sb("k_m", [QD, HEADS, T])
        v_m = sb("v_m", [P, TT, HEADS * MV])
        glu_a = sb("glu_a", [P, 2, T])
        glu_e = sb("glu_e", [P, 2, T])
        u_pad = sb("u_pad", [P, 2, TAPS - 1 + T])
        cv = sb("cv", [P, 2, 2, T])
        ln_rs = sb("ln_rs", [P, T])
        s_sb = sb("s_sb", [P, 2, 3 * P])
        e_sb = sb("e_sb", [P, 2, 3 * P])
        pt_sb = sb("pt_sb", [P, 2, 3 * P])
        neg_max = sb("neg_max", [P, 3 * HEADS, 2])
        row_sum = sb("row_sum", [P, 3 * HEADS, 2])
        coef = sb("coef", [P, 3 * HEADS, 2])
        o_w = sb("o_w", [P, 4, 2, DV])
        od = sb("od", [P, HEADS, 2, DV])
        od_sq = sb("od_sq", [P, HEADS, 2, DV])
        o_ss = sb("o_ss", [P, HEADS, 2])
        o_ms = sb("o_ms", [P, HEADS, 2])
        o_rstd = sb("o_rstd", [P, HEADS, 2])
        temps.close()
        dense = ExitStack()
        region[0] = dense
        d_sg = sb("d_sg", [P, 2, 2, T])
        d_prod = sb("d_prod", [P, 2, 2, T])
        d_hi = sb("d_hi", [P, 2, 2, T], F32R)
        d_lo = sb("d_lo", [P, 2, 2, T], F32R)
        dense.close()
        mixers.close()
        region[0] = ctx
        raw_m = sb("raw_m", [P, RAW_M - RAW_A, PIECE])
        ht_hi = sb("ht_hi", [P, TT, D], F32R)
        ht_lo = sb("ht_lo", [P, TT, D], F32R)
        g_bc = sb("g_bc", [P, D])
        lg = sb("lg", [P, TT, NE])
        m8 = sb("m8", [P, TT, NE])
        idx = sb("idx", [P, TT, NE], U32)
        idf = sb("idf", [P, TT, NE])
        gap = sb("gap", [P, TT])
        e2 = sb("e2", [P, TT])
        w_top = sb("w_top", [P, 3, TT])
        oh = sb("oh", [P, 2, TT, NE])
        gw = sb("gw", [P, 2, TT, NE])
        chosen = sb("chosen", [P, TT, NE])
        less1 = sb("less1", [P, TT, NE])
        pos = sb("pos", [P, TT, NE])
        pos_m = sb("pos_m", [P, TT, NE])
        pos_hi = sb("pos_hi", [P, TT, NE])
        cnt = sb("cnt", [P, NE])
        over = sb("over", [P, NE])
        incl = sb("incl", [P, NE])
        rank = sb("rank", [P, NE])
        sel = sb("sel", [P, 3, NE])
        junk = sb("junk", [P, 15, NE])
        it_f = sb("it_f", [P, 4])
        it_i = sb("it_i", [P, 4], I32)
        pos_item = sb("pos_item", [P, TT, ITEMS_MAX + 1])
        g_item = sb("g_item", [P, TT, ITEMS_MAX + 1])
        p_col = sb("p_col", [P, TT])
        g_col = sb("g_col", [P, TT])
        onehot = sb("onehot", [P, TT, P], F32R)
        onehot_t = sb("onehot_t", [P, TT, P], F32R)
        m_sg = sb("m_sg", [P, 2, FC])
        m_prod = sb("m_prod", [P, 2, FC])
        m_hi = sb("m_hi", [P, 2, 2, P], F32R)
        m_lo = sb("m_lo", [P, 2, 2, P], F32R)
        sel_hi = hT_hi[:, 0:4, :].rearrange("p a b -> p (a b)").rearrange("p (k s) -> p k s", k=KT)
        sel_lo = hT_lo[:, 0:4, :].rearrange("p a b -> p (a b)").rearrange("p (k s) -> p k s", k=KT)
        y_hi = hT_hi[:, 4:8, :].rearrange("p a b -> p (a b)")
        y_lo = hT_lo[:, 4:8, :].rearrange("p a b -> p (a b)")

        ident = consts[:, K_ID:K_ID + P]
        upper = consts[:, K_U:K_U + P]
        iota = consts[:, K_IOTA:K_IOTA + P]
        rotate = consts[0:QD, K_R:K_R + QD]
        mask = tabs[:, K_MASK:K_MASK + 3 * P]
        dist = tabs[:, K_DIST:K_DIST + 3 * P]
        cos = tabs[0:QD, K_COS:K_COS + T]
        sin = tabs[0:QD, K_SIN:K_SIN + T]

        x_in = sem("x_in")
        early_in = sem("early_in")
        params_in = sem("params_in")
        small_in = sem("small_in")
        raw_in = [sem(f"raw_in{s}") for s in range(RAW_M)]
        gfin_in = sem("gfin_in")
        out_sent = sem("out_sent")
        hi_ready = sem("hi_ready")
        lo_ready = sem("lo_ready")
        piece_used = sem("piece_used")
        const_set = sem("const_set")
        setup_t = sem("setup_t")
        setup_v = sem("setup_v")
        setup_a = sem("setup_a")
        sumsq = sem("sumsq")
        ms_ready = sem("ms_ready")
        rstd_ready = sem("rstd_ready")
        xn_ready = sem("xn_ready")
        hT_mm = sem("hT_mm")
        hThi_done = sem("hThi_done")
        hTlo_done = sem("hTlo_done")
        proj_evac = sem("proj_evac")
        mid_mm = sem("mid_mm")
        mid_act = sem("mid_act")
        mid_dve = sem("mid_dve")
        conv_step = sem("conv_step")
        conv_act = sem("conv_act")
        s_mm = sem("s_mm")
        s_biased = sem("s_biased")
        s_max = sem("s_max")
        exp_done = sem("exp_done")
        pt_mm = sem("pt_mm")
        pt_ready = sem("pt_ready")
        pv_mm = sem("pv_mm")
        coef_ready = sem("coef_ready")
        o_read = sem("o_read")
        od_step = sem("od_step")
        od_act = sem("od_act")
        od_pow = sem("od_pow")
        yT_mm = sem("yT_mm")
        cat_hi = sem("cat_hi")
        cat_lo = sem("cat_lo")
        x_upd = sem("x_upd")
        sg_done = sem("sg_done")
        prod_done = sem("prod_done")
        act_t = sem("act_t")
        act_hi = sem("act_hi")
        act_lo = sem("act_lo")
        route_mm = sem("route_mm")
        route_v = sem("route_v")
        route_a = sem("route_a")
        items_ready = sem("items_ready")
        onehot_done = sem("onehot_done")
        gather_mm = sem("gather_mm")
        gather_hi = sem("gather_hi")
        gather_lo = sem("gather_lo")
        onehot_tmm = sem("onehot_tmm")
        onehot_tdone = sem("onehot_tdone")
        yhi_done = sem("yhi_done")
        ylo_done = sem("ylo_done")
        scat_mm = sem("scat_mm")
        h_rows = sem("h_rows")
        ht_split = sem("ht_split")

        block = ctx.enter_context(nc.Block())

        def raw_slot(n):
            return raw_a[:, n % RAW_A, :], raw_in[n % RAW_A], 16 * (n // RAW_A + 1)

        trunk_uses = [len(range(s, NA, RAW_A)) if s < RAW_A else 0 for s in range(RAW_M)]

        def expert_slot(i, j):
            s = j % RAW_M
            tile = raw_a[:, s, :] if s < RAW_A else raw_m[:, s - RAW_A, :]
            return tile, raw_in[s], 16 * (trunk_uses[s] + j // RAW_M + 1) + i * (16 * NFF // RAW_M)

        def in_piece_view(t, p):
            c = IN_PIECES[p][1]
            return t[:, 0:KT * c].rearrange("p (k n) -> p k n", k=KT)

        def ff_src(wg, wu, wd, kind, c):
            if kind == "D":
                return wd[c * FC:(c + 1) * FC, :].rearrange("(k p) n -> p k n", p=P)
            w = wg if kind == "G" else wu
            return w[:, c * FC:(c + 1) * FC].rearrange("(k p) n -> p k n", p=P)

        def ff_view(t, kind):
            return t.rearrange("p (k n) -> p k n", n=D if kind == "D" else FC)

        def in_done(l, p):
            return LAYER_PIECE0[l] + p + 1

        def out_done(l):
            return LAYER_PIECE0[l] + NIN + NOUT

        def dense_done(kind, c):
            return LAYER_PIECE0[0] + NIN + NOUT + ORDER.index((kind, c)) + 1

        def expert_done(i, kind, c):
            return NA + ORDER.index((kind, c)) + 1 + i * NFF

        def transposed_after(kind, c):
            if kind == "G" and c >= 1:
                return c - 1
            if kind == "D" and c == NCH - 2:
                return NCH - 1
            return None

        trunk_width = {}
        for l in range(LAYERS):
            for p in range(NIN):
                trunk_width[LAYER_PIECE0[l] + p] = KT * IN_PIECES[p][1]

        @block.sync
        def _(sp):
            sp.dma_start(x[:], a["x"].rearrange("b (t p) d -> p (b t) d", p=P)).then_inc(x_in, 16)

            def load(n, src, view):
                if n >= RAW_A:
                    sp.wait_ge(lo_ready, n - RAW_A + 1)
                t, s, _ = raw_slot(n)
                sp.dma_start(view(t), src).then_inc(s, 16)

            def load_small(l):
                sp.dma_start(w_pw[:], a["w_pw"][l].rearrange("(k p) n -> p k n", p=P)).then_inc(small_in, 16)
                sp.dma_start(w_uq[:], a["w_uq"][l].rearrange("(k p) n -> p k n", p=P)).then_inc(small_in, 16)
                sp.dma_start(w_ukv[:], a["w_ukv"][l]).then_inc(small_in, 16)

            for l in range(LAYERS):
                n0 = LAYER_PIECE0[l]
                for p, (c0, cn) in enumerate(IN_PIECES):
                    load(n0 + p, a["w_in"][l][:, c0:c0 + cn].rearrange("(k p) n -> p k n", p=P),
                         lambda t, p=p: in_piece_view(t, p))
                    if l == 0 and p == 2:
                        load_small(0)
                for i in range(NOUT):
                    load(n0 + NIN + i, a["w_out"][l][i * 2 * P:(i + 1) * 2 * P, :].rearrange("(k p) n -> p k n", p=P),
                         lambda t: ff_view(t, "D"))
                if l == 0:
                    sp.wait_ge(mid_mm, MID)
                    load_small(1)
                    for j, (kind, c) in enumerate(ORDER):
                        load(n0 + NIN + NOUT + j,
                             ff_src(a["w_gate_dense"][0], a["w_up_dense"][0], a["w_down_dense"][0], kind, c),
                             lambda t, kind=kind: ff_view(t, kind))

            def expert_loads(e, i, first):
                for j, (kind, c) in enumerate(ORDER):
                    if first and j < RAW_A:
                        sp.wait_ge(lo_ready, max(n for n in range(NA) if n % RAW_A == j) + 1)
                    elif first and j < RAW_M:
                        sp.wait_ge(x_upd, 12)
                    else:
                        sp.wait_ge(lo_ready, NA + j - RAW_M + 1 + i * NFF)
                    t, s, _ = expert_slot(i, j)
                    one = bass.ds(e, 1)
                    if kind == "D":
                        src = a["w_down_exp"][0][one, c * FC:(c + 1) * FC, :].rearrange("e (k p) n -> p (e k) n", p=P)
                    else:
                        w = a["w_gate_exp" if kind == "G" else "w_up_exp"][0]
                        src = w[one, :, c * FC:(c + 1) * FC].rearrange("e (k p) n -> p (e k) n", p=P)
                    sp.dma_start(ff_view(t, kind), src).then_inc(s, 16)

            expert_loads(0, 0, True)
            with sp.Fori(1, NE) as i:
                expert_loads(i, i, False)
            sp.wait_ge(items_ready, 1)
            n_items = sp.value_load(it_i[0:1, 0:1], min_val=NE, max_val=ITEMS_MAX)
            for j in range(3):
                e = sp.value_load(it_i[0:1, 1 + j:2 + j], min_val=0, max_val=NE - 1)
                with sp.If(n_items > NE + j):
                    expert_loads(e, NE + j, False)
            sp.wait_ge(out_sent, 16 * TT)

        @block.gpsimd
        def _(pool):
            pool.dma_start(tabs[:], a["table2"]).then_inc(params_in, 16)
            pool.dma_start(dw_rows[:], a["w_dw"].rearrange("l w c -> (l w) c")).then_inc(params_in, 16)
            for m, name in enumerate(["lambda_q1", "lambda_k1", "lambda_q2", "lambda_k2"]):
                pool.dma_start(lam_in[:, m].rearrange("p l d -> p (l d)"),
                               a[name].rearrange("(o l) d -> o (l d)", o=1).broadcast_to([P, LAYERS * HD])
                               ).then_inc(params_in, 16)
            pool.dma_start(subln[:].rearrange("p l d -> p (l d)"),
                           a["diff_subln"].rearrange("(o l) d -> o (l d)", o=1).broadcast_to([P, LAYERS * DV])
                           ).then_inc(params_in, 16)
            pool.dma_start(wr[:], a["w_router"][0].rearrange("(k p) e -> p k e", p=P)).then_inc(params_in, 16)
            nc.gpsimd.memset(ones[:], 1.0).then_inc(const_set, 1)
            nc.gpsimd.memset(half_neg[:], -0.5).then_inc(const_set, 1)
            nc.gpsimd.memset(eps_rms[:], RMS_EPS).then_inc(const_set, 1)
            nc.gpsimd.memset(eps_ln[:], LN_EPS).then_inc(const_set, 1)
            nc.gpsimd.memset(u_pad[:], 0.0).then_inc(const_set, 1)
            def norm_pow(j):
                pool.wait_ge(ms_ready, j + 1)
                nc.gpsimd.tensor_tensor(rstd[:], ms[:], half_neg[:, 0:TT], ALU.pow).then_inc(rstd_ready, 1)

            for l in range(LAYERS):
                norm_pow(2 * l)
                if l > 0:
                    pool.wait_ge(x_upd, 8)
                    nc.gpsimd.memset(u_pad[:], 0.0).then_inc(const_set, 1)
                pool.wait_ge(od_step, OD_STEPS * l + 5)
                nc.gpsimd.tensor_tensor(o_rstd[:].rearrange("p h t -> p (h t)"), o_ms[:].rearrange("p h t -> p (h t)"),
                                        half_neg[:], ALU.pow).then_inc(od_pow, 1)
                if l == LAYERS - 1:
                    pool.wait_ge(x_upd, 12)
                    pool.dma_start(g_bc[:], a["ffn_norm"][l:l + 1, :].broadcast_to([P, D])).then_inc(gfin_in, 16)
                norm_pow(2 * l + 1)
            pool.wait_ge(h_rows, 2)
            pool.dma_start(g_bc[:], a["final_norm"].rearrange("(o d) -> o d", o=1).broadcast_to([P, D])
                           ).then_inc(gfin_in, 16)
            norm_pow(2 * LAYERS)

        def hi_of(n):
            return hi_ring[:, n % SPLIT, :]

        def lo_of(n):
            return lo_ring[:, n % SPLIT, :]

        @block.scalar
        def _(act):
            A = nc.scalar.activation

            def split(n):
                w = trunk_width.get(n, PIECE)
                t, s, v = raw_slot(n)
                act.wait_ge(s, v)
                if n >= SPLIT:
                    act.wait_ge(piece_used, n - SPLIT + 1)
                A(hi_of(n)[:, 0:w], t[:, 0:w], ACT.Copy).then_inc(hi_ready, 1)

            def split_expert(i, j):
                t, s, v = expert_slot(i, j)
                act.wait_ge(s, v)
                act.wait_ge(piece_used, NA + j - SPLIT + 1 + i * NFF)
                A(hi_of(NA + j), t, ACT.Copy).then_inc(hi_ready, 1)

            def norm_squares(j):
                for t in range(TT):
                    A(xn[:, t, :], x[:, t, :], ACT.Square, accum_out=ss[:, t:t + 1]).then_inc(sumsq, 1)

            def norm_evac(j, g0):
                for k in range(KT):
                    if k % 2 == 0:
                        act.wait_ge(hT_mm, 4 * j + k // 2 + 1)
                    A(hT_hi[:, k, :], bank[k // 2][:, (k % 2) * T:(k % 2 + 1) * T], ACT.Copy,
                      scale=vecs[:, g0 + k:g0 + k + 1]).then_inc(hThi_done, 1)

            act.dma_start(consts[:], a["table1"]).then_inc(early_in, 16)
            rows = [("attn_norm", V_ATTN), ("b_glu", V_BGLU), ("b_dw", V_BDW), ("conv_ln_g", V_LNG),
                    ("conv_ln_b", V_LNB), ("b_pw", V_BPW), ("q_norm", V_QN), ("kv_norm", V_KVN),
                    ("ffn_norm", V_FFN)]
            for (name, r0), r1 in zip(rows, [r for _, r in rows[1:]] + [V_END]):
                act.dma_start(vec_rows[r0:r1, :], a[name].rearrange("l (k p) -> (l k) p", p=P)).then_inc(early_in, 16)
            nc.scalar.preload_act_table_set("natural_log_exp_and_others")
            act.wait_ge(const_set, 5)
            act.wait_ge(x_in, 16)
            norm_squares(0)
            split(0)
            act.wait_ge(setup_t, 1)
            A(vecs[:], bank[4][:, 0:V_END], ACT.Copy).then_inc(setup_a, 1)
            act.wait_ge(setup_a, 1)

            for l in range(LAYERS):
                n0 = LAYER_PIECE0[l]
                if l > 0:
                    nc.scalar.preload_act_table_set("natural_log_exp_and_others")
                    act.wait_ge(x_upd, 8)
                    norm_squares(2 * l)
                    split(n0)
                split(n0 + 1)
                norm_evac(2 * l, V_ATTN + KT * l)
                split(n0 + 2)
                if l == 0:
                    act.wait_ge(setup_t, 2)
                    A(dw[:], bank[7][:, 0:2 * LAYERS * TAPS].rearrange("p (c w) -> p c w", c=2),
                      ACT.Copy).then_inc(setup_a, 1)
                    act.wait_ge(params_in, 16 * N_PARAMS)
                    A(wr_hi[:], wr[:], ACT.Copy).then_inc(setup_a, 1)

                def mid(g):
                    act.wait_ge(mid_mm, MID * l + g + 1)

                def mid_inc(ins):
                    ins.then_inc(mid_act, 1)

                for p in range(NIN):
                    act.wait_ge(piece_used, in_done(l, p))
                    b = bank[4 + p % 4]
                    if p == 0:
                        A(glu_a[:, 0, :], b[:, 0:T], ACT.Identity,
                          bias=vecs[:, V_BGLU + 4 * l:V_BGLU + 4 * l + 1])
                        r = A(glu_a[:, 1, :], b[:, T:2 * T], ACT.Identity,
                              bias=vecs[:, V_BGLU + 4 * l + 1:V_BGLU + 4 * l + 2])
                    elif p == 1:
                        if l == 0:
                            act.wait_ge(setup_v, 1)
                        A(glu_e[:, 0, :], b[:, 0:T], ACT.Exp, scale=-1.0,
                          bias=neg_vecs[:, V_BGLU + 4 * l + 2:V_BGLU + 4 * l + 3])
                        r = A(glu_e[:, 1, :], b[:, T:2 * T], ACT.Exp, scale=-1.0,
                              bias=neg_vecs[:, V_BGLU + 4 * l + 3:V_BGLU + 4 * l + 4])
                    elif p == 2:
                        A(cq[:], b[:].rearrange("p (c t) -> p c t", c=2), ACT.Copy)
                        r = A(sq_q[:], b[:].rearrange("p (c t) -> p c t", c=2), ACT.Square)
                    elif p == 3:
                        A(ckv[:], b[:, 0:T], ACT.Copy)
                        A(sq_kv[:], b[:, 0:T], ACT.Square)
                        r = A(kr[:], b[0:QD, T:2 * T], ACT.Copy)
                    elif p < 7:
                        r = A(dqk[:, 2 * (p - 4):2 * (p - 4) + 2, :], b[:].rearrange("p (c t) -> p c t", c=2), ACT.Copy)
                    else:
                        r = A(dv[:, :, (p - 7) * 192:(p - 6) * 192],
                              b[:, 0:384].rearrange("p (t n) -> p t n", t=TT), ACT.Copy)
                    r.then_inc(proj_evac, 1)
                    split(n0 + 3 + p)
                    if l == 0 and p == 1:
                        act.wait_ge(setup_v, 3)
                        A(lam_exp[:], lam_dot[:], ACT.Exp).then_inc(setup_a, 1)
                    if p == 4:
                        mid(0)
                        A(rs[:, 0, :], bank[0][:, 0:T], ACT.Ln, scale=1.0 / QR, bias=eps_rms[:])
                        A(rs[:, 1, :], bank[0][:, T:2 * T], ACT.Ln, scale=1.0 / KR, bias=eps_rms[:]).then_inc(conv_act, 1)
                        act.wait_ge(conv_act, CA * l + 1)
                        mid_inc(A(rs[:], rs[:], ACT.Exp, scale=-0.5))
                    if p == 6:
                        for r3 in range(3):
                            mid(1 + r3)
                            mid_inc(A(q_m[:, 2 * r3:2 * r3 + 2, :],
                                      bank[1 + r3][0:QD, :].rearrange("p (h t) -> p h t", h=2), ACT.Copy))
                for t in range(TT):
                    mid(5 + t)
                    mid_inc(A(v_m[:, t, :], bank[1 + t][:, 0:HEADS * MV], ACT.Copy))
                for r3 in range(3):
                    mid(7 + r3)
                    mid_inc(A(k_m[0:NOPE, 2 * r3:2 * r3 + 2, :],
                              bank[MID_BANK[7 + r3]][0:NOPE, :].rearrange("p (h t) -> p h t", h=2), ACT.Copy))
                act.wait_ge(mid_dve, DVE_MID_STEPS * l + 6)
                mid_inc(A(k_m[NOPE:QD, :, :], kr[NOPE:QD, :].unsqueeze(1).broadcast_to([ROPE, HEADS, T]), ACT.Copy))

                for k in range(UNITS + 4):
                    if 1 <= k <= UNITS:
                        u = k - 1
                        act.wait_ge(s_max, 2 * (UNITS * l + u + 1))
                        if UNITS * l + u >= 2:
                            act.wait_ge(pt_mm, UNITS * l + u - 1)
                        A(e_sb[:, u % 2, 0:P], s_sb[:, u % 2, 0:P], ACT.Exp, bias=neg_max[:, u, 0:1],
                          accum_out=row_sum[:, u, 0:1])
                        A(e_sb[:, u % 2, P:3 * P], s_sb[:, u % 2, P:3 * P], ACT.Exp, bias=neg_max[:, u, 1:2],
                          accum_out=row_sum[:, u, 1:2]).then_inc(exp_done, 1)
                    if 2 <= k < UNITS + 2:
                        u = k - 2
                        act.wait_ge(pt_mm, UNITS * l + u + 1)
                        if UNITS * l + u >= 2:
                            act.wait_ge(pv_mm, UNITS * l + u - 1)
                        A(pt_sb[:, u % 2, :], bank[3 + u % 2][:, 0:3 * P], ACT.Copy).then_inc(pt_ready, 1)
                    if k == 6:
                        act.wait_ge(conv_step, CS * l + CS_CENTRED)
                        A(glu_e[:], cv[:, 1], ACT.Square).then_inc(conv_act, 1)
                    if k == 8:
                        mid(14)
                        A(ln_rs[:], bank[7][:, 0:T], ACT.Ln, scale=1.0 / CONV, bias=eps_ln[:]).then_inc(conv_act, 1)
                        act.wait_ge(conv_act, CA * l + 3)
                        A(ln_rs[:], ln_rs[:], ACT.Exp, scale=-0.5).then_inc(conv_act, 1)
                    if k == 10:
                        act.wait_ge(conv_step, CS * l + CS_NORMED)
                        for c in range(2):
                            A(glu_e[:, c, :], cv[:, 0, c, :], ACT.Exp,
                              scale=neg_vecs[:, V_LNG + 2 * l + c:V_LNG + 2 * l + c + 1],
                              bias=neg_vecs[:, V_LNB + 2 * l + c:V_LNB + 2 * l + c + 1])
                            r = A(glu_a[:, c, :], cv[:, 0, c, :], ACT.Identity,
                                  scale=vecs[:, V_LNG + 2 * l + c:V_LNG + 2 * l + c + 1],
                                  bias=vecs[:, V_LNB + 2 * l + c:V_LNB + 2 * l + c + 1])
                        r.then_inc(conv_act, 1)
                    if k == 14:
                        mid(15)
                        for c in range(2):
                            A(hT_hi[:, c, :], bank[7][:, c * T:(c + 1) * T], ACT.Identity,
                              bias=vecs[:, V_BPW + 2 * l + c:V_BPW + 2 * l + c + 1]).then_inc(cat_hi, 1)
                    if k == 18:
                        act.wait_ge(od_step, OD_STEPS * l + 3)
                        A(od_sq[:], od[:], ACT.Square).then_inc(od_act, 1)
                for r3 in range(3):
                    act.wait_ge(yT_mm, 3 * l + r3 + 1)
                    A(hT_hi[:, 2 + 2 * r3:4 + 2 * r3, :], bank[r3][:].rearrange("p (c t) -> p c t", c=2),
                      ACT.Copy).then_inc(cat_hi, 1)
                split(n0 + 12)
                act.wait_ge(x_upd, 8 * l + 4)
                norm_squares(2 * l + 1)
                if l == 0:
                    f0 = n0 + NIN + NOUT
                    split(f0)
                    norm_evac(1, V_FFN)
                    split(f0 + 1)
                    for j, (kind, c) in enumerate(ORDER):
                        if j + 2 < NFF:
                            split(f0 + j + 2)
                        if kind == "U":
                            act.wait_ge(piece_used, dense_done("U", c))
                            for f in range(2):
                                if c >= 2:
                                    act.wait_ge(prod_done, 2 * (c - 2) + f + 1)
                                A(d_sg[:, c % 2, f, :], bank[(c % 2) * 2 + f][:, 0:T], ACT.Silu).then_inc(sg_done, 1)
                            for f in range(2):
                                act.wait_ge(prod_done, 2 * c + f + 1)
                                if c >= 2:
                                    act.wait_ge(piece_used, dense_done("D", c - 2))
                                A(d_hi[:, c % 2, f, :], d_prod[:, c % 2, f, :], ACT.Copy).then_inc(act_hi, 1)
                else:
                    norm_evac(3, V_FFN + KT)

            act.wait_ge(h_rows, 2)
            A(ht_hi[:], xn[:], ACT.Copy).then_inc(ht_split, 1)
            act.wait_ge(route_v, RV_GAP)
            A(e2[:], gap[:], ACT.Exp).then_inc(route_a, 1)
            split_expert(0, 0)
            split_expert(0, 1)

            def gather_evac(i):
                for h in range(2):
                    act.wait_ge(gather_mm, 4 * i + h + 1)
                    A(sel_hi[:, 4 * h:4 * h + 4, :], bank[6 + h][:].rearrange("p (k s) -> p k s", k=4),
                      ACT.Copy).then_inc(gather_hi, 1)

            gather_evac(0)
            act.wait_ge(items_ready, 1)
            n_items = act.value_load(it_i[0:1, 0:1], min_val=NE, max_val=ITEMS_MAX)
            with act.Fori(0, n_items) as i:
                for j, (kind, c) in enumerate(ORDER):
                    if j + 2 < NFF:
                        split_expert(i, j + 2)
                    else:
                        with act.If(i < n_items - 1):
                            split_expert(i, j + 2)
                    if kind == "U":
                        act.wait_ge(piece_used, expert_done(i, "U", c))
                        act.wait_ge(prod_done, GU0 + c - 1 + i * NCH)
                        A(m_sg[:, c % 2, :], bank[c % 2][:, 0:FC], ACT.Silu).then_inc(sg_done, 1)
                    if kind == "U" and c == 1:
                        act.wait_ge(onehot_tmm, i + 1)
                        A(onehot_t[:], bank[6][:, 0:TT * P].rearrange("p (t s) -> p t s", t=TT),
                          ACT.Copy).then_inc(onehot_tdone, 1)
                    tc = transposed_after(kind, c)
                    if tc is not None:
                        act.wait_ge(act_t, tc + 1 + i * NCH)
                        if tc >= 2:
                            act.wait_ge(piece_used, expert_done(i, "D", tc - 2))
                        A(m_hi[:, tc % 2, :, :], bank[2 + tc % 2][:, 0:2 * P].rearrange("p (f s) -> p f s", f=2),
                          ACT.Copy).then_inc(act_hi, 1)
                gather_evac(i + 1)
                act.wait_ge(piece_used, expert_done(i, "D", NCH - 1))
                for h in range(2):
                    A(y_hi[:, h * 512:(h + 1) * 512], bank[4 + h][:], ACT.Copy).then_inc(yhi_done, 1)
            act.wait_ge(x_upd, XU0 + n_items * 4)
            norm_squares(4)
            act.wait_ge(xn_ready, 5 * TT)
            act.dma_start(out.rearrange("b (t p) d -> p (b t) d", p=P)[:, 0, :], xn[:, 0, :]).then_inc(out_sent, 16)
            act.dma_start(out.rearrange("b (t p) d -> p (b t) d", p=P)[:, 1, :], xn[:, 1, :]).then_inc(out_sent, 16)

        @block.vector
        def _(dve):
            V = nc.vector

            def split(n):
                w = trunk_width.get(n, PIECE)
                dve.wait_ge(hi_ready, n + 1)
                V.tensor_tensor(lo_of(n)[:, 0:w], raw_slot(n)[0][:, 0:w], hi_of(n)[:, 0:w].bitcast(F32),
                                ALU.subtract).then_inc(lo_ready, 1)

            def split_expert(i, j):
                dve.wait_ge(hi_ready, NA + j + 1 + i * NFF)
                V.tensor_tensor(lo_of(NA + j), expert_slot(i, j)[0], hi_of(NA + j).bitcast(F32),
                                ALU.subtract).then_inc(lo_ready, 1)

            def norm_ms(j):
                dve.wait_ge(sumsq, TT * (j + 1))
                V.tensor_scalar(ms[:], ss[:], 1.0 / D, RMS_EPS, ALU.mult, ALU.add).then_inc(ms_ready, 1)

            def norm_rows(j):
                dve.wait_ge(rstd_ready, j + 1)
                for t in range(TT):
                    V.tensor_scalar(xn[:, t, :], x[:, t, :], rstd[:, t:t + 1], None, ALU.mult).then_inc(xn_ready, 1)

            def norm_evac(j, g0):
                for k in range(KT):
                    dve.wait_ge(hThi_done, KT * j + 2 * (k // 2) + 2)
                    V.scalar_tensor_tensor(hT_lo[:, k, :], bank[k // 2][:, (k % 2) * T:(k % 2 + 1) * T],
                                           vecs[:, g0 + k:g0 + k + 1], hT_hi[:, k, :].bitcast(F32),
                                           ALU.mult, ALU.subtract).then_inc(hTlo_done, 1)

            def add_to_x(done, banks):
                for q in range(4):
                    t, n = q // 2, q % 2
                    if q == 0:
                        dve.wait_ge(piece_used, done)
                    V.tensor_tensor(x[:, t, n * 512:(n + 1) * 512], x[:, t, n * 512:(n + 1) * 512], banks[q][:],
                                    ALU.add).then_inc(x_upd, 1)

            norm_ms(0)
            norm_rows(0)
            split(0)
            dve.wait_ge(setup_a, 1)
            V.tensor_scalar(neg_vecs[:], vecs[:], -1.0, None, ALU.mult).then_inc(setup_v, 1)

            for l in range(LAYERS):
                n0 = LAYER_PIECE0[l]
                lam_init = 0.8 - 0.6 * math.exp(-0.3 * l)
                if l > 0:
                    norm_ms(2 * l)
                    norm_rows(2 * l)
                    split(n0)
                split(n0 + 1)
                norm_evac(2 * l, V_ATTN + KT * l)
                split(n0 + 2)

                def setup():
                    dve.wait_ge(params_in, 16 * N_PARAMS)
                    V.tensor_tensor(lam_prod[:], lam_in[:, 0:4:2], lam_in[:, 1:4:2], ALU.mult).then_inc(setup_v, 1)
                    dve.wait_ge(setup_v, 2)
                    V.tensor_reduce(lam_dot[:], lam_prod[:], AX.X, ALU.add).then_inc(setup_v, 1)
                    for h in range(HEADS):
                        slope = 2.0 ** (-8.0 * (h + 1) / HEADS)
                        V.scalar_tensor_tensor(bias[:, h, :], dist, -slope, mask, ALU.mult, ALU.add).then_inc(setup_v, 1)
                    dve.wait_ge(setup_a, 3)
                    V.tensor_tensor(wr_lo[:], wr[:], wr_hi[:].bitcast(F32), ALU.subtract).then_inc(setup_v, 1)
                    for m in range(LAYERS):
                        li = 0.8 - 0.6 * math.exp(-0.3 * m)
                        V.tensor_scalar(subln[:, m], subln[:, m], 1.0 - li, None, ALU.mult).then_inc(setup_v, 1)

                def setup_lambda():
                    dve.wait_ge(setup_a, 4)
                    V.tensor_tensor(neg_lam[:], lam_exp[:, 1], lam_exp[:, 0], ALU.subtract).then_inc(setup_v, 1)
                    dve.wait_ge(setup_v, SETUP_V - LAYERS)
                    for m in range(LAYERS):
                        li = 0.8 - 0.6 * math.exp(-0.3 * m)
                        V.tensor_scalar(neg_lam[:, m:m + 1], neg_lam[:, m:m + 1], -li, None, ALU.add).then_inc(setup_v, 1)

                cs = [CS * l]
                ms_ = [DVE_MID_STEPS * l]

                def conv(ins):
                    cs[0] += 1
                    ins.then_inc(conv_step, 1)

                def mids(ins):
                    ms_[0] += 1
                    ins.then_inc(mid_dve, 1)

                def taps(lo, hi):
                    for w in range(lo, hi):
                        for c in range(2):
                            win = u_pad[:, c, w:w + T]
                            wc = dw[:, c, TAPS * l + w:TAPS * l + w + 1]
                            b = V_BDW + 2 * l + c
                            if w == 0:
                                conv(V.tensor_scalar(cv[:, 0, c, :], win, wc, vecs[:, b:b + 1], ALU.mult, ALU.add))
                            else:
                                dve.wait_ge(conv_step, cs[0] - 1)
                                conv(V.scalar_tensor_tensor(cv[:, w % 2, c, :], win, wc, cv[:, (w + 1) % 2, c, :],
                                                            ALU.mult, ALU.add))

                def glu():
                    dve.wait_ge(proj_evac, NIN * l + 2)
                    conv(V.tensor_scalar(glu_e[:], glu_e[:], 1.0, None, ALU.add))
                    dve.wait_ge(conv_step, cs[0])
                    conv(V.reciprocal(glu_e[:], glu_e[:]))
                    dve.wait_ge(conv_step, cs[0])
                    dve.wait_ge(const_set, 5 + l)
                    for c in range(2):
                        conv(V.tensor_tensor(u_pad[:, c, TAPS - 1:], glu_a[:, c, :], glu_e[:, c, :], ALU.mult))
                    dve.wait_ge(conv_step, cs[0])

                def latents():
                    dve.wait_ge(mid_act, ACT_MID_STEPS * l + 1)
                    for c in range(2):
                        mids(V.scalar_tensor_tensor(cq[:, c, :], cq[:, c, :],
                                                    vecs[:, V_QN + 2 * l + c:V_QN + 2 * l + c + 1], rs[:, 0, :],
                                                    ALU.mult, ALU.mult))
                    mids(V.scalar_tensor_tensor(ckv[:], ckv[:], vecs[:, V_KVN + l:V_KVN + l + 1], rs[:, 1, :],
                                                ALU.mult, ALU.mult))

                for p in range(NIN):
                    dve_split = n0 + 3 + p
                    split(dve_split)
                    if l == 0 and p == 0:
                        setup()
                    if l == 0 and p == 4:
                        setup_lambda()
                    if p == 1:
                        glu()
                    if p >= 2 and p != 5:
                        t0 = {2: 0, 3: 5, 4: 9, 6: 13, 7: 18, 8: 24}[p]
                        taps(t0, {2: 5, 3: 9, 4: 13, 6: 18, 7: 24, 8: TAPS}[p])
                    if p == 5:
                        latents()
                dve.wait_ge(mid_mm, MID * l + 5)
                mids(V.tensor_tensor(kr[:], kr[:], cos, ALU.mult))
                mids(V.tensor_tensor(rot[:, 0, :], bank[0][0:QD, 0:T], sin, ALU.mult))
                dve.wait_ge(mid_dve, ms_[0])
                mids(V.tensor_tensor(kr[:], kr[:], rot[:, 0, :], ALU.add))

                def rope_q():
                    for r3 in range(3):
                        pair = q_m[:, 2 * r3:2 * r3 + 2, :]
                        wide = [QD, 2, T]
                        dve.wait_ge(mid_mm, MID * l + 11 + r3)
                        dve.wait_ge(mid_dve, ms_[0])
                        mids(V.tensor_tensor(pair, pair, cos.unsqueeze(1).broadcast_to(wide), ALU.mult))
                        mids(V.tensor_tensor(rot[:], bank[MID_BANK[10 + r3]][0:QD, :].rearrange("p (h t) -> p h t", h=2),
                                             sin.unsqueeze(1).broadcast_to(wide), ALU.mult))
                        dve.wait_ge(mid_dve, ms_[0])
                        mids(V.tensor_tensor(pair, pair, rot[:], ALU.add))

                rope_q()

                cr = [CR * l]
                ods = [OD_STEPS * l]

                def coefs(ins):
                    cr[0] += 1
                    ins.then_inc(coef_ready, 1)

                def odst(ins):
                    ods[0] += 1
                    ins.then_inc(od_step, 1)

                def normalise(g):
                    u0, un = 4 * g, min(4, UNITS - 4 * g)
                    last = u0 + un - 1
                    dve.wait_ge(exp_done, UNITS * l + last + 1)
                    coefs(V.reciprocal(coef[:, u0:u0 + un], row_sum[:, u0:u0 + un]))
                    dve.wait_ge(coef_ready, cr[0])
                    if g < 3:
                        odd = coef[:, u0 + 1:u0 + 4:2]
                        coefs(V.tensor_scalar(odd, odd, neg_lam[:, l:l + 1], None, ALU.mult))
                        dve.wait_ge(coef_ready, cr[0])
                    dve.wait_ge(pv_mm, UNITS * l + last + 1)
                    src = bank[5 + g % 2][:, 0:P * un].rearrange("p (u t d) -> p u t d", u=un, t=2)
                    cf = coef[:, u0:u0 + un].unsqueeze(3).broadcast_to([P, un, 2, DV])
                    if g < 3:
                        if g > 0:
                            dve.wait_ge(od_step, ods[0])
                        V.tensor_tensor(o_w[:], src, cf, ALU.mult).then_inc(o_read, 1)
                        dve.wait_ge(o_read, 5 * l + g + 1)
                        odst(V.tensor_tensor(od[:, 2 * g:2 * g + 2], o_w[:, 0:4:2], o_w[:, 1:4:2], ALU.add))
                    else:
                        h0 = u0 - 2 * HEADS
                        dst = xn[:, :, h0 * MV:(h0 + un) * MV].rearrange("p t (u d) -> p u t d", u=un)
                        V.tensor_tensor(dst, src, cf, ALU.mult).then_inc(o_read, 1)

                for k in range(UNITS + 5):
                    if k < UNITS:
                        u = k
                        dve.wait_ge(s_mm, UNITS * l + u + 1)
                        if UNITS * l + u >= 2:
                            dve.wait_ge(exp_done, UNITS * l + u - 1)
                        if u < 2 * HEADS:
                            sc, bi = HD ** -0.5, bias[:, u // 2, :]
                        else:
                            sc, bi = QD ** -0.5, mask
                        if l == 0 and u == 0:
                            dve.wait_ge(setup_v, SETUP_V)
                        V.scalar_tensor_tensor(s_sb[:, u % 2, :], bank[u % 3][:, 0:3 * P], sc, bi,
                                               ALU.mult, ALU.add).then_inc(s_biased, 1)
                        dve.wait_ge(s_biased, UNITS * l + u + 1)
                        V.tensor_reduce(neg_max[:, u, 0:1], s_sb[:, u % 2, 0:P], AX.X, ALU.max,
                                        negate=True).then_inc(s_max, 1)
                        V.tensor_reduce(neg_max[:, u, 1:2], s_sb[:, u % 2, P:3 * P], AX.X, ALU.max,
                                        negate=True).then_inc(s_max, 1)
                    if k >= 8 and k % 4 == 0 and (k - 8) // 4 < 4:
                        normalise((k - 8) // 4)
                    if k == UNITS + 3:
                        normalise(4)
                    if k == 5:
                        dve.wait_ge(mid_mm, MID * l + 14)
                        mean = bank[7][:, 0:T].unsqueeze(1).broadcast_to([P, 2, T])
                        conv(V.scalar_tensor_tensor(cv[:, 1], mean, -1.0 / CONV, cv[:, 0], ALU.mult, ALU.add))
                    if k == 9:
                        dve.wait_ge(conv_act, CA * l + 4)
                        conv(V.tensor_tensor(cv[:, 0], cv[:, 1], ln_rs[:].unsqueeze(1).broadcast_to([P, 2, T]), ALU.mult))
                    if k == 11:
                        dve.wait_ge(conv_act, CA * l + 5)
                        conv(V.tensor_scalar(glu_e[:], glu_e[:], 1.0, None, ALU.add))
                        dve.wait_ge(conv_step, cs[0])
                        conv(V.reciprocal(glu_e[:], glu_e[:]))
                        dve.wait_ge(conv_step, cs[0])
                        conv(V.tensor_tensor(glu_a[:], glu_a[:], glu_e[:], ALU.mult))
                    if k == 15:
                        for c in range(2):
                            dve.wait_ge(cat_hi, 5 * l + 2)
                            V.scalar_tensor_tensor(hT_lo[:, c, :], bank[7][:, c * T:(c + 1) * T],
                                                   vecs[:, V_BPW + 2 * l + c:V_BPW + 2 * l + c + 1],
                                                   hT_hi[:, c, :].bitcast(F32), ALU.add, ALU.subtract).then_inc(cat_lo, 1)
                    if k == 19:
                        dve.wait_ge(od_act, l + 1)
                        odst(V.tensor_reduce(o_ss[:], od_sq[:], AX.X, ALU.add))
                        dve.wait_ge(od_step, ods[0])
                        odst(V.tensor_scalar(o_ms[:], o_ss[:], 1.0 / DV, LN_EPS, ALU.mult, ALU.add))
                    if k == 20:
                        dve.wait_ge(od_pow, l + 1)
                        odst(V.tensor_tensor(od_sq[:], od[:], o_rstd[:].unsqueeze(3).broadcast_to([P, HEADS, 2, DV]),
                                             ALU.mult))
                        dve.wait_ge(od_step, ods[0])
                        dst = xn[:, :, HEADS * MV:2 * HEADS * MV].rearrange("p t (h d) -> p h t d", h=HEADS)
                        gain = subln[:, l].unsqueeze(1).unsqueeze(1).broadcast_to([P, HEADS, 2, DV])
                        odst(V.tensor_tensor(dst, od_sq[:], gain, ALU.mult))
                for r3 in range(3):
                    dve.wait_ge(cat_hi, 5 * l + 3 + r3)
                    V.tensor_tensor(hT_lo[:, 2 + 2 * r3:4 + 2 * r3, :], bank[r3][:].rearrange("p (c t) -> p c t", c=2),
                                    hT_hi[:, 2 + 2 * r3:4 + 2 * r3, :].bitcast(F32), ALU.subtract).then_inc(cat_lo, 1)
                split(n0 + 12)
                add_to_x(out_done(l), bank[3:7])
                norm_ms(2 * l + 1)
                norm_rows(2 * l + 1)
                if l == 0:
                    f0 = n0 + NIN + NOUT
                    split(f0)
                    norm_evac(1, V_FFN)
                    split(f0 + 1)
                    for j, (kind, c) in enumerate(ORDER):
                        if j + 2 < NFF:
                            split(f0 + j + 2)
                        if kind == "U":
                            for f in range(2):
                                dve.wait_ge(sg_done, 2 * c + f + 1)
                                if c >= 2:
                                    dve.wait_ge(act_lo, 2 * (c - 2) + f + 1)
                                V.tensor_tensor(d_prod[:, c % 2, f, :], bank[(c % 2) * 2 + f][:, T:2 * T],
                                                d_sg[:, c % 2, f, :], ALU.mult).then_inc(prod_done, 1)
                            for f in range(2):
                                dve.wait_ge(act_hi, 2 * c + f + 1)
                                V.tensor_tensor(d_lo[:, c % 2, f, :], d_prod[:, c % 2, f, :],
                                                d_hi[:, c % 2, f, :].bitcast(F32), ALU.subtract).then_inc(act_lo, 1)
                    add_to_x(dense_done("D", NCH - 1), bank[4:8])
                else:
                    norm_evac(3, V_FFN + KT)

            dve.wait_ge(gfin_in, 16)
            dve.wait_ge(hT_mm, 16)
            for t in range(TT):
                V.tensor_tensor(xn[:, t, :], xn[:, t, :], g_bc[:], ALU.mult).then_inc(h_rows, 1)
            rv = [0]

            def step(ins, wait=True):
                rv[0] += 1
                ins.then_inc(route_v, 1)
                if wait:
                    dve.wait_ge(route_v, rv[0])

            dve.wait_ge(route_mm, 1)
            step(V.tensor_copy(lg[:], bank[4][:, 0:TT * NE].rearrange("p (t e) -> p t e", t=TT)))
            for t in range(TT):
                step(V.max(m8[:, t, :], lg[:, t, :]), wait=t == TT - 1)
            step(V.tensor_tensor(gap[:], m8[:, :, 1], m8[:, :, 0], ALU.subtract), wait=False)
            assert rv[0] == RV_GAP
            for t in range(TT):
                step(V.max_index(idx[:, t, :], m8[:, t, :], lg[:, t, :]), wait=t == TT - 1)
            step(V.tensor_copy(idf[:], idx[:]))
            for t in range(TT):
                for m in range(2):
                    step(V.tensor_scalar(oh[:, m, t, :], iota[:, 0:NE], idf[:, t, m:m + 1], None, ALU.is_equal),
                         wait=False)
            dve.wait_ge(route_v, rv[0])
            step(V.tensor_tensor(chosen[:], oh[:, 0], oh[:, 1], ALU.add), wait=False)
            assert rv[0] == RV_CHOSEN
            dve.wait_ge(route_a, 1)
            step(V.tensor_scalar(w_top[:, 2, :], e2[:], 1.0, None, ALU.add))
            step(V.reciprocal(w_top[:, 0, :], w_top[:, 2, :]))
            step(V.tensor_tensor(w_top[:, 1, :], e2[:], w_top[:, 0, :], ALU.mult))
            for t in range(TT):
                for m in range(2):
                    step(V.tensor_scalar(gw[:, m, t, :], oh[:, m, t, :], w_top[:, m, t:t + 1], None, ALU.mult),
                         wait=False)
            step(V.tensor_scalar(less1[:], chosen[:], -1.0, None, ALU.add), wait=False)
            step(V.memset(pos_item[:], -1.0), wait=False)
            step(V.memset(g_item[:], 0.0))
            step(V.tensor_tensor(g_item[:, :, 0:NE], gw[:, 0], gw[:, 1], ALU.add), wait=False)
            dve.wait_ge(route_mm, 2)
            step(V.tensor_copy(pos[:], bank[5][:, 0:TT * NE].rearrange("p (t e) -> p t e", t=TT)), wait=False)
            step(V.tensor_copy(cnt[:], bank[5][:, TT * NE:3 * NE]))
            step(V.tensor_tensor(pos[:], pos[:], chosen[:], ALU.mult), wait=False)
            step(V.tensor_scalar(over[:], cnt[:], float(P), None, ALU.is_gt))
            step(V.tensor_tensor(pos_m[:], pos[:], less1[:], ALU.add), wait=False)
            step(V.tensor_tensor_scan(incl[:], ones[:, 0:NE], over[:], 0.0, ALU.mult, ALU.add))
            step(V.tensor_copy(pos_item[:, :, 0:NE], pos_m[:]), wait=False)
            step(V.tensor_scalar(pos_hi[:], pos_m[:], -float(P), None, ALU.add), wait=False)
            step(V.tensor_tensor(rank[:], incl[:], over[:], ALU.subtract))
            for j in range(3):
                step(V.scalar_tensor_tensor(sel[:, j, :], rank[:], float(j), over[:], ALU.is_equal, ALU.mult),
                     wait=False)
            step(V.tensor_scalar(it_f[:, 0:1], incl[:, NE - 1:NE], float(NE), None, ALU.add))
            m = 0
            for j in range(3):
                for t in range(TT):
                    for src, dst in ((pos_hi, pos_item), (g_item, g_item)):
                        step(V.tensor_tensor_reduce(junk[:, m, :], sel[:, j, :], src[:, t, 0:NE], 1.0, 0.0, ALU.mult,
                                                    ALU.add, dst[:, t, NE + j:NE + j + 1]), wait=False)
                        m += 1
                step(V.tensor_tensor_reduce(junk[:, m, :], sel[:, j, :], iota[:, 0:NE], 1.0, 0.0, ALU.mult, ALU.add,
                                            it_f[:, 1 + j:2 + j]), wait=False)
                m += 1
            dve.wait_ge(route_v, rv[0])
            V.tensor_copy(it_i[:], it_f[:]).then_inc(items_ready, 1)

            def make_onehot(i):
                V.tensor_copy(p_col[:], pos_item[:, :, bass.ds(i, 1)].rearrange("p t o -> p (t o)")
                              ).then_inc(onehot_done, 1)
                dve.wait_ge(onehot_done, 1 + i * 3)
                for t in range(TT):
                    V.tensor_scalar(onehot[:, t, :], iota, p_col[:, t:t + 1], None, ALU.is_equal
                                    ).then_inc(onehot_done, 1)

            def gather_evac(i):
                for h in range(2):
                    dve.wait_ge(gather_mm, 4 * i + 3 + h)
                    V.tensor_copy(sel_lo[:, 4 * h:4 * h + 4, :], bank[h][:].rearrange("p (k s) -> p k s", k=4)
                                  ).then_inc(gather_lo, 1)

            make_onehot(0)
            dve.wait_ge(ht_split, 1)
            V.tensor_tensor(ht_lo[:], xn[:], ht_hi[:].bitcast(F32), ALU.subtract).then_inc(ht_split, 1)
            split_expert(0, 0)
            split_expert(0, 1)
            gather_evac(0)
            dve.wait_ge(items_ready, 1)
            n_items = dve.value_load(it_i[0:1, 0:1], min_val=NE, max_val=ITEMS_MAX)
            with dve.Fori(0, n_items) as i:
                for j, (kind, c) in enumerate(ORDER):
                    if j + 2 < NFF:
                        split_expert(i, j + 2)
                    else:
                        with dve.If(i < n_items - 1):
                            split_expert(i, j + 2)
                    if kind == "U":
                        dve.wait_ge(sg_done, GU0 + c + 1 + i * NCH)
                        if c >= 2:
                            dve.wait_ge(act_t, c - 1 + i * NCH)
                        V.tensor_tensor(m_prod[:, c % 2, :], bank[c % 2][:, FC:2 * FC], m_sg[:, c % 2, :],
                                        ALU.mult).then_inc(prod_done, 1)
                    tc = transposed_after(kind, c)
                    if tc is not None:
                        dve.wait_ge(act_hi, GU0 + tc + 1 + i * NCH)
                        V.tensor_tensor(m_lo[:, tc % 2, :, :], bank[2 + tc % 2][:, 0:2 * P].rearrange("p (f s) -> p f s", f=2),
                                        m_hi[:, tc % 2, :, :].bitcast(F32), ALU.subtract).then_inc(act_lo, 1)
                    if kind == "U" and c == 5:
                        dve.wait_ge(onehot_tmm, i + 1)
                        dve.wait_ge(x_upd, XU0 + 4 * i)
                        V.tensor_copy(g_col[:], g_item[:, :, bass.ds(i, 1)].rearrange("p t o -> p (t o)")
                                      ).then_inc(route_v, 1)
                        dve.wait_ge(gather_mm, 4 + 4 * i)
                        dve.wait_ge(onehot_done, 3 + 3 * i)
                        make_onehot(i + 1)
                gather_evac(i + 1)
                for h in range(2):
                    dve.wait_ge(yhi_done, 2 * i + 1 + h)
                    V.tensor_tensor(y_lo[:, h * 512:(h + 1) * 512], bank[4 + h][:],
                                    y_hi[:, h * 512:(h + 1) * 512].bitcast(F32), ALU.subtract).then_inc(ylo_done, 1)
                dve.wait_ge(route_v, rv[0] + 1 + i)
                for q in range(4):
                    t, n = q // 2, q % 2
                    dve.wait_ge(scat_mm, 4 * i + q + 1)
                    dve.wait_ge(x_upd, XU0 - 3 + q + 4 * i)
                    xs = x[:, t, n * 512:(n + 1) * 512]
                    V.scalar_tensor_tensor(xs, bank[6 + q % 2][:], g_col[:, t:t + 1], xs, ALU.mult, ALU.add
                                           ).then_inc(x_upd, 1)
            norm_ms(4)
            dve.wait_ge(rstd_ready, 5)
            dve.wait_ge(gfin_in, 32)
            for t in range(TT):
                V.scalar_tensor_tensor(xn[:, t, :], x[:, t, :], rstd[:, t:t + 1], g_bc[:], ALU.mult, ALU.mult
                                       ).then_inc(xn_ready, 1)

        @block.tensor
        def _(pe):
            M = nc.tensor.matmul

            def mm3(o, lh, ll, rh, rl, start, stop):
                M(o, lh, rh, start=start, stop=False)
                M(o, lh, rl, start=False, stop=False)
                return M(o, ll, rh, start=False, stop=stop)

            def norm_transposes(j):
                for b in range(4):
                    if b == 0:
                        pe.wait_ge(xn_ready, TT * (j + 1))
                    for kk in range(2):
                        for t in range(TT):
                            k = 2 * b + kk
                            r = nc.tensor.transpose(bank[b][:, kk * T + t * P:kk * T + (t + 1) * P],
                                                    xn[:, t, k * P:(k + 1) * P], ident)
                    r.then_inc(hT_mm, 1)

            pe.wait_ge(early_in, 16 * N_EARLY)
            pe.wait_ge(const_set, 5)
            for l in range(LAYERS):
                n0 = LAYER_PIECE0[l]
                norm_transposes(2 * l)
                if l == 0:
                    nc.tensor.transpose(bank[4][:, 0:V_END], vec_rows[:], ident[0:V_END, 0:V_END]).then_inc(setup_t, 1)
                    pe.wait_ge(params_in, 16 * N_PARAMS)
                    nt = LAYERS * TAPS
                    for c in range(2):
                        r = nc.tensor.transpose(bank[7][:, c * nt:(c + 1) * nt], dw_rows[:, c * P:(c + 1) * P],
                                                ident[0:nt, 0:nt])
                    r.then_inc(setup_t, 1)

                def mid_start(g):
                    gp = g - 4
                    if gp in MID_ACT:
                        pe.wait_ge(mid_act, ACT_MID_STEPS * l + MID_ACT[gp])
                    else:
                        pe.wait_ge(mid_dve, DVE_MID_STEPS * l + MID_DVE[gp])

                def project(p):
                    n = n0 + p
                    pe.wait_ge(lo_ready, n + 1)
                    if p == 0:
                        pe.wait_ge(hTlo_done, KT * (2 * l + 1))
                    if p >= 4:
                        pe.wait_ge(proj_evac, NIN * l + p - 3)
                    elif l == 0 and p in (0, 3):
                        pe.wait_ge(setup_a, 1 if p == 0 else 2)
                    b = bank[4 + p % 4]
                    wh, wl = in_piece_view(hi_of(n), p), in_piece_view(lo_of(n), p)
                    if p < 7:
                        cols = [(0, P), (P, P)] if p != 3 else [(0, P), (KR - NOPE, QD)]
                        for m, (c0, cn) in enumerate(cols):
                            for k in range(KT):
                                r = mm3(b[0:cn, m * T:(m + 1) * T], wh[:, k, c0:c0 + cn], wl[:, k, c0:c0 + cn],
                                        hT_hi[:, k, :], hT_lo[:, k, :], k == 0, k == KT - 1)
                    else:
                        for t in range(TT):
                            for k in range(KT):
                                tok = slice(t * P, (t + 1) * P)
                                r = mm3(b[:, t * 192:(t + 1) * 192], hT_hi[:, k, tok], hT_lo[:, k, tok],
                                        wh[:, k, :], wl[:, k, :], k == 0, k == KT - 1)
                    r.then_inc(piece_used, 1)

                for p in range(NIN):
                    project(p)
                    if p == 4:
                        pe.wait_ge(proj_evac, NIN * l + 4)
                        for c in range(2):
                            M(bank[0][:, 0:T], ones[:], sq_q[:, c, :], start=c == 0, stop=c == 1)
                        M(bank[0][:, T:2 * T], ones[:], sq_kv[:], start=True, stop=True).then_inc(mid_mm, 1)
                    if p == 6:
                        pe.wait_ge(small_in, 48 * (l + 1))
                        pe.wait_ge(mid_dve, DVE_MID_STEPS * l + 3)
                        for r3 in range(3):
                            for hh in range(2):
                                h = 2 * r3 + hh
                                for c in range(2):
                                    r = M(bank[1 + r3][0:QD, hh * T:(hh + 1) * T], w_uq[:, c, h * QD:(h + 1) * QD],
                                          cq[:, c, :], start=c == 0, stop=c == 1)
                            r.then_inc(mid_mm, 1)
                        mid_start(4)
                        M(bank[0][0:QD, 0:T], rotate, kr[:], start=True, stop=True).then_inc(mid_mm, 1)
                for t in range(TT):
                    mid_start(5 + t)
                    wv = w_ukv[:].rearrange("p (h n) -> p h n", h=HEADS)[:, :, NOPE:]
                    M(bank[1 + t][:, 0:HEADS * MV], ckv[:, t * P:(t + 1) * P], wv, start=True, stop=True
                      ).then_inc(mid_mm, 1)
                for r3 in range(3):
                    mid_start(7 + r3)
                    for hh in range(2):
                        h = 2 * r3 + hh
                        r = M(bank[MID_BANK[7 + r3]][0:NOPE, hh * T:(hh + 1) * T], w_ukv[:, h * KVD:h * KVD + NOPE], ckv[:],
                              start=True, stop=True)
                    r.then_inc(mid_mm, 1)
                for r3 in range(3):
                    mid_start(10 + r3)
                    M(bank[MID_BANK[10 + r3]][0:QD, :], rotate, q_m[:, 2 * r3:2 * r3 + 2, :].rearrange("p h t -> p (h t)"),
                      start=True, stop=True).then_inc(mid_mm, 1)

                def scores(u):
                    if u == 0:
                        pe.wait_ge(proj_evac, NIN * (l + 1))
                        pe.wait_ge(mid_dve, DVE_MID_STEPS * (l + 1))
                        pe.wait_ge(mid_act, ACT_MID_STEPS * (l + 1))
                    if u >= 3:
                        pe.wait_ge(s_biased, UNITS * l + u - 2)
                    if u < 2 * HEADS:
                        h, half = u // 2, u % 2
                        r0 = (h % 2) * DV + half * HD
                        q, kk = dqk[r0:r0 + HD, h // 2, :], dqk[r0:r0 + HD, 3 + h // 2, :]
                    else:
                        q, kk = q_m[:, u - 2 * HEADS, :], k_m[:, u - 2 * HEADS, :]
                    M(bank[u % 3][:, 0:P], q[:, 0:P], kk[:, 0:P], start=True, stop=True)
                    M(bank[u % 3][:, P:3 * P], q[:, P:2 * P], kk[:, :], start=True, stop=True).then_inc(s_mm, 1)

                def transposes(u):
                    pe.wait_ge(exp_done, UNITS * l + u + 1)
                    if u >= 2:
                        pe.wait_ge(pt_ready, UNITS * l + u - 1)
                    for b in range(3):
                        r = nc.tensor.transpose(bank[3 + u % 2][:, b * P:(b + 1) * P], e_sb[:, u % 2, b * P:(b + 1) * P],
                                                ident)
                    r.then_inc(pt_mm, 1)

                def values(u):
                    g = u // 4
                    pe.wait_ge(pt_ready, UNITS * l + u + 1)
                    if u % 4 == 0 and g >= 2:
                        pe.wait_ge(o_read, 5 * l + g - 1)
                    v = dv if u < 2 * HEADS else v_m
                    h = u // 2 if u < 2 * HEADS else u - 2 * HEADS
                    o = bank[5 + g % 2][:, (u % 4) * P:(u % 4 + 1) * P]
                    pt = pt_sb[:, u % 2, :]
                    M(o[:, 0:DV], pt[:, 0:P], v[:, 0, h * DV:(h + 1) * DV], start=True, stop=True)
                    M(o[:, DV:2 * DV], pt[:, P:2 * P], v[:, 0, h * DV:(h + 1) * DV], start=True, stop=False)
                    M(o[:, DV:2 * DV], pt[:, 2 * P:3 * P], v[:, 1, h * DV:(h + 1) * DV], start=False, stop=True
                      ).then_inc(pv_mm, 1)

                for k in range(UNITS + 3):
                    if k < UNITS:
                        scores(k)
                    if 2 <= k < UNITS + 2:
                        transposes(k - 2)
                    if k >= 3:
                        values(k - 3)
                    if k == 4:
                        pe.wait_ge(conv_step, CS * l + CS_TAPS)
                        for c in range(2):
                            r = M(bank[7][:, 0:T], ones[:], cv[:, 0, c, :], start=c == 0, stop=c == 1)
                        r.then_inc(mid_mm, 1)
                    if k == 7:
                        pe.wait_ge(conv_act, CA * l + 2)
                        for c in range(2):
                            r = M(bank[7][:, 0:T], ones[:], glu_e[:, c, :], start=c == 0, stop=c == 1)
                        r.then_inc(mid_mm, 1)
                    if k == 13:
                        pe.wait_ge(conv_step, CS * (l + 1))
                        for m in range(2):
                            for c in range(2):
                                r = M(bank[7][:, m * T:(m + 1) * T], w_pw[:, c, m * P:(m + 1) * P], glu_a[:, c, :],
                                      start=c == 0, stop=c == 1)
                        r.then_inc(mid_mm, 1)
                pe.wait_ge(o_read, 5 * (l + 1))
                pe.wait_ge(od_step, OD_STEPS * (l + 1))
                for r3 in range(3):
                    for kk in range(2):
                        for t in range(TT):
                            c0 = (2 * r3 + kk) * P
                            r = nc.tensor.transpose(bank[r3][:, kk * T + t * P:kk * T + (t + 1) * P],
                                                    xn[:, t, c0:c0 + P], ident)
                    r.then_inc(yT_mm, 1)
                for i in range(NOUT):
                    n = n0 + NIN + i
                    pe.wait_ge(lo_ready, n + 1)
                    pe.wait_ge(cat_lo, 5 * l + 2 + i)
                    wh, wl = ff_view(hi_of(n), "D"), ff_view(lo_of(n), "D")
                    for kk in range(2):
                        k = 2 * i + kk
                        for q in range(4):
                            t, nn = q // 2, q % 2
                            r = mm3(bank[3 + q][:], hT_hi[:, k, t * P:(t + 1) * P], hT_lo[:, k, t * P:(t + 1) * P],
                                    wh[:, kk, nn * 512:(nn + 1) * 512], wl[:, kk, nn * 512:(nn + 1) * 512],
                                    k == 0, k == KT - 1)
                    r.then_inc(piece_used, 1)
                norm_transposes(2 * l + 1)
                if l == 0:
                    f0 = n0 + NIN + NOUT
                    pe.wait_ge(hTlo_done, 2 * KT)
                    for j, (kind, c) in enumerate(ORDER):
                        n = f0 + j
                        pe.wait_ge(lo_ready, n + 1)
                        wh, wl = ff_view(hi_of(n), kind), ff_view(lo_of(n), kind)
                        if kind == "D":
                            pe.wait_ge(act_lo, 2 * c + 2)
                            for f in range(2):
                                for q in range(4):
                                    t, nn = q // 2, q % 2
                                    tok = slice(t * P, (t + 1) * P)
                                    r = mm3(bank[4 + q][:], d_hi[:, c % 2, f, tok], d_lo[:, c % 2, f, tok],
                                            wh[:, f, nn * 512:(nn + 1) * 512], wl[:, f, nn * 512:(nn + 1) * 512],
                                            c == 0 and f == 0, c == NCH - 1 and f == 1)
                            r.then_inc(piece_used, 1)
                        else:
                            if kind == "G" and c >= 2:
                                pe.wait_ge(prod_done, 2 * (c - 1))
                            for f in range(2):
                                o = bank[(c % 2) * 2 + f][:, 0:T] if kind == "G" else bank[(c % 2) * 2 + f][:, T:2 * T]
                                for k in range(KT):
                                    r = mm3(o, wh[:, k, f * P:(f + 1) * P], wl[:, k, f * P:(f + 1) * P],
                                            hT_hi[:, k, :], hT_lo[:, k, :], k == 0, k == KT - 1)
                            r.then_inc(piece_used, 1)
            pe.wait_ge(hTlo_done, 4 * KT)
            pe.wait_ge(setup_v, SETUP_V)
            for t in range(TT):
                tok = slice(t * P, (t + 1) * P)
                for k in range(KT):
                    for m, (lh, rh) in enumerate([(hT_hi, wr_hi), (hT_hi, wr_lo), (hT_lo, wr_hi), (hT_lo, wr_lo)]):
                        r = M(bank[4][:, t * NE:(t + 1) * NE], lh[:, k, tok], rh[:, k, :],
                              start=k == 0 and m == 0, stop=k == KT - 1 and m == 3)
            r.then_inc(route_mm, 1)
            pe.wait_ge(route_v, RV_CHOSEN)
            M(bank[5][:, 0:NE], upper, chosen[:, 0, :], start=True, stop=True)
            M(bank[5][:, NE:2 * NE], ones[:], chosen[:, 0, :], start=True, stop=False)
            M(bank[5][:, NE:2 * NE], upper, chosen[:, 1, :], start=False, stop=True)
            M(bank[5][:, 2 * NE:3 * NE], ones[:], chosen[:, 0, :], start=True, stop=False)
            M(bank[5][:, 2 * NE:3 * NE], ones[:], chosen[:, 1, :], start=False, stop=True).then_inc(route_mm, 1)

            def gather(i):
                pe.wait_ge(onehot_done, 3 + 3 * i)
                for src, b0 in ((ht_hi, 6), (ht_lo, 0)):
                    for h in range(2):
                        for kk in range(4):
                            k = 4 * h + kk
                            for t in range(TT):
                                r = M(bank[b0 + h][:, kk * P:(kk + 1) * P], src[:, t, k * P:(k + 1) * P],
                                      onehot[:, t, :], start=t == 0, stop=t == TT - 1)
                        r.then_inc(gather_mm, 1)

            def transpose_act(i, c):
                pe.wait_ge(prod_done, GU0 + c + 1 + i * NCH)
                pe.wait_ge(act_lo, GU0 + c - 1 + i * NCH)
                for f in range(2):
                    r = nc.tensor.transpose(bank[2 + c % 2][:, f * P:(f + 1) * P], m_prod[:, c % 2, f * P:(f + 1) * P],
                                            ident)
                r.then_inc(act_t, 1)

            pe.wait_ge(ht_split, 2)
            gather(0)
            pe.wait_ge(items_ready, 1)
            n_items = pe.value_load(it_i[0:1, 0:1], min_val=NE, max_val=ITEMS_MAX)
            with pe.Fori(0, n_items) as i:
                for j, (kind, c) in enumerate(ORDER):
                    pe.wait_ge(lo_ready, NA + j + 1 + i * NFF)
                    wh, wl = ff_view(hi_of(NA + j), kind), ff_view(lo_of(NA + j), kind)
                    if kind == "D":
                        if c == NCH - 1:
                            transpose_act(i, c)
                            pe.wait_ge(onehot_tdone, i + 1)
                            gather(i + 1)
                        pe.wait_ge(act_lo, GU0 + c + 1 + i * NCH)
                        for f in range(2):
                            for n in range(2):
                                r = mm3(bank[4 + n][:], m_hi[:, c % 2, f, :], m_lo[:, c % 2, f, :],
                                        wh[:, f, n * 512:(n + 1) * 512], wl[:, f, n * 512:(n + 1) * 512],
                                        c == 0 and f == 0, c == NCH - 1 and f == 1)
                    else:
                        if kind == "G" and c == 0:
                            pe.wait_ge(gather_hi, 2 + 2 * i)
                            pe.wait_ge(gather_lo, 2 + 2 * i)
                        elif kind == "G" and c >= 2:
                            pe.wait_ge(prod_done, GU0 + c - 1 + i * NCH)
                        o = bank[c % 2][:, 0:FC] if kind == "G" else bank[c % 2][:, FC:2 * FC]
                        for k in range(KT):
                            r = mm3(o, sel_hi[:, k, :], sel_lo[:, k, :], wh[:, k, :], wl[:, k, :], k == 0, k == KT - 1)
                    r.then_inc(piece_used, 1)
                    if kind == "G" and c >= 1:
                        transpose_act(i, c - 1)
                    if kind == "U" and c == 1:
                        pe.wait_ge(x_upd, XU0 + 4 * i)
                        for t in range(TT):
                            r = nc.tensor.transpose(bank[6][:, t * P:(t + 1) * P], onehot[:, t, :].bitcast(F32), ident)
                        r.then_inc(onehot_tmm, 1)
                for q in range(4):
                    t, n = q // 2, q % 2
                    if q < 2:
                        pe.wait_ge(gather_hi, 4 + 2 * i)
                        pe.wait_ge(ylo_done, 2 * i + n + 1)
                    else:
                        pe.wait_ge(x_upd, XU0 + q - 1 + 4 * i)
                    b = bank[6 + q % 2]
                    M(b[:], onehot_t[:, t, :], y_hi[:, n * 512:(n + 1) * 512], start=True, stop=False)
                    M(b[:], onehot_t[:, t, :], y_lo[:, n * 512:(n + 1) * 512], start=False, stop=True
                      ).then_inc(scat_mm, 1)


_INS = ["x", "attn_norm", "w_in", "b_glu", "w_dw", "b_dw", "conv_ln_g", "conv_ln_b", "w_pw", "b_pw", "q_norm", "w_uq",
        "kv_norm", "w_ukv", "lambda_q1", "lambda_k1", "lambda_q2", "lambda_k2", "diff_subln", "w_out", "ffn_norm",
        "w_gate_dense", "w_up_dense", "w_down_dense", "w_router", "w_gate_exp", "w_up_exp", "w_down_exp", "final_norm"]


def kernel(**inputs):
    import concourse.bacc as bacc
    from concourse.bass_utils import run_bass_kernel_spmd as run

    nc = bacc.Bacc("TRN2", target_bir_lowering=False, num_devices=1)
    arrays = {name: np.ascontiguousarray(inputs[name]) for name in _INS}
    arrays["table1"], arrays["table2"] = tables()
    a = {name: nc.dram_tensor(f"in_{name}", v.shape, F32, kind="ExternalInput").ap() for name, v in arrays.items()}
    out = nc.dram_tensor("out", (1, T, D), F32, kind="ExternalOutput").ap()
    build(nc, a, out)
    r = run(nc, [{f"in_{name}": v for name, v in arrays.items()}], core_ids=[0])
    return r.results[0]["out"]
```

```python
import math
from contextlib import ExitStack

import numpy as np

import concourse.bass as bass
from concourse import mybir

ALU = mybir.AluOpType
ACT = mybir.ActivationFunctionType
AX = mybir.AxisListType
F32 = mybir.dt.float32
F32R = mybir.dt.float32r
I32 = mybir.dt.int32
U32 = mybir.dt.uint32

P = 128
D = 1024
T = 256
TT = T // P
KT = D // P
LAYERS = 2
CONV = 256
TAPS = 31
NOPE, ROPE, MV = 64, 32, 64
QR, KR = 256, 128
HEADS = 6
QD = NOPE + ROPE
KVD = NOPE + MV
HD, DV = 32, 64
FF = 2816
NE = 8
RMS_EPS, LN_EPS = 1e-6, 1e-5
MASKED = -1e30

C_CQ = 2 * CONV
C_CKV = C_CQ + QR
C_KR = C_CKV + KR
C_DQ = C_KR + ROPE
C_DV = C_DQ + 2 * HEADS * DV
IN_COLS = C_DV + HEADS * DV
IN_PIECES = [(0, 256), (256, 256), (C_CQ, 256), (C_CKV, KR + ROPE), (C_DQ, 256), (C_DQ + 256, 256),
             (C_DQ + 512, 256), (C_DV, 192), (C_DV + 192, 192)]
NIN = len(IN_PIECES)
NOUT = 4
FC = 256
NCH = FF // FC
NFF = 3 * NCH
PIECE = 2048
RAW_A, RAW_M, SPLIT = 4, 11, 3
NA = 2 * (NIN + NOUT) + NFF
ITEMS_MAX = NE + 3
LAYER_PIECE0 = [0, NIN + NOUT + NFF]


N_EARLY = 10
N_PARAMS = 8
MID = 16
OD_STEPS = 7

MID_BANK = [0, 1, 2, 3, 0, 1, 2, 3, 0, 1, 2, 3, 0, 7, 7, 7]
MID_ACT = {0: 1, 1: 2, 2: 3, 3: 4, 5: 5, 6: 6, 7: 7, 8: 8, 9: 9}
ACT_MID_STEPS = 10
DVE_MID_STEPS = 15
MID_DVE = {4: 5, 10: 8, 11: 11, 12: 14}

UNITS = 3 * HEADS
CA = 5
CS_U = 5
CS_TAPS = CS_U - 1 + TAPS * 2
CS_CENTRED = CS_TAPS + 1
CS_NORMED = CS_CENTRED + 1
CS = CS_NORMED + 3
RV_GAP, RV_CHOSEN = 5, 13
GU0 = 2 * NCH
XU0 = 12

CR = 8
SETUP_V = 5 + 2 * LAYERS + HEADS


def ff_order():
    order = [("G", 0), ("U", 0)]
    for c in range(1, NCH):
        order += [("G", c), ("U", c), ("D", c - 1)]
    return order + [("D", NCH - 1)]


ORDER = ff_order()

OUT_ORDER = [3, 0, 2, 1]
V_ATTN, V_BGLU, V_BDW, V_LNG, V_LNB, V_BPW, V_QN, V_KVN, V_FFN, V_END = 0, 16, 24, 28, 32, 36, 40, 44, 46, 62

K_ID = 0
K_U = K_ID + P
K_IOTA = K_U + P
K_R = K_IOTA + P
K_END1 = K_R + QD
K_MASK = 0
K_DIST = K_MASK + 3 * P
K_COS = K_DIST + 3 * P
K_SIN = K_COS + T
K_END2 = K_SIN + T


def tables():
    one = np.zeros((P, K_END1), np.float32)
    one[:, K_ID:K_ID + P] = np.eye(P)
    one[:, K_U:K_U + P] = np.triu(np.ones((P, P)), 1)
    one[:, K_IOTA:K_IOTA + P] = np.arange(P)
    half = ROPE // 2
    for a in range(half):
        one[NOPE + half + a, K_R + NOPE + a] = -1.0
        one[NOPE + a, K_R + NOPE + half + a] = 1.0
    two = np.zeros((P, K_END2), np.float32)
    q = np.arange(P)[:, None]
    dist = np.concatenate([q - np.arange(P)[None], q + P - np.arange(T)[None]], 1)
    two[:, K_MASK:K_MASK + 3 * P] = np.where(dist < 0, MASKED, 0.0)
    two[:, K_DIST:K_DIST + 3 * P] = np.maximum(dist, 0)
    freq = np.float32(10000.0) ** (-np.arange(half, dtype=np.float32) / np.float32(half))
    ang = np.arange(T, dtype=np.float32)[None, :] * freq[:, None].astype(np.float32)
    two[:NOPE, K_COS:K_COS + T] = 1.0
    for r in range(2):
        lo = NOPE + r * half
        two[lo:lo + half, K_COS:K_COS + T] = np.cos(ang)
        two[lo:lo + half, K_SIN:K_SIN + T] = np.sin(ang)
    return one, two


def build(nc, a, out):
    with ExitStack() as ctx:
        region = [ctx]

        def sb(name, shape, dt=F32):
            return region[0].enter_context(nc.sbuf_tensor(name, shape, dt))

        def sem(name):
            return ctx.enter_context(nc.semaphore(name))

        bank = [ctx.enter_context(nc.psum_tensor(f"bank{i}", [P, 512], F32)) for i in range(8)]

        hi_ring = sb("hi_ring", [P, SPLIT, PIECE], F32R)
        lo_ring = sb("lo_ring", [P, SPLIT, PIECE], F32R)
        raw_a = sb("raw_a", [P, RAW_A, PIECE])
        x = sb("x", [P, TT, D])
        xn = sb("xn", [P, TT, D])
        hT_hi = sb("hT_hi", [P, KT, T], F32R)
        hT_lo = sb("hT_lo", [P, KT, T], F32R)
        consts = sb("consts", [P, K_END1])
        ones = sb("ones", [P, P])
        vecs = sb("vecs", [P, V_END])
        neg_vecs = sb("neg_vecs", [P, V_END])
        ss = sb("ss", [P, TT])
        ms = sb("ms", [P, TT])
        rstd = sb("rstd", [P, TT])
        half_neg = sb("half_neg", [P, 2 * HEADS])
        eps_rms = sb("eps_rms", [P, 1])
        eps_ln = sb("eps_ln", [P, 1])
        wr = sb("wr", [P, KT, NE])
        wr_parts = sb("wr_parts", [P, KT, 2, NE], F32R)

        mixers = ExitStack()
        region[0] = mixers
        w_pw = sb("w_pw", [P, 2, CONV])
        w_uq = sb("w_uq", [P, 2, HEADS * QD])
        w_ukv = sb("w_ukv", [P, HEADS * KVD])
        tabs = sb("tabs", [P, K_END2])
        bias = sb("bias", [P, HEADS, 3 * P])
        vec_rows = sb("vec_rows", [V_END, P])
        dw_rows = sb("dw_rows", [LAYERS * TAPS, CONV])
        dw = sb("dw", [P, 2, LAYERS * TAPS])
        subln = sb("subln", [P, LAYERS, DV])
        lam_in = sb("lam_in", [P, 4, LAYERS, HD])
        lam_prod = sb("lam_prod", [P, 2, LAYERS, HD])
        lam_dot = sb("lam_dot", [P, 2, LAYERS])
        lam_exp = sb("lam_exp", [P, 2, LAYERS])
        neg_lam = sb("neg_lam", [P, LAYERS])
        temps = ExitStack()
        region[0] = temps
        cq = sb("cq", [P, 2, T])
        ckv = sb("ckv", [P, T])
        kr = sb("kr", [QD, T])
        sq_q = sb("sq_q", [P, 2, T])
        sq_kv = sb("sq_kv", [P, T])
        rs = sb("rs", [P, 2, T])
        dqk = sb("dqk", [P, 6, T])
        dv = sb("dv", [P, TT, HEADS * DV])
        q_m = sb("q_m", [QD, HEADS, T])
        rot = sb("rot", [QD, 2, T])
        k_m = sb("k_m", [QD, HEADS, T])
        v_m = sb("v_m", [P, TT, HEADS * MV])
        glu_a = sb("glu_a", [P, 2, T])
        glu_e = sb("glu_e", [P, 2, T])
        u_pad = sb("u_pad", [P, 2, TAPS - 1 + T])
        cv = sb("cv", [P, 2, 2, T])
        ln_rs = sb("ln_rs", [P, T])
        s_sb = sb("s_sb", [P, 2, 3 * P])
        e_sb = sb("e_sb", [P, 2, 3 * P])
        pt_sb = sb("pt_sb", [P, 2, 3 * P])
        neg_max = sb("neg_max", [P, 3 * HEADS, 2])
        row_sum = sb("row_sum", [P, 3 * HEADS, 2])
        coef = sb("coef", [P, 3 * HEADS, 2])
        o_w = sb("o_w", [P, 4, 2, DV])
        od = sb("od", [P, HEADS, 2, DV])
        od_sq = sb("od_sq", [P, HEADS, 2, DV])
        o_ss = sb("o_ss", [P, HEADS, 2])
        o_ms = sb("o_ms", [P, HEADS, 2])
        o_rstd = sb("o_rstd", [P, HEADS, 2])
        temps.close()
        dense = ExitStack()
        region[0] = dense
        d_sg = sb("d_sg", [P, 2, 2, T])
        d_prod = sb("d_prod", [P, 2, 2, T])
        d_hi = sb("d_hi", [P, 2, 2, T], F32R)
        d_lo = sb("d_lo", [P, 2, 2, T], F32R)
        dense.close()
        mixers.close()
        region[0] = ctx
        raw_m = sb("raw_m", [P, RAW_M - RAW_A, PIECE])
        ht_hi = sb("ht_hi", [P, TT, D], F32R)
        ht_lo = sb("ht_lo", [P, TT, D], F32R)
        g_bc = sb("g_bc", [P, D])
        lg_t = sb("lg_t", [2 * NE, T])
        lg = sb("lg", [P, TT, NE])
        m8 = sb("m8", [P, TT, NE])
        idx = sb("idx", [P, TT, NE], U32)
        idf = sb("idf", [P, TT, NE])
        gap = sb("gap", [P, TT])
        e2 = sb("e2", [P, TT])
        w_top = sb("w_top", [P, 3, TT])
        oh = sb("oh", [P, 2, TT, NE])
        gw = sb("gw", [P, 2, TT, NE])
        chosen = sb("chosen", [P, TT, NE])
        less1 = sb("less1", [P, TT, NE])
        pos = sb("pos", [P, TT, NE])
        pos_m = sb("pos_m", [P, TT, NE])
        pos_hi = sb("pos_hi", [P, TT, NE])
        cnt = sb("cnt", [P, NE])
        over = sb("over", [P, NE])
        incl = sb("incl", [P, NE])
        rank = sb("rank", [P, NE])
        sel = sb("sel", [P, 3, NE])
        junk = sb("junk", [P, 15, NE])
        it_f = sb("it_f", [P, 4])
        it_i = sb("it_i", [P, 4], I32)
        pos_item = sb("pos_item", [P, TT, ITEMS_MAX + 1])
        g_item = sb("g_item", [P, TT, ITEMS_MAX + 1])
        p_col = sb("p_col", [P, TT])
        g_col = sb("g_col", [P, TT])
        onehot = sb("onehot", [P, TT, P], F32R)
        onehot_t = sb("onehot_t", [P, TT, P], F32R)
        m_sg = sb("m_sg", [P, 2, FC])
        m_prod = sb("m_prod", [P, 2, FC])
        m_hi = sb("m_hi", [P, 2, 2, P], F32R)
        m_lo = sb("m_lo", [P, 2, 2, P], F32R)
        sel_hi = hT_hi[:, 0:4, :].rearrange("p a b -> p (a b)").rearrange("p (k s) -> p k s", k=KT)
        sel_lo = hT_lo[:, 0:4, :].rearrange("p a b -> p (a b)").rearrange("p (k s) -> p k s", k=KT)
        y_hi = hT_hi[:, 4:8, :].rearrange("p a b -> p (a b)")
        y_lo = hT_lo[:, 4:8, :].rearrange("p a b -> p (a b)")

        ident = consts[:, K_ID:K_ID + P]
        upper = consts[:, K_U:K_U + P]
        iota = consts[:, K_IOTA:K_IOTA + P]
        rotate = consts[0:QD, K_R:K_R + QD]
        mask = tabs[:, K_MASK:K_MASK + 3 * P]
        dist = tabs[:, K_DIST:K_DIST + 3 * P]
        cos = tabs[0:QD, K_COS:K_COS + T]
        sin = tabs[0:QD, K_SIN:K_SIN + T]

        x_in = [sem(f"x_in{t}") for t in range(TT)]
        early_in = sem("early_in")
        params_in = sem("params_in")
        small_in = sem("small_in")
        raw_in = [sem(f"raw_in{s}") for s in range(RAW_M)]
        gfin_in = sem("gfin_in")
        out_sent = sem("out_sent")
        hi_ready = sem("hi_ready")
        lo_ready = sem("lo_ready")
        piece_used = sem("piece_used")
        const_set = sem("const_set")
        setup_t = sem("setup_t")
        setup_v = sem("setup_v")
        setup_a = sem("setup_a")
        sumsq = sem("sumsq")
        ms_ready = sem("ms_ready")
        rstd_ready = sem("rstd_ready")
        xn_ready = sem("xn_ready")
        hT_mm = sem("hT_mm")
        hThi_done = sem("hThi_done")
        hTlo_done = sem("hTlo_done")
        proj_evac = sem("proj_evac")
        mid_mm = sem("mid_mm")
        mid_act = sem("mid_act")
        mid_dve = sem("mid_dve")
        conv_step = sem("conv_step")
        conv_act = sem("conv_act")
        s_mm = sem("s_mm")
        s_biased = sem("s_biased")
        s_max = sem("s_max")
        exp_done = sem("exp_done")
        pt_mm = sem("pt_mm")
        pt_ready = sem("pt_ready")
        pv_mm = sem("pv_mm")
        coef_ready = sem("coef_ready")
        o_read = sem("o_read")
        od_step = sem("od_step")
        od_act = sem("od_act")
        od_pow = sem("od_pow")
        yT_mm = sem("yT_mm")
        cat_hi = sem("cat_hi")
        cat_lo = sem("cat_lo")
        acc_part = sem("acc_part")
        x_upd = sem("x_upd")
        sg_done = sem("sg_done")
        prod_done = sem("prod_done")
        act_t = sem("act_t")
        act_hi = sem("act_hi")
        act_lo = sem("act_lo")
        route_mm = sem("route_mm")
        route_v = sem("route_v")
        route_a = sem("route_a")
        items_ready = sem("items_ready")
        onehot_done = sem("onehot_done")
        gather_mm = sem("gather_mm")
        gathered = sem("gathered")
        onehot_tmm = sem("onehot_tmm")
        onehot_tdone = sem("onehot_tdone")
        yhi_done = sem("yhi_done")
        ylo_done = [sem(f"ylo_done{h}") for h in range(2)]
        scat_mm = [sem(f"scat_mm{q}") for q in range(4)]
        logits_mm = sem("logits_mm")
        logits_out = sem("logits_out")
        h_rows = sem("h_rows")
        ht_split = sem("ht_split")
        ht_lo_done = sem("ht_lo_done")

        block = ctx.enter_context(nc.Block())

        def raw_slot(n):
            return raw_a[:, n % RAW_A, :], raw_in[n % RAW_A], 16 * (n // RAW_A + 1)

        trunk_uses = [len(range(s, NA, RAW_A)) if s < RAW_A else 0 for s in range(RAW_M)]

        def expert_slot(i, j):
            s = j % RAW_M
            tile = raw_a[:, s, :] if s < RAW_A else raw_m[:, s - RAW_A, :]
            return tile, raw_in[s], 16 * (trunk_uses[s] + j // RAW_M + 1) + i * (16 * NFF // RAW_M)

        def in_piece_view(t, p):
            c = IN_PIECES[p][1]
            return t[:, 0:KT * c].rearrange("p (k n) -> p k n", k=KT)

        def ff_src(wg, wu, wd, kind, c):
            if kind == "D":
                return wd[c * FC:(c + 1) * FC, :].rearrange("(k p) n -> p k n", p=P)
            w = wg if kind == "G" else wu
            return w[:, c * FC:(c + 1) * FC].rearrange("(k p) n -> p k n", p=P)

        def ff_view(t, kind):
            return t.rearrange("p (k n) -> p k n", n=D if kind == "D" else FC)

        def in_done(l, p):
            return LAYER_PIECE0[l] + p + 1

        def out_done(l):
            return LAYER_PIECE0[l] + NIN + NOUT

        def dense_done(kind, c):
            return LAYER_PIECE0[0] + NIN + NOUT + ORDER.index((kind, c)) + 1

        def expert_done(i, kind, c):
            return NA + ORDER.index((kind, c)) + 1 + i * NFF

        def transposed_after(kind, c):
            if kind == "G" and c >= 1:
                return c - 1
            if kind == "D" and c == NCH - 2:
                return NCH - 1
            return None

        trunk_width = {}
        for l in range(LAYERS):
            for p in range(NIN):
                trunk_width[LAYER_PIECE0[l] + p] = KT * IN_PIECES[p][1]

        @block.sync
        def _(sp):
            for t in range(TT):
                sp.dma_start(x[:, t, :], a["x"][0, t * P:(t + 1) * P, :]).then_inc(x_in[t], 16)
            sp.dma_start(consts[:], a["table1"]).then_inc(early_in, 16)
            rows = [("attn_norm", V_ATTN), ("b_glu", V_BGLU), ("b_dw", V_BDW), ("conv_ln_g", V_LNG),
                    ("conv_ln_b", V_LNB), ("b_pw", V_BPW), ("q_norm", V_QN), ("kv_norm", V_KVN),
                    ("ffn_norm", V_FFN)]
            for (name, r0), r1 in zip(rows, [r for _, r in rows[1:]] + [V_END]):
                sp.dma_start(vec_rows[r0:r1, :], a[name].rearrange("l (k p) -> (l k) p", p=P)).then_inc(early_in, 16)

            def load(n, src, view):
                if n >= RAW_A:
                    sp.wait_ge(lo_ready, n - RAW_A + 1)
                t, s, _ = raw_slot(n)
                sp.dma_start(view(t), src).then_inc(s, 16)

            def load_small(l):
                sp.dma_start(w_pw[:], a["w_pw"][l].rearrange("(k p) n -> p k n", p=P)).then_inc(small_in, 16)
                sp.dma_start(w_uq[:], a["w_uq"][l].rearrange("(k p) n -> p k n", p=P)).then_inc(small_in, 16)
                sp.dma_start(w_ukv[:], a["w_ukv"][l]).then_inc(small_in, 16)

            for l in range(LAYERS):
                n0 = LAYER_PIECE0[l]
                for p, (c0, cn) in enumerate(IN_PIECES):
                    load(n0 + p, a["w_in"][l][:, c0:c0 + cn].rearrange("(k p) n -> p k n", p=P),
                         lambda t, p=p: in_piece_view(t, p))
                    if l == 0 and p == 2:
                        load_small(0)
                for i in range(NOUT):
                    k0 = OUT_ORDER[i] * 2 * P
                    load(n0 + NIN + i, a["w_out"][l][k0:k0 + 2 * P, :].rearrange("(k p) n -> p k n", p=P),
                         lambda t: ff_view(t, "D"))
                if l == 0:
                    sp.wait_ge(mid_mm, MID)
                    load_small(1)
                    for j, (kind, c) in enumerate(ORDER):
                        load(n0 + NIN + NOUT + j,
                             ff_src(a["w_gate_dense"][0], a["w_up_dense"][0], a["w_down_dense"][0], kind, c),
                             lambda t, kind=kind: ff_view(t, kind))

            def expert_loads(e, i, first):
                for j, (kind, c) in enumerate(ORDER):
                    if first and j < RAW_A:
                        sp.wait_ge(lo_ready, max(n for n in range(NA) if n % RAW_A == j) + 1)
                    elif first and j < RAW_M:
                        sp.wait_ge(x_upd, 12)
                    else:
                        sp.wait_ge(lo_ready, NA + j - RAW_M + 1 + i * NFF)
                    t, s, _ = expert_slot(i, j)
                    one = bass.ds(e, 1)
                    if kind == "D":
                        src = a["w_down_exp"][0][one, c * FC:(c + 1) * FC, :].rearrange("e (k p) n -> p (e k) n", p=P)
                    else:
                        w = a["w_gate_exp" if kind == "G" else "w_up_exp"][0]
                        src = w[one, :, c * FC:(c + 1) * FC].rearrange("e (k p) n -> p (e k) n", p=P)
                    sp.dma_start(ff_view(t, kind), src).then_inc(s, 16)

            expert_loads(0, 0, True)
            with sp.Fori(1, NE) as i:
                expert_loads(i, i, False)
            sp.wait_ge(items_ready, 1)
            n_items = sp.value_load(it_i[0:1, 0:1], min_val=NE, max_val=ITEMS_MAX)
            for j in range(3):
                e = sp.value_load(it_i[0:1, 1 + j:2 + j], min_val=0, max_val=NE - 1)
                with sp.If(n_items > NE + j):
                    expert_loads(e, NE + j, False)
            sp.wait_ge(out_sent, 16 * TT)

        @block.gpsimd
        def _(pool):
            pool.dma_start(tabs[:], a["table2"]).then_inc(params_in, 16)
            pool.dma_start(dw_rows[:], a["w_dw"].rearrange("l w c -> (l w) c")).then_inc(params_in, 16)
            for m, name in enumerate(["lambda_q1", "lambda_k1", "lambda_q2", "lambda_k2"]):
                pool.dma_start(lam_in[:, m].rearrange("p l d -> p (l d)"),
                               a[name].rearrange("(o l) d -> o (l d)", o=1).broadcast_to([P, LAYERS * HD])
                               ).then_inc(params_in, 16)
            pool.dma_start(subln[:].rearrange("p l d -> p (l d)"),
                           a["diff_subln"].rearrange("(o l) d -> o (l d)", o=1).broadcast_to([P, LAYERS * DV])
                           ).then_inc(params_in, 16)
            pool.dma_start(wr[:], a["w_router"][0].rearrange("(k p) e -> p k e", p=P)).then_inc(params_in, 16)
            nc.gpsimd.memset(ones[:], 1.0).then_inc(const_set, 1)
            nc.gpsimd.memset(half_neg[:], -0.5).then_inc(const_set, 1)
            nc.gpsimd.memset(eps_rms[:], RMS_EPS).then_inc(const_set, 1)
            nc.gpsimd.memset(eps_ln[:], LN_EPS).then_inc(const_set, 1)
            nc.gpsimd.memset(u_pad[:], 0.0).then_inc(const_set, 1)
            def norm_pow(j):
                for t in range(TT):
                    pool.wait_ge(ms_ready, TT * j + t + 1)
                    nc.gpsimd.tensor_tensor(rstd[:, t:t + 1], ms[:, t:t + 1], half_neg[:, 0:1], ALU.pow
                                            ).then_inc(rstd_ready, 1)

            for l in range(LAYERS):
                norm_pow(2 * l)
                if l > 0:
                    pool.wait_ge(x_upd, 8)
                    nc.gpsimd.memset(u_pad[:], 0.0).then_inc(const_set, 1)
                pool.wait_ge(od_step, OD_STEPS * l + 5)
                nc.gpsimd.tensor_tensor(o_rstd[:].rearrange("p h t -> p (h t)"), o_ms[:].rearrange("p h t -> p (h t)"),
                                        half_neg[:], ALU.pow).then_inc(od_pow, 1)
                if l == LAYERS - 1:
                    pool.wait_ge(x_upd, 12)
                    pool.dma_start(g_bc[:], a["ffn_norm"][l:l + 1, :].broadcast_to([P, D])).then_inc(gfin_in, 16)
                norm_pow(2 * l + 1)
            pool.wait_ge(gfin_in, 16)
            pool.wait_ge(hT_mm, 16)
            for t in range(TT):
                nc.gpsimd.tensor_tensor(xn[:, t, :], xn[:, t, :], g_bc[:], ALU.mult).then_inc(h_rows, 1)
            pool.wait_ge(h_rows, 2)
            pool.dma_start(g_bc[:], a["final_norm"].rearrange("(o d) -> o d", o=1).broadcast_to([P, D])
                           ).then_inc(gfin_in, 16)
            norm_pow(2 * LAYERS)

        def hi_of(n):
            return hi_ring[:, n % SPLIT, :]

        def lo_of(n):
            return lo_ring[:, n % SPLIT, :]

        @block.scalar
        def _(act):
            A = nc.scalar.activation

            def split(n):
                w = trunk_width.get(n, PIECE)
                t, s, v = raw_slot(n)
                act.wait_ge(s, v)
                if n >= SPLIT:
                    act.wait_ge(piece_used, n - SPLIT + 1)
                A(hi_of(n)[:, 0:w], t[:, 0:w], ACT.Copy).then_inc(hi_ready, 1)

            def split_expert(i, j):
                t, s, v = expert_slot(i, j)
                act.wait_ge(s, v)
                act.wait_ge(piece_used, NA + j - SPLIT + 1 + i * NFF)
                A(hi_of(NA + j), t, ACT.Copy).then_inc(hi_ready, 1)

            def norm_squares(j, upd=None):
                for t in range(TT):
                    if upd is None:
                        act.wait_ge(x_in[t], 16)
                    else:
                        act.wait_ge(x_upd, upd + 2 * t + 2)
                    A(xn[:, t, :], x[:, t, :], ACT.Square, accum_out=ss[:, t:t + 1]).then_inc(sumsq, 1)

            def norm_evac(j, g0):
                for k in range(KT):
                    if k % 2 == 0:
                        act.wait_ge(hT_mm, 4 * j + k // 2 + 1)
                    A(hT_hi[:, k, :], bank[k // 2][:, (k % 2) * T:(k % 2 + 1) * T], ACT.Copy,
                      scale=vecs[:, g0 + k:g0 + k + 1]).then_inc(hThi_done, 1)

            nc.scalar.preload_act_table_set("natural_log_exp_and_others")
            act.wait_ge(const_set, 5)
            norm_squares(0)
            split(0)
            act.wait_ge(setup_t, 1)
            A(vecs[:], bank[4][:, 0:V_END], ACT.Copy).then_inc(setup_a, 1)
            act.wait_ge(setup_a, 1)

            for l in range(LAYERS):
                n0 = LAYER_PIECE0[l]
                if l > 0:
                    nc.scalar.preload_act_table_set("natural_log_exp_and_others")
                    norm_squares(2 * l, 4)
                    split(n0)
                split(n0 + 1)
                norm_evac(2 * l, V_ATTN + KT * l)
                split(n0 + 2)
                if l == 0:
                    act.wait_ge(setup_t, 2)
                    A(dw[:], bank[7][:, 0:2 * LAYERS * TAPS].rearrange("p (c w) -> p c w", c=2),
                      ACT.Copy).then_inc(setup_a, 1)
                    act.wait_ge(params_in, 16 * N_PARAMS)
                    A(wr_parts[:, :, 0, :], wr[:], ACT.Copy).then_inc(setup_a, 1)

                def mid(g):
                    act.wait_ge(mid_mm, MID * l + g + 1)

                def mid_inc(ins):
                    ins.then_inc(mid_act, 1)

                for p in range(NIN):
                    act.wait_ge(piece_used, in_done(l, p))
                    b = bank[4 + p % 4]
                    if p == 0:
                        A(glu_a[:, 0, :], b[:, 0:T], ACT.Identity,
                          bias=vecs[:, V_BGLU + 4 * l:V_BGLU + 4 * l + 1])
                        r = A(glu_a[:, 1, :], b[:, T:2 * T], ACT.Identity,
                              bias=vecs[:, V_BGLU + 4 * l + 1:V_BGLU + 4 * l + 2])
                    elif p == 1:
                        if l == 0:
                            act.wait_ge(setup_v, 1)
                        A(glu_e[:, 0, :], b[:, 0:T], ACT.Exp, scale=-1.0,
                          bias=neg_vecs[:, V_BGLU + 4 * l + 2:V_BGLU + 4 * l + 3])
                        r = A(glu_e[:, 1, :], b[:, T:2 * T], ACT.Exp, scale=-1.0,
                              bias=neg_vecs[:, V_BGLU + 4 * l + 3:V_BGLU + 4 * l + 4])
                    elif p == 2:
                        A(cq[:], b[:].rearrange("p (c t) -> p c t", c=2), ACT.Copy)
                        r = A(sq_q[:], b[:].rearrange("p (c t) -> p c t", c=2), ACT.Square)
                    elif p == 3:
                        A(ckv[:], b[:, 0:T], ACT.Copy)
                        A(sq_kv[:], b[:, 0:T], ACT.Square)
                        r = A(kr[:], b[0:QD, T:2 * T], ACT.Copy)
                    elif p < 7:
                        r = A(dqk[:, 2 * (p - 4):2 * (p - 4) + 2, :], b[:].rearrange("p (c t) -> p c t", c=2), ACT.Copy)
                    else:
                        r = A(dv[:, :, (p - 7) * 192:(p - 6) * 192],
                              b[:, 0:384].rearrange("p (t n) -> p t n", t=TT), ACT.Copy)
                    r.then_inc(proj_evac, 1)
                    split(n0 + 3 + p)
                    if l == 0 and p == 1:
                        act.wait_ge(setup_v, 3)
                        A(lam_exp[:], lam_dot[:], ACT.Exp).then_inc(setup_a, 1)
                    if p == 4:
                        mid(0)
                        A(rs[:, 0, :], bank[0][:, 0:T], ACT.Ln, scale=1.0 / QR, bias=eps_rms[:])
                        A(rs[:, 1, :], bank[0][:, T:2 * T], ACT.Ln, scale=1.0 / KR, bias=eps_rms[:]).then_inc(conv_act, 1)
                        act.wait_ge(conv_act, CA * l + 1)
                        mid_inc(A(rs[:], rs[:], ACT.Exp, scale=-0.5))
                    if p == 5:
                        for r3 in range(3):
                            mid(1 + r3)
                            mid_inc(A(q_m[:, 2 * r3:2 * r3 + 2, :],
                                      bank[1 + r3][0:QD, :].rearrange("p (h t) -> p h t", h=2), ACT.Copy))
                    if p == 6:
                        for t in range(TT):
                            mid(5 + t)
                            mid_inc(A(v_m[:, t, :], bank[1 + t][:, 0:HEADS * MV], ACT.Copy))
                    if p == 7:
                        for r3 in range(3):
                            mid(7 + r3)
                            mid_inc(A(k_m[0:NOPE, 2 * r3:2 * r3 + 2, :],
                                      bank[MID_BANK[7 + r3]][0:NOPE, :].rearrange("p (h t) -> p h t", h=2), ACT.Copy))
                act.wait_ge(mid_dve, DVE_MID_STEPS * l + 6)
                mid_inc(A(k_m[NOPE:QD, :, :], kr[NOPE:QD, :].unsqueeze(1).broadcast_to([ROPE, HEADS, T]), ACT.Copy))

                for k in range(UNITS + 4):
                    if 1 <= k <= UNITS:
                        u = k - 1
                        act.wait_ge(s_max, 2 * (UNITS * l + u + 1))
                        if UNITS * l + u >= 2:
                            act.wait_ge(pt_mm, UNITS * l + u - 1)
                        A(e_sb[:, u % 2, 0:P], s_sb[:, u % 2, 0:P], ACT.Exp, bias=neg_max[:, u, 0:1],
                          accum_out=row_sum[:, u, 0:1])
                        A(e_sb[:, u % 2, P:3 * P], s_sb[:, u % 2, P:3 * P], ACT.Exp, bias=neg_max[:, u, 1:2],
                          accum_out=row_sum[:, u, 1:2]).then_inc(exp_done, 1)
                    if 2 <= k < UNITS + 2:
                        u = k - 2
                        act.wait_ge(pt_mm, UNITS * l + u + 1)
                        if UNITS * l + u >= 2:
                            act.wait_ge(pv_mm, UNITS * l + u - 1)
                        A(pt_sb[:, u % 2, :], bank[3 + u % 2][:, 0:3 * P], ACT.Copy).then_inc(pt_ready, 1)
                    if k == 13:
                        act.wait_ge(conv_step, CS * l + CS_CENTRED)
                        A(glu_e[:], cv[:, 1], ACT.Square).then_inc(conv_act, 1)
                    if k == 15:
                        mid(14)
                        A(ln_rs[:], bank[7][:, 0:T], ACT.Ln, scale=1.0 / CONV, bias=eps_ln[:]).then_inc(conv_act, 1)
                        act.wait_ge(conv_act, CA * l + 3)
                        A(ln_rs[:], ln_rs[:], ACT.Exp, scale=-0.5).then_inc(conv_act, 1)
                    if k == 16:
                        act.wait_ge(conv_step, CS * l + CS_NORMED)
                        for c in range(2):
                            A(glu_e[:, c, :], cv[:, 0, c, :], ACT.Exp,
                              scale=neg_vecs[:, V_LNG + 2 * l + c:V_LNG + 2 * l + c + 1],
                              bias=neg_vecs[:, V_LNB + 2 * l + c:V_LNB + 2 * l + c + 1])
                            r = A(glu_a[:, c, :], cv[:, 0, c, :], ACT.Identity,
                                  scale=vecs[:, V_LNG + 2 * l + c:V_LNG + 2 * l + c + 1],
                                  bias=vecs[:, V_LNB + 2 * l + c:V_LNB + 2 * l + c + 1])
                        r.then_inc(conv_act, 1)
                    if k == UNITS + 1:
                        mid(15)
                        for c in range(2):
                            A(hT_hi[:, c, :], bank[7][:, c * T:(c + 1) * T], ACT.Identity,
                              bias=vecs[:, V_BPW + 2 * l + c:V_BPW + 2 * l + c + 1]).then_inc(cat_hi, 1)
                    if k == 17:
                        act.wait_ge(od_step, OD_STEPS * l + 3)
                        A(od_sq[:], od[:], ACT.Square).then_inc(od_act, 1)
                for m, r3 in enumerate((2, 1, 0)):
                    act.wait_ge(yT_mm, 3 * l + m + 1)
                    A(hT_hi[:, 2 + 2 * r3:4 + 2 * r3, :], bank[r3][:].rearrange("p (c t) -> p c t", c=2),
                      ACT.Copy).then_inc(cat_hi, 1)
                    if m == 0:
                        split(n0 + 12)
                norm_squares(2 * l + 1, 8 * l)
                if l == 0:
                    f0 = n0 + NIN + NOUT
                    split(f0)
                    norm_evac(1, V_FFN)
                    split(f0 + 1)
                    for j, (kind, c) in enumerate(ORDER):
                        if j + 2 < NFF:
                            split(f0 + j + 2)
                        if kind == "U":
                            act.wait_ge(piece_used, dense_done("U", c))
                            for f in range(2):
                                if c >= 2:
                                    act.wait_ge(prod_done, 2 * (c - 2) + f + 1)
                                A(d_sg[:, c % 2, f, :], bank[(c % 2) * 2 + f][:, 0:T], ACT.Silu).then_inc(sg_done, 1)
                            for f in range(2):
                                act.wait_ge(prod_done, 2 * c + f + 1)
                                if c >= 2:
                                    act.wait_ge(piece_used, dense_done("D", c - 2))
                                A(d_hi[:, c % 2, f, :], d_prod[:, c % 2, f, :], ACT.Copy).then_inc(act_hi, 1)
                else:
                    norm_evac(3, V_FFN + KT)

            split_expert(0, 0)
            act.wait_ge(logits_mm, 1)
            A(lg_t[:], bank[4][0:2 * NE, 0:T], ACT.Copy).then_inc(logits_out, 1)
            for t in range(TT):
                act.wait_ge(h_rows, t + 1)
                A(ht_hi[:, t, :], xn[:, t, :], ACT.Copy).then_inc(ht_split, 1)
            act.wait_ge(route_v, RV_GAP)
            A(e2[:], gap[:], ACT.Exp).then_inc(route_a, 1)
            split_expert(0, 1)

            def gather_evac(i):
                for h in range(4):
                    act.wait_ge(gather_mm, 4 * i + h + 1)
                    part, b = (sel_hi, bank[6 + h]) if h < 2 else (sel_lo, bank[h - 2])
                    h0 = 4 * (h % 2)
                    A(part[:, h0:h0 + 4, :], b[:].rearrange("p (k s) -> p k s", k=4), ACT.Copy).then_inc(gathered, 1)

            def item(i, more):
                for j, (kind, c) in enumerate(ORDER):
                    if j + 2 < NFF or more is True:
                        split_expert(i, j + 2)
                    else:
                        with act.If(more):
                            split_expert(i, j + 2)
                    if kind == "U":
                        act.wait_ge(piece_used, expert_done(i, "U", c))
                        act.wait_ge(prod_done, GU0 + c - 1 + i * NCH)
                        A(m_sg[:, c % 2, :], bank[c % 2][:, 0:FC], ACT.Silu).then_inc(sg_done, 1)
                    if kind == "G" and c == 2:
                        act.wait_ge(onehot_tmm, i + 1)
                        A(onehot_t[:], bank[6][:, 0:TT * P].rearrange("p (t s) -> p t s", t=TT),
                          ACT.Copy).then_inc(onehot_tdone, 1)
                    tc = transposed_after(kind, c)
                    if tc is not None:
                        act.wait_ge(act_t, tc + 1 + i * NCH)
                        if tc >= 2:
                            act.wait_ge(piece_used, expert_done(i, "D", tc - 2))
                        A(m_hi[:, tc % 2, :, :], bank[2 + tc % 2][:, 0:2 * P].rearrange("p (f s) -> p f s", f=2),
                          ACT.Copy).then_inc(act_hi, 1)
                gather_evac(i + 1)
                act.wait_ge(piece_used, expert_done(i, "D", NCH - 1))
                for h in range(2):
                    A(y_hi[:, h * 512:(h + 1) * 512], bank[4 + h][:], ACT.Copy).then_inc(yhi_done, 1)

            gather_evac(0)
            item(0, True)
            act.wait_ge(items_ready, 1)
            n_items = act.value_load(it_i[0:1, 0:1], min_val=NE, max_val=ITEMS_MAX)
            with act.Fori(1, n_items) as i:
                item(i, i < n_items - 1)
            act.wait_ge(x_upd, XU0 + n_items * 4)
            norm_squares(4)
            act.wait_ge(xn_ready, 5 * TT)
            act.dma_start(out.rearrange("b (t p) d -> p (b t) d", p=P)[:, 0, :], xn[:, 0, :]).then_inc(out_sent, 16)
            act.dma_start(out.rearrange("b (t p) d -> p (b t) d", p=P)[:, 1, :], xn[:, 1, :]).then_inc(out_sent, 16)

        @block.vector
        def _(dve):
            V = nc.vector

            def split(n):
                w = trunk_width.get(n, PIECE)
                dve.wait_ge(hi_ready, n + 1)
                V.tensor_tensor(lo_of(n)[:, 0:w], raw_slot(n)[0][:, 0:w], hi_of(n)[:, 0:w].bitcast(F32),
                                ALU.subtract).then_inc(lo_ready, 1)

            def split_expert(i, j):
                dve.wait_ge(hi_ready, NA + j + 1 + i * NFF)
                V.tensor_tensor(lo_of(NA + j), expert_slot(i, j)[0], hi_of(NA + j).bitcast(F32),
                                ALU.subtract).then_inc(lo_ready, 1)

            def norm_ms(j):
                for t in range(TT):
                    dve.wait_ge(sumsq, TT * j + t + 1)
                    V.tensor_scalar(ms[:, t:t + 1], ss[:, t:t + 1], 1.0 / D, RMS_EPS, ALU.mult, ALU.add
                                    ).then_inc(ms_ready, 1)

            def norm_rows(j):
                for t in range(TT):
                    dve.wait_ge(rstd_ready, TT * j + t + 1)
                    V.tensor_scalar(xn[:, t, :], x[:, t, :], rstd[:, t:t + 1], None, ALU.mult).then_inc(xn_ready, 1)

            def norm_evac(j, g0):
                for k in range(KT):
                    dve.wait_ge(hThi_done, KT * j + 2 * (k // 2) + 2)
                    V.scalar_tensor_tensor(hT_lo[:, k, :], bank[k // 2][:, (k % 2) * T:(k % 2 + 1) * T],
                                           vecs[:, g0 + k:g0 + k + 1], hT_hi[:, k, :].bitcast(F32),
                                           ALU.mult, ALU.subtract).then_inc(hTlo_done, 1)

            def add_to_x(done, a, banks):
                for q in range(4):
                    t, n = q // 2, q % 2
                    if q < 3:
                        dve.wait_ge(acc_part, 3 * a + q + 1)
                    else:
                        dve.wait_ge(piece_used, done)
                    V.tensor_tensor(x[:, t, n * 512:(n + 1) * 512], x[:, t, n * 512:(n + 1) * 512], banks[q][:],
                                    ALU.add).then_inc(x_upd, 1)

            norm_ms(0)
            norm_rows(0)
            split(0)
            dve.wait_ge(setup_a, 1)
            V.tensor_scalar(neg_vecs[:], vecs[:], -1.0, None, ALU.mult).then_inc(setup_v, 1)

            for l in range(LAYERS):
                n0 = LAYER_PIECE0[l]
                lam_init = 0.8 - 0.6 * math.exp(-0.3 * l)
                if l > 0:
                    norm_ms(2 * l)
                    norm_rows(2 * l)
                    split(n0)
                split(n0 + 1)
                norm_evac(2 * l, V_ATTN + KT * l)
                split(n0 + 2)

                def setup():
                    dve.wait_ge(params_in, 16 * N_PARAMS)
                    V.tensor_tensor(lam_prod[:], lam_in[:, 0:4:2], lam_in[:, 1:4:2], ALU.mult).then_inc(setup_v, 1)
                    dve.wait_ge(setup_v, 2)
                    V.tensor_reduce(lam_dot[:], lam_prod[:], AX.X, ALU.add).then_inc(setup_v, 1)
                    for h in range(HEADS):
                        slope = 2.0 ** (-8.0 * (h + 1) / HEADS)
                        V.scalar_tensor_tensor(bias[:, h, :], dist, -slope, mask, ALU.mult, ALU.add).then_inc(setup_v, 1)
                    dve.wait_ge(setup_a, 3)
                    V.tensor_tensor(wr_parts[:, :, 1, :], wr[:], wr_parts[:, :, 0, :].bitcast(F32), ALU.subtract).then_inc(setup_v, 1)
                    for m in range(LAYERS):
                        li = 0.8 - 0.6 * math.exp(-0.3 * m)
                        V.tensor_scalar(subln[:, m], subln[:, m], 1.0 - li, None, ALU.mult).then_inc(setup_v, 1)

                def setup_lambda():
                    dve.wait_ge(setup_a, 4)
                    V.tensor_tensor(neg_lam[:], lam_exp[:, 1], lam_exp[:, 0], ALU.subtract).then_inc(setup_v, 1)
                    dve.wait_ge(setup_v, SETUP_V - LAYERS)
                    for m in range(LAYERS):
                        li = 0.8 - 0.6 * math.exp(-0.3 * m)
                        V.tensor_scalar(neg_lam[:, m:m + 1], neg_lam[:, m:m + 1], -li, None, ALU.add).then_inc(setup_v, 1)

                cs = [CS * l]
                ms_ = [DVE_MID_STEPS * l]

                def conv(ins):
                    cs[0] += 1
                    ins.then_inc(conv_step, 1)

                def mids(ins):
                    ms_[0] += 1
                    ins.then_inc(mid_dve, 1)

                def taps(lo, hi):
                    for w in range(lo, hi):
                        for c in range(2):
                            win = u_pad[:, c, w:w + T]
                            wc = dw[:, c, TAPS * l + w:TAPS * l + w + 1]
                            b = V_BDW + 2 * l + c
                            if w == 0:
                                conv(V.tensor_scalar(cv[:, 0, c, :], win, wc, vecs[:, b:b + 1], ALU.mult, ALU.add))
                            else:
                                dve.wait_ge(conv_step, cs[0] - 1)
                                conv(V.scalar_tensor_tensor(cv[:, w % 2, c, :], win, wc, cv[:, (w + 1) % 2, c, :],
                                                            ALU.mult, ALU.add))

                def glu():
                    dve.wait_ge(proj_evac, NIN * l + 2)
                    conv(V.tensor_scalar(glu_e[:], glu_e[:], 1.0, None, ALU.add))
                    dve.wait_ge(conv_step, cs[0])
                    conv(V.reciprocal(glu_e[:], glu_e[:]))
                    dve.wait_ge(conv_step, cs[0])
                    dve.wait_ge(const_set, 5 + l)
                    for c in range(2):
                        conv(V.tensor_tensor(u_pad[:, c, TAPS - 1:], glu_a[:, c, :], glu_e[:, c, :], ALU.mult))
                    dve.wait_ge(conv_step, cs[0])

                def latents():
                    dve.wait_ge(mid_act, ACT_MID_STEPS * l + 1)
                    for c in range(2):
                        mids(V.scalar_tensor_tensor(cq[:, c, :], cq[:, c, :],
                                                    vecs[:, V_QN + 2 * l + c:V_QN + 2 * l + c + 1], rs[:, 0, :],
                                                    ALU.mult, ALU.mult))
                    mids(V.scalar_tensor_tensor(ckv[:], ckv[:], vecs[:, V_KVN + l:V_KVN + l + 1], rs[:, 1, :],
                                                ALU.mult, ALU.mult))

                for p in range(NIN):
                    dve_split = n0 + 3 + p
                    split(dve_split)
                    if l == 0 and p == 0:
                        setup()
                    if l == 0 and p == 4:
                        setup_lambda()
                    if p == 1:
                        glu()
                    if p == 4:
                        latents()
                    if p == 5:
                        dve.wait_ge(mid_mm, MID * l + 5)
                        mids(V.tensor_tensor(kr[:], kr[:], cos, ALU.mult))
                        mids(V.tensor_tensor(rot[:, 0, :], bank[0][0:QD, 0:T], sin, ALU.mult))
                        dve.wait_ge(mid_dve, ms_[0])
                        mids(V.tensor_tensor(kr[:], kr[:], rot[:, 0, :], ALU.add))
                    if p >= 6:
                        taps(3 * (p - 6), 3 * (p - 5))

                def rope_q():
                    for r3 in range(3):
                        pair = q_m[:, 2 * r3:2 * r3 + 2, :]
                        wide = [QD, 2, T]
                        dve.wait_ge(mid_mm, MID * l + 11 + r3)
                        dve.wait_ge(mid_dve, ms_[0])
                        mids(V.tensor_tensor(pair, pair, cos.unsqueeze(1).broadcast_to(wide), ALU.mult))
                        mids(V.tensor_tensor(rot[:], bank[MID_BANK[10 + r3]][0:QD, :].rearrange("p (h t) -> p h t", h=2),
                                             sin.unsqueeze(1).broadcast_to(wide), ALU.mult))
                        dve.wait_ge(mid_dve, ms_[0])
                        mids(V.tensor_tensor(pair, pair, rot[:], ALU.add))

                rope_q()

                cr = [CR * l]
                ods = [OD_STEPS * l]

                def coefs(ins):
                    cr[0] += 1
                    ins.then_inc(coef_ready, 1)

                def odst(ins):
                    ods[0] += 1
                    ins.then_inc(od_step, 1)

                def normalise(g):
                    u0, un = 4 * g, min(4, UNITS - 4 * g)
                    last = u0 + un - 1
                    dve.wait_ge(exp_done, UNITS * l + last + 1)
                    coefs(V.reciprocal(coef[:, u0:u0 + un], row_sum[:, u0:u0 + un]))
                    dve.wait_ge(coef_ready, cr[0])
                    if g < 3:
                        odd = coef[:, u0 + 1:u0 + 4:2]
                        coefs(V.tensor_scalar(odd, odd, neg_lam[:, l:l + 1], None, ALU.mult))
                        dve.wait_ge(coef_ready, cr[0])
                    dve.wait_ge(pv_mm, UNITS * l + last + 1)
                    src = bank[5 + g % 2][:, 0:P * un].rearrange("p (u t d) -> p u t d", u=un, t=2)
                    cf = coef[:, u0:u0 + un].unsqueeze(3).broadcast_to([P, un, 2, DV])
                    if g < 3:
                        if g > 0:
                            dve.wait_ge(od_step, ods[0])
                        V.tensor_tensor(o_w[:], src, cf, ALU.mult).then_inc(o_read, 1)
                        dve.wait_ge(o_read, 5 * l + g + 1)
                        odst(V.tensor_tensor(od[:, 2 * g:2 * g + 2], o_w[:, 0:4:2], o_w[:, 1:4:2], ALU.add))
                    else:
                        h0 = u0 - 2 * HEADS
                        dst = xn[:, :, h0 * MV:(h0 + un) * MV].rearrange("p t (u d) -> p u t d", u=un)
                        V.tensor_tensor(dst, src, cf, ALU.mult).then_inc(o_read, 1)

                for k in range(UNITS + 5):
                    if k < UNITS:
                        u = k
                        dve.wait_ge(s_mm, UNITS * l + u + 1)
                        if UNITS * l + u >= 2:
                            dve.wait_ge(exp_done, UNITS * l + u - 1)
                        if u < 2 * HEADS:
                            sc, bi = HD ** -0.5, bias[:, u // 2, :]
                        else:
                            sc, bi = QD ** -0.5, mask
                        if l == 0 and u == 0:
                            dve.wait_ge(setup_v, SETUP_V)
                        V.scalar_tensor_tensor(s_sb[:, u % 2, :], bank[u % 3][:, 0:3 * P], sc, bi,
                                               ALU.mult, ALU.add).then_inc(s_biased, 1)
                        dve.wait_ge(s_biased, UNITS * l + u + 1)
                        V.tensor_reduce(neg_max[:, u, 0:1], s_sb[:, u % 2, 0:P], AX.X, ALU.max,
                                        negate=True).then_inc(s_max, 1)
                        V.tensor_reduce(neg_max[:, u, 1:2], s_sb[:, u % 2, P:3 * P], AX.X, ALU.max,
                                        negate=True).then_inc(s_max, 1)
                    if k >= 8 and k % 4 == 0 and (k - 8) // 4 < 4:
                        normalise((k - 8) // 4)
                    if k == UNITS + 3:
                        normalise(4)
                    if k <= 10:
                        taps(9 + 2 * k, 11 + 2 * k)
                    if k == 12:
                        dve.wait_ge(mid_mm, MID * l + 14)
                        mean = bank[7][:, 0:T].unsqueeze(1).broadcast_to([P, 2, T])
                        conv(V.scalar_tensor_tensor(cv[:, 1], mean, -1.0 / CONV, cv[:, 0], ALU.mult, ALU.add))
                    if k == 15:
                        dve.wait_ge(conv_act, CA * l + 4)
                        conv(V.tensor_tensor(cv[:, 0], cv[:, 1], ln_rs[:].unsqueeze(1).broadcast_to([P, 2, T]), ALU.mult))
                    if k == 17:
                        dve.wait_ge(conv_act, CA * l + 5)
                        conv(V.tensor_scalar(glu_e[:], glu_e[:], 1.0, None, ALU.add))
                        dve.wait_ge(conv_step, cs[0])
                        conv(V.reciprocal(glu_e[:], glu_e[:]))
                        dve.wait_ge(conv_step, cs[0])
                        conv(V.tensor_tensor(glu_a[:], glu_a[:], glu_e[:], ALU.mult))
                    if k == UNITS + 2:
                        for c in range(2):
                            dve.wait_ge(cat_hi, 5 * l + 2)
                            V.scalar_tensor_tensor(hT_lo[:, c, :], bank[7][:, c * T:(c + 1) * T],
                                                   vecs[:, V_BPW + 2 * l + c:V_BPW + 2 * l + c + 1],
                                                   hT_hi[:, c, :].bitcast(F32), ALU.add, ALU.subtract).then_inc(cat_lo, 1)
                    if k == 18:
                        dve.wait_ge(od_act, l + 1)
                        odst(V.tensor_reduce(o_ss[:], od_sq[:], AX.X, ALU.add))
                        dve.wait_ge(od_step, ods[0])
                        odst(V.tensor_scalar(o_ms[:], o_ss[:], 1.0 / DV, LN_EPS, ALU.mult, ALU.add))
                    if k == 19:
                        dve.wait_ge(od_pow, l + 1)
                        odst(V.tensor_tensor(od_sq[:], od[:], o_rstd[:].unsqueeze(3).broadcast_to([P, HEADS, 2, DV]),
                                             ALU.mult))
                        dve.wait_ge(od_step, ods[0])
                        dst = xn[:, :, HEADS * MV:2 * HEADS * MV].rearrange("p t (h d) -> p h t d", h=HEADS)
                        gain = subln[:, l].unsqueeze(1).unsqueeze(1).broadcast_to([P, HEADS, 2, DV])
                        odst(V.tensor_tensor(dst, od_sq[:], gain, ALU.mult))
                for m, r3 in enumerate((2, 1, 0)):
                    if m == 1:
                        split(n0 + 12)
                    dve.wait_ge(cat_hi, 5 * l + 3 + m)
                    V.tensor_tensor(hT_lo[:, 2 + 2 * r3:4 + 2 * r3, :], bank[r3][:].rearrange("p (c t) -> p c t", c=2),
                                    hT_hi[:, 2 + 2 * r3:4 + 2 * r3, :].bitcast(F32), ALU.subtract).then_inc(cat_lo, 1)
                add_to_x(out_done(l), 2 * l, bank[3:7])
                norm_ms(2 * l + 1)
                norm_rows(2 * l + 1)
                if l == 0:
                    f0 = n0 + NIN + NOUT
                    split(f0)
                    norm_evac(1, V_FFN)
                    split(f0 + 1)
                    for j, (kind, c) in enumerate(ORDER):
                        if j + 2 < NFF:
                            split(f0 + j + 2)
                        if kind == "U":
                            for f in range(2):
                                dve.wait_ge(sg_done, 2 * c + f + 1)
                                if c >= 2:
                                    dve.wait_ge(act_lo, 2 * (c - 2) + f + 1)
                                V.tensor_tensor(d_prod[:, c % 2, f, :], bank[(c % 2) * 2 + f][:, T:2 * T],
                                                d_sg[:, c % 2, f, :], ALU.mult).then_inc(prod_done, 1)
                            for f in range(2):
                                dve.wait_ge(act_hi, 2 * c + f + 1)
                                V.tensor_tensor(d_lo[:, c % 2, f, :], d_prod[:, c % 2, f, :],
                                                d_hi[:, c % 2, f, :].bitcast(F32), ALU.subtract).then_inc(act_lo, 1)
                    add_to_x(dense_done("D", NCH - 1), 1, bank[4:8])
                else:
                    norm_evac(3, V_FFN + KT)

            def split_rows(t):
                dve.wait_ge(ht_split, t + 1)
                V.tensor_tensor(ht_lo[:, t, :], xn[:, t, :], ht_hi[:, t, :].bitcast(F32), ALU.subtract
                                ).then_inc(ht_lo_done, 1)

            split_expert(0, 0)
            rv = [0]

            def step(ins, wait=True):
                rv[0] += 1
                ins.then_inc(route_v, 1)
                if wait:
                    dve.wait_ge(route_v, rv[0])

            dve.wait_ge(route_mm, 1)
            parts = bank[4][:, T:T + TT * 2 * NE].rearrange("p (t m e) -> p t m e", t=TT, m=2)
            step(V.tensor_copy(lg[:], parts[:, :, 1]))
            step(V.tensor_tensor(lg[:], lg[:], parts[:, :, 0], ALU.add))
            for t in range(TT):
                step(V.max(m8[:, t, :], lg[:, t, :]), wait=t == TT - 1)
            step(V.tensor_tensor(gap[:], m8[:, :, 1], m8[:, :, 0], ALU.subtract), wait=False)
            assert rv[0] == RV_GAP
            for t in range(TT):
                step(V.max_index(idx[:, t, :], m8[:, t, :], lg[:, t, :]), wait=t == TT - 1)
            step(V.tensor_copy(idf[:], idx[:]))
            for t in range(TT):
                for m in range(2):
                    step(V.tensor_scalar(oh[:, m, t, :], iota[:, 0:NE], idf[:, t, m:m + 1], None, ALU.is_equal),
                         wait=False)
            dve.wait_ge(route_v, rv[0])
            step(V.tensor_tensor(chosen[:], oh[:, 0], oh[:, 1], ALU.add))
            assert rv[0] == RV_CHOSEN
            step(V.tensor_scalar(less1[:], chosen[:], -1.0, None, ALU.add), wait=False)
            step(V.memset(pos_item[:], -1.0), wait=False)
            step(V.memset(g_item[:], 0.0))
            dve.wait_ge(route_mm, 2)
            step(V.tensor_tensor(pos[:], bank[5][:, 0:TT * NE].rearrange("p (t e) -> p t e", t=TT), chosen[:],
                                 ALU.mult))
            step(V.tensor_tensor(pos_item[:, :, 0:NE], pos[:], less1[:], ALU.add))

            def make_onehot(i):
                V.tensor_copy(p_col[:], pos_item[:, :, bass.ds(i, 1)].rearrange("p t o -> p (t o)")
                              ).then_inc(onehot_done, 1)
                dve.wait_ge(onehot_done, 1 + i * 3)
                for t in range(TT):
                    V.tensor_scalar(onehot[:, t, :], iota, p_col[:, t:t + 1], None, ALU.is_equal
                                    ).then_inc(onehot_done, 1)

            make_onehot(0)
            for t in range(TT):
                split_rows(t)
            split_expert(0, 1)
            dve.wait_ge(route_a, 1)
            step(V.tensor_scalar(w_top[:, 2, :], e2[:], 1.0, None, ALU.add))
            step(V.reciprocal(w_top[:, 0, :], w_top[:, 2, :]))
            step(V.tensor_tensor(w_top[:, 1, :], e2[:], w_top[:, 0, :], ALU.mult))
            for t in range(TT):
                for m in range(2):
                    step(V.tensor_scalar(gw[:, m, t, :], oh[:, m, t, :], w_top[:, m, t:t + 1], None, ALU.mult),
                         wait=False)
            step(V.tensor_copy(cnt[:], bank[5][:, TT * NE:3 * NE]))
            step(V.tensor_tensor(g_item[:, :, 0:NE], gw[:, 0], gw[:, 1], ALU.add), wait=False)
            step(V.tensor_scalar(over[:], cnt[:], float(P), None, ALU.is_gt))
            step(V.tensor_tensor_scan(incl[:], ones[:, 0:NE], over[:], 0.0, ALU.mult, ALU.add))
            step(V.tensor_scalar(pos_hi[:], pos_item[:, :, 0:NE], -float(P), None, ALU.add), wait=False)
            step(V.tensor_tensor(rank[:], incl[:], over[:], ALU.subtract))
            for j in range(3):
                step(V.scalar_tensor_tensor(sel[:, j, :], rank[:], float(j), over[:], ALU.is_equal, ALU.mult),
                     wait=False)
            step(V.tensor_scalar(it_f[:, 0:1], incl[:, NE - 1:NE], float(NE), None, ALU.add))
            m = 0
            for j in range(3):
                for t in range(TT):
                    for src, dst in ((pos_hi, pos_item), (g_item, g_item)):
                        step(V.tensor_tensor_reduce(junk[:, m, :], sel[:, j, :], src[:, t, 0:NE], 1.0, 0.0, ALU.mult,
                                                    ALU.add, dst[:, t, NE + j:NE + j + 1]), wait=False)
                        m += 1
                step(V.tensor_tensor_reduce(junk[:, m, :], sel[:, j, :], iota[:, 0:NE], 1.0, 0.0, ALU.mult, ALU.add,
                                            it_f[:, 1 + j:2 + j]), wait=False)
                m += 1
            dve.wait_ge(route_v, rv[0])
            V.tensor_copy(it_i[:], it_f[:]).then_inc(items_ready, 1)

            def scatter_add(items, q):
                t, n = q // 2, q % 2
                dve.wait_ge(scat_mm[q], items)
                dve.wait_ge(x_upd, XU0 - 7 + q + 4 * items)
                xs = x[:, t, n * 512:(n + 1) * 512]
                V.scalar_tensor_tensor(xs, bank[6 + q % 2][:], g_col[:, t:t + 1], xs, ALU.mult, ALU.add
                                       ).then_inc(x_upd, 1)

            def item(i, more, first=False):
                for j, (kind, c) in enumerate(ORDER):
                    if j + 2 < NFF or more is True:
                        split_expert(i, j + 2)
                    else:
                        with dve.If(more):
                            split_expert(i, j + 2)
                    if kind == "U":
                        dve.wait_ge(sg_done, GU0 + c + 1 + i * NCH)
                        if c >= 2:
                            dve.wait_ge(act_t, c - 1 + i * NCH)
                        V.tensor_tensor(m_prod[:, c % 2, :], bank[c % 2][:, FC:2 * FC], m_sg[:, c % 2, :],
                                        ALU.mult).then_inc(prod_done, 1)
                    if not first and c <= 1 and kind == ("U", "G")[c]:
                        scatter_add(i, 2 * c)
                        scatter_add(i, 2 * c + 1)
                    tc = transposed_after(kind, c)
                    if tc is not None:
                        dve.wait_ge(act_hi, GU0 + tc + 1 + i * NCH)
                        V.tensor_tensor(m_lo[:, tc % 2, :, :], bank[2 + tc % 2][:, 0:2 * P].rearrange("p (f s) -> p f s", f=2),
                                        m_hi[:, tc % 2, :, :].bitcast(F32), ALU.subtract).then_inc(act_lo, 1)
                    if kind == "U" and c == 5:
                        dve.wait_ge(onehot_tmm, i + 1)
                        dve.wait_ge(x_upd, XU0 + 4 * i)
                        V.tensor_copy(g_col[:], g_item[:, :, bass.ds(i, 1)].rearrange("p t o -> p (t o)")
                                      ).then_inc(route_v, 1)
                        dve.wait_ge(gather_mm, 4 + 4 * i)
                        dve.wait_ge(onehot_done, 3 + 3 * i)
                        make_onehot(i + 1)
                        dve.wait_ge(route_v, rv[0] + 1 + i)
                for h in range(2):
                    dve.wait_ge(yhi_done, 2 * i + 1 + h)
                    V.tensor_tensor(y_lo[:, h * 512:(h + 1) * 512], bank[4 + h][:],
                                    y_hi[:, h * 512:(h + 1) * 512].bitcast(F32), ALU.subtract).then_inc(ylo_done[h], 1)

            item(0, True, first=True)
            n_items = dve.value_load(it_i[0:1, 0:1], min_val=NE, max_val=ITEMS_MAX)
            with dve.Fori(1, n_items) as i:
                item(i, i < n_items - 1)
            for q in range(4):
                scatter_add(n_items, q)
            norm_ms(4)
            dve.wait_ge(gfin_in, 32)
            for t in range(TT):
                dve.wait_ge(rstd_ready, 4 * TT + t + 1)
                V.scalar_tensor_tensor(xn[:, t, :], x[:, t, :], rstd[:, t:t + 1], g_bc[:], ALU.mult, ALU.mult
                                       ).then_inc(xn_ready, 1)

        @block.tensor
        def _(pe):
            M = nc.tensor.matmul

            def mm3(o, lh, ll, rh, rl, start, stop):
                M(o, lh, rh, start=start, stop=False)
                M(o, lh, rl, start=False, stop=False)
                return M(o, ll, rh, start=False, stop=stop)

            def norm_transposes(j):
                for t in range(TT):
                    pe.wait_ge(xn_ready, TT * j + t + 1)
                    for b in range(4):
                        for kk in range(2):
                            k = 2 * b + kk
                            r = nc.tensor.transpose(bank[b][:, kk * T + t * P:kk * T + (t + 1) * P],
                                                    xn[:, t, k * P:(k + 1) * P], ident)
                        if t == TT - 1:
                            r.then_inc(hT_mm, 1)

            pe.wait_ge(early_in, 16 * N_EARLY)
            pe.wait_ge(const_set, 5)
            for l in range(LAYERS):
                n0 = LAYER_PIECE0[l]
                norm_transposes(2 * l)
                if l == 0:
                    nc.tensor.transpose(bank[4][:, 0:V_END], vec_rows[:], ident[0:V_END, 0:V_END]).then_inc(setup_t, 1)
                    pe.wait_ge(params_in, 16 * N_PARAMS)
                    nt = LAYERS * TAPS
                    for c in range(2):
                        r = nc.tensor.transpose(bank[7][:, c * nt:(c + 1) * nt], dw_rows[:, c * P:(c + 1) * P],
                                                ident[0:nt, 0:nt])
                    r.then_inc(setup_t, 1)

                def mid_start(g):
                    gp = g - 4
                    if gp in MID_ACT:
                        pe.wait_ge(mid_act, ACT_MID_STEPS * l + MID_ACT[gp])
                    else:
                        pe.wait_ge(mid_dve, DVE_MID_STEPS * l + MID_DVE[gp])

                def project(p):
                    n = n0 + p
                    pe.wait_ge(lo_ready, n + 1)
                    if p >= 4:
                        pe.wait_ge(proj_evac, NIN * l + p - 3)
                    elif l == 0 and p in (0, 3):
                        pe.wait_ge(setup_a, 1 if p == 0 else 2)
                    b = bank[4 + p % 4]
                    wh, wl = in_piece_view(hi_of(n), p), in_piece_view(lo_of(n), p)
                    if p < 7:
                        cols = [(0, P), (P, P)] if p != 3 else [(0, P), (KR - NOPE, QD)]
                        for m, (c0, cn) in enumerate(cols):
                            for k in range(KT):
                                if p == 0 and m == 0:
                                    pe.wait_ge(hTlo_done, KT * 2 * l + k + 1)
                                r = mm3(b[0:cn, m * T:(m + 1) * T], wh[:, k, c0:c0 + cn], wl[:, k, c0:c0 + cn],
                                        hT_hi[:, k, :], hT_lo[:, k, :], k == 0, k == KT - 1)
                    else:
                        for t in range(TT):
                            for k in range(KT):
                                tok = slice(t * P, (t + 1) * P)
                                r = mm3(b[:, t * 192:(t + 1) * 192], hT_hi[:, k, tok], hT_lo[:, k, tok],
                                        wh[:, k, :], wl[:, k, :], k == 0, k == KT - 1)
                    r.then_inc(piece_used, 1)

                for p in range(NIN):
                    project(p)
                    if p == 4:
                        pe.wait_ge(proj_evac, NIN * l + 4)
                        for c in range(2):
                            M(bank[0][:, 0:T], ones[:], sq_q[:, c, :], start=c == 0, stop=c == 1)
                        M(bank[0][:, T:2 * T], ones[:], sq_kv[:], start=True, stop=True).then_inc(mid_mm, 1)
                    if p == 5:
                        pe.wait_ge(small_in, 48 * (l + 1))
                        pe.wait_ge(mid_dve, DVE_MID_STEPS * l + 3)
                        for r3 in range(3):
                            for hh in range(2):
                                h = 2 * r3 + hh
                                for c in range(2):
                                    r = M(bank[1 + r3][0:QD, hh * T:(hh + 1) * T], w_uq[:, c, h * QD:(h + 1) * QD],
                                          cq[:, c, :], start=c == 0, stop=c == 1)
                            r.then_inc(mid_mm, 1)
                        mid_start(4)
                        M(bank[0][0:QD, 0:T], rotate, kr[:], start=True, stop=True).then_inc(mid_mm, 1)
                    if p == 6:
                        for t in range(TT):
                            mid_start(5 + t)
                            wv = w_ukv[:].rearrange("p (h n) -> p h n", h=HEADS)[:, :, NOPE:]
                            M(bank[1 + t][:, 0:HEADS * MV], ckv[:, t * P:(t + 1) * P], wv, start=True, stop=True
                              ).then_inc(mid_mm, 1)
                    if p == 7:
                        for r3 in range(3):
                            mid_start(7 + r3)
                            for hh in range(2):
                                h = 2 * r3 + hh
                                r = M(bank[MID_BANK[7 + r3]][0:NOPE, hh * T:(hh + 1) * T],
                                      w_ukv[:, h * KVD:h * KVD + NOPE], ckv[:], start=True, stop=True)
                            r.then_inc(mid_mm, 1)
                for r3 in range(3):
                    mid_start(10 + r3)
                    M(bank[MID_BANK[10 + r3]][0:QD, :], rotate, q_m[:, 2 * r3:2 * r3 + 2, :].rearrange("p h t -> p (h t)"),
                      start=True, stop=True).then_inc(mid_mm, 1)

                def scores(u):
                    if u == 0:
                        pe.wait_ge(proj_evac, NIN * (l + 1))
                        pe.wait_ge(mid_dve, DVE_MID_STEPS * (l + 1))
                        pe.wait_ge(mid_act, ACT_MID_STEPS * (l + 1))
                    if u >= 3:
                        pe.wait_ge(s_biased, UNITS * l + u - 2)
                    if u < 2 * HEADS:
                        h, half = u // 2, u % 2
                        r0 = (h % 2) * DV + half * HD
                        q, kk = dqk[r0:r0 + HD, h // 2, :], dqk[r0:r0 + HD, 3 + h // 2, :]
                    else:
                        q, kk = q_m[:, u - 2 * HEADS, :], k_m[:, u - 2 * HEADS, :]
                    M(bank[u % 3][:, 0:P], q[:, 0:P], kk[:, 0:P], start=True, stop=True)
                    M(bank[u % 3][:, P:3 * P], q[:, P:2 * P], kk[:, :], start=True, stop=True).then_inc(s_mm, 1)

                def transposes(u):
                    pe.wait_ge(exp_done, UNITS * l + u + 1)
                    if u >= 2:
                        pe.wait_ge(pt_ready, UNITS * l + u - 1)
                    for b in range(3):
                        r = nc.tensor.transpose(bank[3 + u % 2][:, b * P:(b + 1) * P], e_sb[:, u % 2, b * P:(b + 1) * P],
                                                ident)
                    r.then_inc(pt_mm, 1)

                def values(u):
                    g = u // 4
                    pe.wait_ge(pt_ready, UNITS * l + u + 1)
                    if u % 4 == 0 and g >= 2:
                        pe.wait_ge(o_read, 5 * l + g - 1)
                    v = dv if u < 2 * HEADS else v_m
                    h = u // 2 if u < 2 * HEADS else u - 2 * HEADS
                    o = bank[5 + g % 2][:, (u % 4) * P:(u % 4 + 1) * P]
                    pt = pt_sb[:, u % 2, :]
                    M(o[:, 0:DV], pt[:, 0:P], v[:, 0, h * DV:(h + 1) * DV], start=True, stop=True)
                    M(o[:, DV:2 * DV], pt[:, P:2 * P], v[:, 0, h * DV:(h + 1) * DV], start=True, stop=False)
                    M(o[:, DV:2 * DV], pt[:, 2 * P:3 * P], v[:, 1, h * DV:(h + 1) * DV], start=False, stop=True
                      ).then_inc(pv_mm, 1)

                for k in range(UNITS + 3):
                    if k < UNITS:
                        scores(k)
                    if 2 <= k < UNITS + 2:
                        transposes(k - 2)
                    if k >= 3:
                        values(k - 3)
                    if k == 11:
                        pe.wait_ge(conv_step, CS * l + CS_TAPS)
                        for c in range(2):
                            r = M(bank[7][:, 0:T], ones[:], cv[:, 0, c, :], start=c == 0, stop=c == 1)
                        r.then_inc(mid_mm, 1)
                    if k == 14:
                        pe.wait_ge(conv_act, CA * l + 2)
                        for c in range(2):
                            r = M(bank[7][:, 0:T], ones[:], glu_e[:, c, :], start=c == 0, stop=c == 1)
                        r.then_inc(mid_mm, 1)
                    if k == 18:
                        pe.wait_ge(conv_step, CS * (l + 1))
                        for m in range(2):
                            for c in range(2):
                                r = M(bank[7][:, m * T:(m + 1) * T], w_pw[:, c, m * P:(m + 1) * P], glu_a[:, c, :],
                                      start=c == 0, stop=c == 1)
                        r.then_inc(mid_mm, 1)
                def y_transposes(r3):
                    for kk in range(2):
                        for t in range(TT):
                            c0 = (2 * r3 + kk) * P
                            r = nc.tensor.transpose(bank[r3][:, kk * T + t * P:kk * T + (t + 1) * P],
                                                    xn[:, t, c0:c0 + P], ident)
                    r.then_inc(yT_mm, 1)

                pe.wait_ge(od_step, OD_STEPS * (l + 1))
                y_transposes(2)
                for i in range(NOUT):
                    if i == 1:
                        pe.wait_ge(o_read, 5 * (l + 1))
                        y_transposes(1)
                        y_transposes(0)
                    n = n0 + NIN + i
                    pe.wait_ge(lo_ready, n + 1)
                    pe.wait_ge(cat_lo, 5 * l + (3, 3, 4, 5)[i])
                    wh, wl = ff_view(hi_of(n), "D"), ff_view(lo_of(n), "D")
                    last = i == NOUT - 1
                    order = [(kk, q) for q in range(4) for kk in range(2)] if last else \
                            [(kk, q) for kk in range(2) for q in range(4)]
                    for kk, q in order:
                        k, t, nn = 2 * OUT_ORDER[i] + kk, q // 2, q % 2
                        r = mm3(bank[3 + q][:], hT_hi[:, k, t * P:(t + 1) * P], hT_lo[:, k, t * P:(t + 1) * P],
                                wh[:, kk, nn * 512:(nn + 1) * 512], wl[:, kk, nn * 512:(nn + 1) * 512],
                                i == 0 and kk == 0, last and kk == 1)
                        if last and kk == 1 and q < 3:
                            r.then_inc(acc_part, 1)
                    r.then_inc(piece_used, 1)
                norm_transposes(2 * l + 1)
                if l == 0:
                    f0 = n0 + NIN + NOUT
                    for j, (kind, c) in enumerate(ORDER):
                        n = f0 + j
                        pe.wait_ge(lo_ready, n + 1)
                        wh, wl = ff_view(hi_of(n), kind), ff_view(lo_of(n), kind)
                        if kind == "D":
                            pe.wait_ge(act_lo, 2 * c + 2)
                            last = c == NCH - 1
                            order = [(f, q) for q in range(4) for f in range(2)] if last else \
                                    [(f, q) for f in range(2) for q in range(4)]
                            for f, q in order:
                                t, nn = q // 2, q % 2
                                tok = slice(t * P, (t + 1) * P)
                                r = mm3(bank[4 + q][:], d_hi[:, c % 2, f, tok], d_lo[:, c % 2, f, tok],
                                        wh[:, f, nn * 512:(nn + 1) * 512], wl[:, f, nn * 512:(nn + 1) * 512],
                                        c == 0 and f == 0, last and f == 1)
                                if last and f == 1 and q < 3:
                                    r.then_inc(acc_part, 1)
                            r.then_inc(piece_used, 1)
                        else:
                            if kind == "G" and c >= 2:
                                pe.wait_ge(prod_done, 2 * (c - 1))
                            for f in range(2):
                                o = bank[(c % 2) * 2 + f][:, 0:T] if kind == "G" else bank[(c % 2) * 2 + f][:, T:2 * T]
                                for k in range(KT):
                                    if j == 0 and f == 0:
                                        pe.wait_ge(hTlo_done, KT + max(k + 1, 2))
                                    r = mm3(o, wh[:, k, f * P:(f + 1) * P], wl[:, k, f * P:(f + 1) * P],
                                            hT_hi[:, k, :], hT_lo[:, k, :], k == 0, k == KT - 1)
                            r.then_inc(piece_used, 1)
            pe.wait_ge(setup_v, SETUP_V)
            for k in range(KT):
                pe.wait_ge(hTlo_done, 3 * KT + k + 1)
                w = wr_parts[:, k].rearrange("p m e -> p (m e)")
                M(bank[4][0:2 * NE, 0:T], w, hT_hi[:, k, :], start=k == 0, stop=False)
                r = M(bank[4][0:2 * NE, 0:T], w, hT_lo[:, k, :], start=False, stop=k == KT - 1)
            r.then_inc(logits_mm, 1)
            pe.wait_ge(logits_out, 1)
            for t in range(TT):
                r = nc.tensor.transpose(bank[4][:, T + t * 2 * NE:T + (t + 1) * 2 * NE], lg_t[:, t * P:(t + 1) * P],
                                        ident[0:2 * NE, 0:2 * NE])
            r.then_inc(route_mm, 1)
            pe.wait_ge(route_v, RV_CHOSEN)
            M(bank[5][:, 0:NE], upper, chosen[:, 0, :], start=True, stop=True)
            M(bank[5][:, NE:2 * NE], ones[:], chosen[:, 0, :], start=True, stop=False)
            M(bank[5][:, NE:2 * NE], upper, chosen[:, 1, :], start=False, stop=True)
            M(bank[5][:, 2 * NE:3 * NE], ones[:], chosen[:, 0, :], start=True, stop=False)
            M(bank[5][:, 2 * NE:3 * NE], ones[:], chosen[:, 1, :], start=False, stop=True).then_inc(route_mm, 1)

            def gather(i, first=False):
                pe.wait_ge(onehot_done, 3 + 3 * i)
                for src, b0, parts_done in ((ht_hi, 6, ht_split), (ht_lo, 0, ht_lo_done)):
                    if first:
                        pe.wait_ge(parts_done, TT)
                    for h in range(2):
                        for kk in range(4):
                            k = 4 * h + kk
                            for t in range(TT):
                                r = M(bank[b0 + h][:, kk * P:(kk + 1) * P], src[:, t, k * P:(k + 1) * P],
                                      onehot[:, t, :], start=t == 0, stop=t == TT - 1)
                        r.then_inc(gather_mm, 1)

            def scatter(items, q):
                t, n = q // 2, q % 2
                if q < 2:
                    pe.wait_ge(ylo_done[n], items)
                else:
                    pe.wait_ge(x_upd, XU0 + q - 5 + 4 * items)
                b = bank[6 + q % 2]
                M(b[:], onehot_t[:, t, :], y_hi[:, n * 512:(n + 1) * 512], start=True, stop=False)
                M(b[:], onehot_t[:, t, :], y_lo[:, n * 512:(n + 1) * 512], start=False, stop=True
                  ).then_inc(scat_mm[q], 1)

            def transpose_act(i, c):
                pe.wait_ge(prod_done, GU0 + c + 1 + i * NCH)
                pe.wait_ge(act_lo, GU0 + c - 1 + i * NCH)
                for f in range(2):
                    r = nc.tensor.transpose(bank[2 + c % 2][:, f * P:(f + 1) * P], m_prod[:, c % 2, f * P:(f + 1) * P],
                                            ident)
                r.then_inc(act_t, 1)

            def item(i, first=False):
                for j, (kind, c) in enumerate(ORDER):
                    pe.wait_ge(lo_ready, NA + j + 1 + i * NFF)
                    wh, wl = ff_view(hi_of(NA + j), kind), ff_view(lo_of(NA + j), kind)
                    if kind == "D":
                        if c == NCH - 1:
                            transpose_act(i, c)
                            pe.wait_ge(onehot_tdone, i + 1)
                            gather(i + 1)
                        pe.wait_ge(act_lo, GU0 + c + 1 + i * NCH)
                        for f in range(2):
                            for n in range(2):
                                r = mm3(bank[4 + n][:], m_hi[:, c % 2, f, :], m_lo[:, c % 2, f, :],
                                        wh[:, f, n * 512:(n + 1) * 512], wl[:, f, n * 512:(n + 1) * 512],
                                        c == 0 and f == 0, c == NCH - 1 and f == 1)
                    else:
                        if kind == "G" and c >= 2:
                            pe.wait_ge(prod_done, GU0 + c - 1 + i * NCH)
                        o = bank[c % 2][:, 0:FC] if kind == "G" else bank[c % 2][:, FC:2 * FC]
                        for k in range(KT):
                            if kind == "G" and c == 0 and k % 4 == 0:
                                pe.wait_ge(gathered, 3 + k // 4 + 4 * i)
                            r = mm3(o, sel_hi[:, k, :], sel_lo[:, k, :], wh[:, k, :], wl[:, k, :], k == 0, k == KT - 1)
                    r.then_inc(piece_used, 1)
                    if kind == "G" and c >= 1:
                        transpose_act(i, c - 1)
                    if not first and c <= 1 and kind == ("U", "G")[c]:
                        scatter(i, 2 * c)
                        scatter(i, 2 * c + 1)
                    if kind == "G" and c == 2:
                        pe.wait_ge(x_upd, XU0 + 4 * i)
                        for t in range(TT):
                            r = nc.tensor.transpose(bank[6][:, t * P:(t + 1) * P], onehot[:, t, :].bitcast(F32), ident)
                        r.then_inc(onehot_tmm, 1)

            gather(0, first=True)
            item(0, first=True)
            pe.wait_ge(items_ready, 1)
            n_items = pe.value_load(it_i[0:1, 0:1], min_val=NE, max_val=ITEMS_MAX)
            with pe.Fori(1, n_items) as i:
                item(i)
            for q in range(4):
                scatter(n_items, q)


_INS = ["x", "attn_norm", "w_in", "b_glu", "w_dw", "b_dw", "conv_ln_g", "conv_ln_b", "w_pw", "b_pw", "q_norm", "w_uq",
        "kv_norm", "w_ukv", "lambda_q1", "lambda_k1", "lambda_q2", "lambda_k2", "diff_subln", "w_out", "ffn_norm",
        "w_gate_dense", "w_up_dense", "w_down_dense", "w_router", "w_gate_exp", "w_up_exp", "w_down_exp", "final_norm"]


def kernel(**inputs):
    import concourse.bacc as bacc
    from concourse.bass_utils import run_bass_kernel_spmd as run

    nc = bacc.Bacc("TRN2", target_bir_lowering=False, num_devices=1)
    arrays = {name: np.ascontiguousarray(inputs[name]) for name in _INS}
    arrays["table1"], arrays["table2"] = tables()
    a = {name: nc.dram_tensor(f"in_{name}", v.shape, F32, kind="ExternalInput").ap() for name, v in arrays.items()}
    out = nc.dram_tensor("out", (1, T, D), F32, kind="ExternalOutput").ap()
    build(nc, a, out)
    r = run(nc, [{f"in_{name}": v for name, v in arrays.items()}], core_ids=[0])
    return r.results[0]["out"]
```

```python
import math
from contextlib import ExitStack

import numpy as np

import concourse.bass as bass
from concourse import mybir

ALU = mybir.AluOpType
ACT = mybir.ActivationFunctionType
AX = mybir.AxisListType
F32 = mybir.dt.float32
F32R = mybir.dt.float32r
I32 = mybir.dt.int32
U32 = mybir.dt.uint32

P = 128
D = 1024
T = 256
TT = T // P
KT = D // P
LAYERS = 2
CONV = 256
TAPS = 31
NOPE, ROPE, MV = 64, 32, 64
QR, KR = 256, 128
HEADS = 6
QD = NOPE + ROPE
KVD = NOPE + MV
HD, DV = 32, 64
FF = 2816
NE = 8
RMS_EPS, LN_EPS = 1e-6, 1e-5
MASKED = -1e30

C_CQ = 2 * CONV
C_CKV = C_CQ + QR
C_KR = C_CKV + KR
C_DQ = C_KR + ROPE
C_DV = C_DQ + 2 * HEADS * DV
IN_COLS = C_DV + HEADS * DV
IN_PIECES = [(0, 256), (256, 256), (C_CQ, 256), (C_CKV, KR + ROPE), (C_DQ, 256), (C_DQ + 256, 256),
             (C_DQ + 512, 256), (C_DV, 192), (C_DV + 192, 192)]
NIN = len(IN_PIECES)
NOUT = 4
FC = 256
NCH = FF // FC
NFF = 3 * NCH
PIECE = 2048
RAW_A, RAW_M, SPLIT = 4, 11, 3
NA = 2 * (NIN + NOUT) + NFF
ITEMS_MAX = NE + 3
LAYER_PIECE0 = [0, NIN + NOUT + NFF]


N_EARLY = 12
N_PARAMS = 6
MID = 16
N_CONST = 4

MID_BANK = [0, 1, 2, 3, 0, 1, 2, 3, 0, 1, 2, 3, 0, 7, 7, 7]
MID_ACT = {0: 1, 1: 2, 2: 3, 3: 4, 5: 5, 6: 6, 10: 8, 11: 9, 12: 10}
ACT_MID_STEPS = 10
ROPE_AT = {6: (0, 1), 7: (2,)}
KEYS_AT = {7: (0, 1, 2)}
DVE_MID_STEPS = 15
MID_DVE = {4: 5, 7: 8, 8: 11, 9: 14}

UNITS = 3 * HEADS
SLOTS = 2 * HEADS
S_BANK, T_BANK, O_BANK = (5, 6, 4), (3, 0), (1, 2)
OUT_BANK = (5, 6, 4, 3)
TAPS_AT = [0, 0, 8, 9, 8, 7, 5, 2, 1]
CA = 5
CS_U = 3
POOL_TAPS = 22
CS_TAPS = CS_U - 1 + TAPS + (TAPS - POOL_TAPS) + 1
CS_CENTRED = CS_TAPS + 1
CS_NORMED = CS_CENTRED + 1
CS = CS_NORMED + 3
RV_GAP, RV_CHOSEN = 5, 13
GU0 = 2 * NCH
XU0 = 12

CR = 3 * HEADS
SETUP_V = 5 + 2 * LAYERS + HEADS


def ff_order():
    order = [("G", 0), ("U", 0)]
    for c in range(1, NCH):
        order += [("G", c), ("U", c), ("D", c - 1)]
    return order + [("D", NCH - 1)]


ORDER = ff_order()

OUT_ORDER = [3, 2, 0, 1]
V_ATTN, V_BGLU, V_BDW, V_LNG, V_LNB, V_BPW, V_QN, V_KVN, V_FFN, V_SUB, V_END = 0, 16, 24, 28, 32, 36, 40, 44, 46, 62, 64

K_ID = 0
K_U = K_ID + P
K_IOTA = K_U + P
K_R = K_IOTA + P
K_BLK = K_R + QD
K_END1 = K_BLK + P
K_MASK = 0
K_DIST = K_MASK + 3 * P
K_COS = K_DIST + 3 * P
K_SIN = K_COS + T
K_END2 = K_SIN + T


def tables():
    one = np.zeros((P, K_END1), np.float32)
    one[:, K_ID:K_ID + P] = np.eye(P)
    one[:, K_U:K_U + P] = np.triu(np.ones((P, P)), 1)
    one[:, K_IOTA:K_IOTA + P] = np.arange(P)
    half = ROPE // 2
    for a in range(half):
        one[NOPE + half + a, K_R + NOPE + a] = -1.0
        one[NOPE + a, K_R + NOPE + half + a] = 1.0
    for h in range(2):
        one[h * DV:(h + 1) * DV, K_BLK + h * DV:K_BLK + (h + 1) * DV] = 1.0
    two = np.zeros((P, K_END2), np.float32)
    q = np.arange(P)[:, None]
    dist = np.concatenate([q - np.arange(P)[None], q + P - np.arange(T)[None]], 1)
    two[:, K_MASK:K_MASK + 3 * P] = np.where(dist < 0, MASKED, 0.0)
    two[:, K_DIST:K_DIST + 3 * P] = np.maximum(dist, 0)
    freq = np.float32(10000.0) ** (-np.arange(half, dtype=np.float32) / np.float32(half))
    ang = np.arange(T, dtype=np.float32)[None, :] * freq[:, None].astype(np.float32)
    two[:NOPE, K_COS:K_COS + T] = 1.0
    for r in range(2):
        lo = NOPE + r * half
        two[lo:lo + half, K_COS:K_COS + T] = np.cos(ang)
        two[lo:lo + half, K_SIN:K_SIN + T] = np.sin(ang)
    return one, two


def build(nc, a, out):
    with ExitStack() as ctx:
        region = [ctx]

        def sb(name, shape, dt=F32):
            return region[0].enter_context(nc.sbuf_tensor(name, shape, dt))

        def sem(name):
            return ctx.enter_context(nc.semaphore(name))

        bank = [ctx.enter_context(nc.psum_tensor(f"bank{i}", [P, 512], F32)) for i in range(8)]

        hi_ring = sb("hi_ring", [P, SPLIT, PIECE], F32R)
        lo_ring = sb("lo_ring", [P, SPLIT, PIECE], F32R)
        raw_a = sb("raw_a", [P, RAW_A, PIECE])
        x = sb("x", [P, TT, D])
        xn = sb("xn", [P, TT, D])
        hT_hi = sb("hT_hi", [P, KT, T], F32R)
        hT_lo = sb("hT_lo", [P, KT, T], F32R)
        consts = sb("consts", [P, K_END1])
        ones = sb("ones", [P, P])
        vecs = sb("vecs", [P, V_END])
        neg_vecs = sb("neg_vecs", [P, V_END])
        ss = sb("ss", [P, TT])
        ms = sb("ms", [P, TT])
        rstd = sb("rstd", [P, TT])
        half_neg = sb("half_neg", [P, 1])
        eps_rms = sb("eps_rms", [P, 1])
        eps_ln = sb("eps_ln", [P, 1])
        wr = sb("wr", [P, KT, NE])
        upper_r = sb("upper_r", [P, P], F32R)
        ones_r = sb("ones_r", [P, P], F32R)
        wr_parts = sb("wr_parts", [P, KT, 2, NE], F32R)

        mixers = ExitStack()
        region[0] = mixers
        w_pw = sb("w_pw", [P, 2, CONV])
        w_uq = sb("w_uq", [P, 2, HEADS * QD])
        w_ukv = sb("w_ukv", [P, HEADS * KVD])
        tabs = sb("tabs", [P, K_END2])
        bias = sb("bias", [P, HEADS, 3 * P])
        vec_rows = sb("vec_rows", [V_END, P])
        dw_rows = sb("dw_rows", [LAYERS * TAPS, CONV])
        dw = sb("dw", [P, 2, LAYERS * TAPS])
        sub_g = sb("sub_g", [P, LAYERS])
        lam_in = sb("lam_in", [P, 4, LAYERS, HD])
        lam_prod = sb("lam_prod", [P, 2, LAYERS, HD])
        lam_dot = sb("lam_dot", [P, 2, LAYERS])
        lam_exp = sb("lam_exp", [P, 2, LAYERS])
        neg_lam = sb("neg_lam", [P, LAYERS])
        temps = ExitStack()
        region[0] = temps
        cq = sb("cq", [P, 2, T])
        ckv = sb("ckv", [P, T])
        kr = sb("kr", [QD, T])
        sq_q = sb("sq_q", [P, 2, T])
        sq_kv = sb("sq_kv", [P, T])
        rs = sb("rs", [P, 2, T])
        dqk = sb("dqk", [P, 6, T])
        dv = sb("dv", [P, TT, HEADS // 2, 3 * DV])
        q_m = sb("q_m", [QD, HEADS, T])
        rot = sb("rot", [QD, 2, T])
        k_m = sb("k_m", [QD, HEADS, T])
        v_m = sb("v_m", [P, TT, HEADS // 2, 3 * MV])
        glu_a = sb("glu_a", [P, 2, T])
        glu_e = sb("glu_e", [P, 2, T])
        u_pad = sb("u_pad", [P, 2, TAPS - 1 + T])
        cv = sb("cv", [P, 2, 2, T])
        ln_rs = sb("ln_rs", [P, T])
        s_sb = sb("s_sb", [P, 3, 3 * P])
        e_sb = sb("e_sb", [P, 3, 2, 3 * P])
        neg_max = sb("neg_max", [P, UNITS, 2])
        row_sum = sb("row_sum", [P, UNITS, 2])
        coef = sb("coef", [P, UNITS, 2])
        ratio = sb("ratio", [P, HEADS, 2])
        temps.close()
        dense = ExitStack()
        region[0] = dense
        d_sg = sb("d_sg", [P, 2, 2, T])
        d_prod = sb("d_prod", [P, 2, 2, T])
        d_hi = sb("d_hi", [P, 2, 2, T], F32R)
        d_lo = sb("d_lo", [P, 2, 2, T], F32R)
        dense.close()
        mixers.close()
        region[0] = ctx
        onehot = sb("onehot", [P, TT, P], F32R)
        onehot_t = sb("onehot_t", [P, TT, P], F32R)
        g_bc = sb("g_bc", [P, D])
        raw_m = sb("raw_m", [P, RAW_M - RAW_A, PIECE])
        ht_hi = sb("ht_hi", [P, TT, D], F32R)
        ht_lo = sb("ht_lo", [P, TT, D], F32R)
        lg_t = sb("lg_t", [2 * NE, T])
        lg = sb("lg", [P, TT, NE])
        m8 = sb("m8", [P, TT, NE])
        idx = sb("idx", [P, TT, NE], U32)
        idf = sb("idf", [P, TT, NE])
        gap = sb("gap", [P, TT])
        e2 = sb("e2", [P, TT])
        w_top = sb("w_top", [P, 3, TT])
        oh = sb("oh", [P, 2, TT, NE])
        gw = sb("gw", [P, 2, TT, NE])
        chosen = sb("chosen", [P, TT, NE], F32R)
        less1 = sb("less1", [P, TT, NE])
        pos = sb("pos", [P, TT, NE])
        pos_hi = sb("pos_hi", [P, TT, NE])
        cnt = sb("cnt", [P, NE])
        over = sb("over", [P, NE])
        incl = sb("incl", [P, NE])
        rank = sb("rank", [P, NE])
        sel = sb("sel", [P, 3, NE])
        junk = sb("junk", [P, 15, NE])
        it_f = sb("it_f", [P, 4])
        it_i = sb("it_i", [P, 4], I32)
        pos_item = sb("pos_item", [P, TT, ITEMS_MAX + 1])
        g_item = sb("g_item", [P, TT, ITEMS_MAX + 1])
        p_col = sb("p_col", [P, TT])
        g_col = sb("g_col", [P, TT])
        m_sg = sb("m_sg", [P, 2, FC])
        m_prod = sb("m_prod", [P, 2, FC])
        m_hi = sb("m_hi", [P, 2, 2, P], F32R)
        m_lo = sb("m_lo", [P, 2, 2, P], F32R)
        sel_hi = hT_hi[:, 0:4, :].rearrange("p a b -> p (a b)").rearrange("p (k s) -> p k s", k=KT)
        sel_lo = hT_lo[:, 0:4, :].rearrange("p a b -> p (a b)").rearrange("p (k s) -> p k s", k=KT)
        y_hi = hT_hi[:, 4:8, :].rearrange("p a b -> p (a b)")
        y_lo = hT_lo[:, 4:8, :].rearrange("p a b -> p (a b)")

        spare = xn[:].rearrange("p t d -> p (t d)")
        pt_sb = spare[:, 0:6 * P].rearrange("p (s n) -> p s n", s=2)
        tap1 = spare[:, 6 * P:6 * P + 2 * T].rearrange("p (s t) -> p s t", s=2)
        o_sq, o_rs, o_y, tap = (spare[:, 6 * P + m * T:6 * P + (m + 1) * T] for m in range(4))

        ident = consts[:, K_ID:K_ID + P]
        upper = consts[:, K_U:K_U + P]
        iota = consts[:, K_IOTA:K_IOTA + P]
        rotate = consts[0:QD, K_R:K_R + QD]
        blocks = consts[:, K_BLK:K_BLK + P]
        mask = tabs[:, K_MASK:K_MASK + 3 * P]
        dist = tabs[:, K_DIST:K_DIST + 3 * P]
        cos = tabs[0:QD, K_COS:K_COS + T]
        sin = tabs[0:QD, K_SIN:K_SIN + T]

        x_in = [sem(f"x_in{t}") for t in range(TT)]
        early_in = sem("early_in")
        taps_in = sem("taps_in")
        params_in = sem("params_in")
        small_in = sem("small_in")
        raw_in = [sem(f"raw_in{s}") for s in range(RAW_M)]
        gfin_in = sem("gfin_in")
        out_sent = sem("out_sent")
        hi_ready = sem("hi_ready")
        lo_ready = sem("lo_ready")
        piece_used = sem("piece_used")
        const_set = sem("const_set")
        setup_t = sem("setup_t")
        setup_v = sem("setup_v")
        setup_a = sem("setup_a")
        sumsq = sem("sumsq")
        ms_ready = sem("ms_ready")
        rstd_ready = sem("rstd_ready")
        xn_ready = sem("xn_ready")
        hT_mm = sem("hT_mm")
        hThi_done = sem("hThi_done")
        hTlo_done = sem("hTlo_done")
        proj_evac = sem("proj_evac")
        mid_mm = sem("mid_mm")
        mid_act = sem("mid_act")
        mid_dve = sem("mid_dve")
        conv_step = sem("conv_step")
        sigmoid = sem("sigmoid")
        conv_act = sem("conv_act")
        s_mm = sem("s_mm")
        s_max = sem("s_max")
        exp_done = sem("exp_done")
        comb_done = sem("comb_done")
        scaled_diff = sem("scaled_diff")
        scaled_mla = sem("scaled_mla")
        pt_mm = sem("pt_mm")
        pt_diff = sem("pt_diff")
        pt_mla = sem("pt_mla")
        pv_mm = sem("pv_mm")
        coef_ready = sem("coef_ready")
        o_squared = sem("o_squared")
        o_ss_mm = sem("o_ss_mm")
        o_ln = sem("o_ln")
        o_rs_done = sem("o_rs_done")
        o_normed = sem("o_normed")
        tap_done = sem("tap_done")
        pool_taps = sem("pool_taps")
        GROUPS = ("conv", "diff", "mla")
        cat_hi = {g: sem(f"cat_hi_{g}") for g in GROUPS}
        cat_lo = {g: sem(f"cat_lo_{g}") for g in GROUPS}
        acc_part = sem("acc_part")
        x_upd = sem("x_upd")
        sg_done = sem("sg_done")
        prod_done = sem("prod_done")
        act_t = sem("act_t")
        act_hi = sem("act_hi")
        act_lo = sem("act_lo")
        route_mm = sem("route_mm")
        route_v = sem("route_v")
        route_a = sem("route_a")
        items_ready = sem("items_ready")
        onehot_done = sem("onehot_done")
        gather_mm = sem("gather_mm")
        gathered = sem("gathered")
        onehot_tmm = sem("onehot_tmm")
        onehot_tdone = sem("onehot_tdone")
        yhi_done = sem("yhi_done")
        ylo_done = [sem(f"ylo_done{h}") for h in range(2)]
        scat_mm = [sem(f"scat_mm{q}") for q in range(4)]
        logits_mm = sem("logits_mm")
        logits_out = sem("logits_out")
        h_rows = sem("h_rows")
        ht_split = sem("ht_split")
        ht_lo_done = sem("ht_lo_done")

        block = ctx.enter_context(nc.Block())

        def raw_slot(n):
            return raw_a[:, n % RAW_A, :], raw_in[n % RAW_A], 16 * (n // RAW_A + 1)

        trunk_uses = [len(range(s, NA, RAW_A)) if s < RAW_A else 0 for s in range(RAW_M)]

        def expert_slot(i, j):
            s = j % RAW_M
            tile = raw_a[:, s, :] if s < RAW_A else raw_m[:, s - RAW_A, :]
            return tile, raw_in[s], 16 * (trunk_uses[s] + j // RAW_M + 1) + i * (16 * NFF // RAW_M)

        def in_piece_view(t, p):
            c = IN_PIECES[p][1]
            return t[:, 0:KT * c].rearrange("p (k n) -> p k n", k=KT)

        def ff_src(wg, wu, wd, kind, c):
            if kind == "D":
                return wd[c * FC:(c + 1) * FC, :].rearrange("(k p) n -> p k n", p=P)
            w = wg if kind == "G" else wu
            return w[:, c * FC:(c + 1) * FC].rearrange("(k p) n -> p k n", p=P)

        def ff_view(t, kind):
            return t.rearrange("p (k n) -> p k n", n=D if kind == "D" else FC)

        def in_done(l, p):
            return LAYER_PIECE0[l] + p + 1

        def out_done(l):
            return LAYER_PIECE0[l] + NIN + NOUT

        def dense_done(kind, c):
            return LAYER_PIECE0[0] + NIN + NOUT + ORDER.index((kind, c)) + 1

        def expert_done(i, kind, c):
            return NA + ORDER.index((kind, c)) + 1 + i * NFF

        def transposed_after(kind, c):
            if kind == "G" and c >= 1:
                return c - 1
            if kind == "D" and c == NCH - 2:
                return NCH - 1
            return None

        trunk_width = {}
        for l in range(LAYERS):
            for p in range(NIN):
                trunk_width[LAYER_PIECE0[l] + p] = KT * IN_PIECES[p][1]

        def load_rows(eng, part):
            rows = [("attn_norm", V_ATTN), ("b_glu", V_BGLU), ("b_dw", V_BDW), ("conv_ln_g", V_LNG),
                    ("conv_ln_b", V_LNB), ("b_pw", V_BPW), ("q_norm", V_QN), ("kv_norm", V_KVN),
                    ("ffn_norm", V_FFN)]
            ends = [r for _, r in rows[1:]] + [V_SUB]
            moves = [(vec_rows[r0:r1, :], a[name].rearrange("l (k p) -> (l k) p", p=P))
                     for (name, r0), r1 in zip(rows, ends)]
            moves += [(vec_rows[V_SUB:V_END, h * DV:(h + 1) * DV], a["diff_subln"]) for h in range(2)]
            for dst, src in moves[part]:
                eng.dma_start(dst, src).then_inc(early_in, 16)

        @block.sync
        def _(sp):
            for t in range(TT):
                sp.dma_start(x[:, t, :], a["x"][0, t * P:(t + 1) * P, :]).then_inc(x_in[t], 16)
            sp.dma_start(consts[:], a["table1"]).then_inc(early_in, 16)
            def load(n, src, view):
                if n >= RAW_A:
                    sp.wait_ge(lo_ready, n - RAW_A + 1)
                t, s, _ = raw_slot(n)
                sp.dma_start(view(t), src).then_inc(s, 16)

            def load_small(l):
                sp.dma_start(w_pw[:], a["w_pw"][l].rearrange("(k p) n -> p k n", p=P)).then_inc(small_in, 16)
                sp.dma_start(w_uq[:], a["w_uq"][l].rearrange("(k p) n -> p k n", p=P)).then_inc(small_in, 16)
                sp.dma_start(w_ukv[:], a["w_ukv"][l]).then_inc(small_in, 16)

            for l in range(LAYERS):
                n0 = LAYER_PIECE0[l]
                for p, (c0, cn) in enumerate(IN_PIECES):
                    if l == 0 and p == 1:
                        load_rows(sp, slice(3, None))
                    load(n0 + p, a["w_in"][l][:, c0:c0 + cn].rearrange("(k p) n -> p k n", p=P),
                         lambda t, p=p: in_piece_view(t, p))
                    if l == 0 and p == 2:
                        load_small(0)
                for i in range(NOUT):
                    k0 = OUT_ORDER[i] * 2 * P
                    load(n0 + NIN + i, a["w_out"][l][k0:k0 + 2 * P, :].rearrange("(k p) n -> p k n", p=P),
                         lambda t: ff_view(t, "D"))
                if l == 0:
                    sp.wait_ge(mid_mm, MID)
                    load_small(1)
                    for j, (kind, c) in enumerate(ORDER):
                        load(n0 + NIN + NOUT + j,
                             ff_src(a["w_gate_dense"][0], a["w_up_dense"][0], a["w_down_dense"][0], kind, c),
                             lambda t, kind=kind: ff_view(t, kind))

            def expert_loads(e, i, first):
                for j, (kind, c) in enumerate(ORDER):
                    if first and j < RAW_A:
                        sp.wait_ge(lo_ready, max(n for n in range(NA) if n % RAW_A == j) + 1)
                    elif first and j < RAW_M:
                        sp.wait_ge(x_upd, 12)
                    else:
                        sp.wait_ge(lo_ready, NA + j - RAW_M + 1 + i * NFF)
                    t, s, _ = expert_slot(i, j)
                    one = bass.ds(e, 1)
                    if kind == "D":
                        src = a["w_down_exp"][0][one, c * FC:(c + 1) * FC, :].rearrange("e (k p) n -> p (e k) n", p=P)
                    else:
                        w = a["w_gate_exp" if kind == "G" else "w_up_exp"][0]
                        src = w[one, :, c * FC:(c + 1) * FC].rearrange("e (k p) n -> p (e k) n", p=P)
                    sp.dma_start(ff_view(t, kind), src).then_inc(s, 16)

            expert_loads(0, 0, True)
            with sp.Fori(1, NE) as i:
                expert_loads(i, i, False)
            sp.wait_ge(items_ready, 1)
            n_items = sp.value_load(it_i[0:1, 0:1], min_val=NE, max_val=ITEMS_MAX)
            for j in range(3):
                e = sp.value_load(it_i[0:1, 1 + j:2 + j], min_val=0, max_val=NE - 1)
                with sp.If(n_items > NE + j):
                    expert_loads(e, NE + j, False)
            sp.wait_ge(xn_ready, TT * 2 * LAYERS + 1)
            sp.dma_start(out[0, 0:P, :], xn[:, 0, :]).then_inc(out_sent, 16)
            sp.wait_ge(out_sent, 16 * TT)

        @block.gpsimd
        def _(pool):
            nc.gpsimd.memset(ones[:], 1.0).then_inc(const_set, 1)
            nc.gpsimd.memset(half_neg[:], -0.5).then_inc(const_set, 1)
            nc.gpsimd.memset(eps_rms[:], RMS_EPS).then_inc(const_set, 1)
            nc.gpsimd.memset(eps_ln[:], LN_EPS).then_inc(const_set, 1)

            def zeros():
                nc.gpsimd.memset(u_pad[:, :, 0:TAPS - 1], 0.0).then_inc(const_set, 1)
                nc.gpsimd.memset(dv[:, :, :, DV:2 * DV], 0.0).then_inc(const_set, 1)
                nc.gpsimd.memset(v_m[:, :, :, MV:2 * MV], 0.0).then_inc(const_set, 1)

            zeros()
            pool.dma_start(dw_rows[:], a["w_dw"].rearrange("l w c -> (l w) c")).then_inc(taps_in, 16)

            def norm_pow(j):
                for t in range(TT):
                    pool.wait_ge(ms_ready, TT * j + t + 1)
                    nc.gpsimd.tensor_tensor(rstd[:, t:t + 1], ms[:, t:t + 1], half_neg[:, 0:1], ALU.pow
                                            ).then_inc(rstd_ready, 1)

            norm_pow(0)
            pool.dma_start(tabs[:], a["table2"]).then_inc(params_in, 16)
            for m, name in enumerate(["lambda_q1", "lambda_k1", "lambda_q2", "lambda_k2"]):
                pool.dma_start(lam_in[:, m].rearrange("p l d -> p (l d)"),
                               a[name].rearrange("(o l) d -> o (l d)", o=1).broadcast_to([P, LAYERS * HD])
                               ).then_inc(params_in, 16)
            pool.dma_start(wr[:], a["w_router"][0].rearrange("(k p) e -> p k e", p=P)).then_inc(params_in, 16)
            for l in range(LAYERS):
                if l > 0:
                    norm_pow(2 * l)
                    pool.wait_ge(x_upd, 8)
                    zeros()
                if l == 0:
                    pool.wait_ge(setup_a, 2)
                pool.wait_ge(conv_step, CS * l + CS_U - 1)
                for w in range(POOL_TAPS):
                    win = u_pad[:, 1, w:w + T]
                    wc = dw[:, 1, TAPS * l + w:TAPS * l + w + 1]
                    if w == 0:
                        b = V_BDW + 2 * l + 1
                        r = nc.gpsimd.tensor_scalar(cv[:, 0, 1, :], win, wc, vecs[:, b:b + 1], ALU.mult, ALU.add)
                    else:
                        pool.wait_ge(pool_taps, POOL_TAPS * l + w)
                        nc.gpsimd.tensor_scalar(tap, win, wc, None, ALU.mult).then_inc(tap_done, 1)
                        pool.wait_ge(tap_done, (POOL_TAPS - 1) * l + w)
                        r = nc.gpsimd.tensor_tensor(cv[:, w % 2, 1, :], tap, cv[:, (w + 1) % 2, 1, :], ALU.add)
                    r.then_inc(pool_taps, 1)
                if l == LAYERS - 1:
                    pool.wait_ge(mid_mm, MID * l + 4)
                    pool.dma_start(g_bc[:], a["ffn_norm"][l:l + 1, :].broadcast_to([P, D])).then_inc(gfin_in, 16)
                norm_pow(2 * l + 1)
            pool.wait_ge(gfin_in, 16)
            pool.wait_ge(hT_mm, 16)
            for t in range(TT):
                nc.gpsimd.tensor_tensor(xn[:, t, :], xn[:, t, :], g_bc[:], ALU.mult).then_inc(h_rows, 1)
            pool.wait_ge(h_rows, 2)
            pool.dma_start(g_bc[:], a["final_norm"].rearrange("(o d) -> o d", o=1).broadcast_to([P, D])
                           ).then_inc(gfin_in, 16)
            norm_pow(2 * LAYERS)

        def units_of(k):
            return [2 * k, 2 * k + 1] if k < HEADS else [HEADS + k]

        def head_of(k):
            return (k, k // 2) if k < HEADS else (2 * (5 - k // 2) + k % 2, 5 - k // 2)

        def hi_of(n):
            return hi_ring[:, n % SPLIT, :]

        def lo_of(n):
            return lo_ring[:, n % SPLIT, :]

        @block.scalar
        def _(act):
            A = nc.scalar.activation

            def split(n):
                w = trunk_width.get(n, PIECE)
                t, s, v = raw_slot(n)
                act.wait_ge(s, v)
                if n >= SPLIT:
                    act.wait_ge(piece_used, n - SPLIT + 1)
                A(hi_of(n)[:, 0:w], t[:, 0:w], ACT.Copy).then_inc(hi_ready, 1)

            def split_expert(i, j):
                t, s, v = expert_slot(i, j)
                act.wait_ge(s, v)
                act.wait_ge(piece_used, NA + j - SPLIT + 1 + i * NFF)
                A(hi_of(NA + j), t, ACT.Copy).then_inc(hi_ready, 1)

            def norm_squares(j, upd=None):
                for t in range(TT):
                    if upd is None:
                        act.wait_ge(x_in[t], 16)
                    else:
                        act.wait_ge(x_upd, upd + 2 * t + 2)
                    A(xn[:, t, :], x[:, t, :], ACT.Square, accum_out=ss[:, t:t + 1]).then_inc(sumsq, 1)

            def norm_evac(j, g0):
                for k in range(KT):
                    if k % 2 == 0:
                        act.wait_ge(hT_mm, 4 * j + k // 2 + 1)
                    A(hT_hi[:, k, :], bank[k // 2][:, (k % 2) * T:(k % 2 + 1) * T], ACT.Copy,
                      scale=vecs[:, g0 + k:g0 + k + 1]).then_inc(hThi_done, 1)

            nc.scalar.preload_act_table_set("natural_log_exp_and_others")
            load_rows(act, slice(0, 3))
            act.wait_ge(const_set, N_CONST)
            norm_squares(0)
            split(0)
            act.wait_ge(setup_t, 1)
            A(vecs[:], bank[4][:, 0:V_END], ACT.Copy).then_inc(setup_a, 1)
            act.wait_ge(setup_a, 1)

            for l in range(LAYERS):
                n0 = LAYER_PIECE0[l]
                if l > 0:
                    split(n0)
                    split(n0 + 1)
                    nc.scalar.preload_act_table_set("natural_log_exp_and_others")
                    norm_squares(2 * l, 4)
                norm_evac(2 * l, V_ATTN + KT * l)
                if l == 0:
                    split(n0 + 1)
                split(n0 + 2)
                if l == 0:
                    act.wait_ge(setup_t, 2)
                    A(dw[:], bank[7][:, 0:2 * LAYERS * TAPS].rearrange("p (c w) -> p c w", c=2),
                      ACT.Copy).then_inc(setup_a, 1)

                def sigmoids(m):
                    A(glu_e[:], glu_e[:], ACT.Ln, bias=ones[:, 0:1]).then_inc(sigmoid, 1)
                    act.wait_ge(sigmoid, 4 * l + 2 * m + 1)
                    A(glu_e[:], glu_e[:], ACT.Exp, scale=-1.0).then_inc(sigmoid, 1)

                def mid(g):
                    act.wait_ge(mid_mm, MID * l + g + 1)

                def mid_inc(ins):
                    ins.then_inc(mid_act, 1)

                def exponentials(k):
                    for i, u in enumerate(units_of(k)):
                        act.wait_ge(s_max, 2 * (UNITS * l + u + 1))
                        if i == 0 and SLOTS * l + k >= 3:
                            act.wait_ge(pt_mm, SLOTS * l + k - 2)
                        e = e_sb[:, k % 3, i, :]
                        A(e[:, 0:P], s_sb[:, u % 3, 0:P], ACT.Exp, scale=-1.0, bias=neg_max[:, u, 0:1],
                          accum_out=row_sum[:, u, 0:1])
                        A(e[:, P:3 * P], s_sb[:, u % 3, P:3 * P], ACT.Exp, scale=-1.0, bias=neg_max[:, u, 1:2],
                          accum_out=row_sum[:, u, 1:2]).then_inc(exp_done, 1)

                def copy_transposed(k):
                    act.wait_ge(pt_mm, SLOTS * l + k + 1)
                    if SLOTS * l + k >= 2:
                        act.wait_ge(pv_mm, SLOTS * l + k - 1)
                    A(pt_sb[:, k % 2, :], bank[T_BANK[k % 2]][:, 0:3 * P], ACT.Copy).then_inc(pt_mla, 1)

                def scale(k):
                    act.wait_ge(comb_done, HEADS * l + k + 1)
                    u, e = units_of(k)[0], e_sb[:, k % 3, 0, :]
                    A(e[:, 0:P], e[:, 0:P], ACT.Copy, scale=coef[:, u, 0:1])
                    A(e[:, P:3 * P], e[:, P:3 * P], ACT.Copy, scale=coef[:, u, 1:2]).then_inc(scaled_diff, 1)

                for p in range(NIN):
                    act.wait_ge(piece_used, in_done(l, p))
                    b = bank[4 + p % 4]
                    if p == 0:
                        A(glu_a[:, 0, :], b[:, 0:T], ACT.Identity,
                          bias=vecs[:, V_BGLU + 4 * l:V_BGLU + 4 * l + 1])
                        r = A(glu_a[:, 1, :], b[:, T:2 * T], ACT.Identity,
                              bias=vecs[:, V_BGLU + 4 * l + 1:V_BGLU + 4 * l + 2])
                    elif p == 1:
                        if l == 0:
                            act.wait_ge(setup_v, 1)
                        A(glu_e[:, 0, :], b[:, 0:T], ACT.Exp, scale=-1.0,
                          bias=neg_vecs[:, V_BGLU + 4 * l + 2:V_BGLU + 4 * l + 3])
                        r = A(glu_e[:, 1, :], b[:, T:2 * T], ACT.Exp, scale=-1.0,
                              bias=neg_vecs[:, V_BGLU + 4 * l + 3:V_BGLU + 4 * l + 4])
                    elif p == 2:
                        A(cq[:], b[:].rearrange("p (c t) -> p c t", c=2), ACT.Copy)
                        r = A(sq_q[:], b[:].rearrange("p (c t) -> p c t", c=2), ACT.Square)
                    elif p == 3:
                        A(ckv[:], b[:, 0:T], ACT.Copy)
                        A(sq_kv[:], b[:, 0:T], ACT.Square)
                        r = A(kr[:], b[0:QD, T:2 * T], ACT.Copy)
                    elif p < 7:
                        r = A(dqk[:, 2 * (p - 4):2 * (p - 4) + 2, :], b[:].rearrange("p (c t) -> p c t", c=2), ACT.Copy)
                    else:
                        src = b[:, 0:384].rearrange("p (t h d) -> p t h d", t=TT, h=3)
                        if p == 7:
                            A(dv[:, :, 0, :].rearrange("p t (h d) -> p t h d", h=3)[:, :, 0:3:2, :], src[:, :, 0:2, :],
                              ACT.Copy)
                            r = A(dv[:, :, 1, 0:DV], src[:, :, 2, :], ACT.Copy)
                        else:
                            A(dv[:, :, 1, 2 * DV:], src[:, :, 0, :], ACT.Copy)
                            r = A(dv[:, :, 2, :].rearrange("p t (h d) -> p t h d", h=3)[:, :, 0:3:2, :],
                                  src[:, :, 1:3, :], ACT.Copy)
                    r.then_inc(proj_evac, 1)
                    if p == 1:
                        act.wait_ge(proj_evac, NIN * l + 2)
                        sigmoids(0)
                    if p < NIN - 1:
                        split(n0 + 3 + p)
                    if l == 0 and p == 1:
                        act.wait_ge(params_in, 16 * N_PARAMS)
                        A(upper_r[:], upper, ACT.Copy)
                        A(ones_r[:], ones[:], ACT.Copy)
                        A(wr_parts[:, :, 0, :], wr[:], ACT.Copy).then_inc(setup_a, 1)
                        act.wait_ge(setup_v, 3)
                        A(lam_exp[:], lam_dot[:], ACT.Exp).then_inc(setup_a, 1)
                    if p == 4:
                        mid(0)
                        A(rs[:, 0, :], bank[0][:, 0:T], ACT.Ln, scale=1.0 / QR, bias=eps_rms[:])
                        A(rs[:, 1, :], bank[0][:, T:2 * T], ACT.Ln, scale=1.0 / KR, bias=eps_rms[:]).then_inc(conv_act, 1)
                        act.wait_ge(conv_act, CA * l + 1)
                        mid_inc(A(rs[:], rs[:], ACT.Exp, scale=-0.5))
                    if p == 5:
                        for r3 in range(3):
                            mid(1 + r3)
                            mid_inc(A(q_m[:, 2 * r3:2 * r3 + 2, :],
                                      bank[1 + r3][0:QD, :].rearrange("p (h t) -> p h t", h=2), ACT.Copy))
                    if p == 6:
                        for t in range(TT):
                            mid(5 + t)
                            mid_inc(A(v_m[:, t].rearrange("p r (h d) -> p r h d", h=3)[:, :, 0:3:2, :],
                                      bank[1 + t][:, 0:HEADS * MV].rearrange("p (r h d) -> p r h d", r=HEADS // 2, h=2),
                                      ACT.Copy))
                        act.wait_ge(mid_dve, DVE_MID_STEPS * l + 6)
                        mid_inc(A(k_m[NOPE:QD, :, :], kr[NOPE:QD, :].unsqueeze(1).broadcast_to([ROPE, HEADS, T]),
                                  ACT.Copy))
                    if p in KEYS_AT:
                        for r3 in KEYS_AT[p]:
                            mid(10 + r3)
                            mid_inc(A(k_m[0:NOPE, 2 * r3:2 * r3 + 2, :],
                                      bank[MID_BANK[10 + r3]][0:NOPE, :].rearrange("p (h t) -> p h t", h=2), ACT.Copy))
                    if p == 7:
                        exponentials(0)
                scale(0)
                for k in range(SLOTS + 3):
                    if 1 <= k < SLOTS:
                        exponentials(k)
                    j = (k - 4) // 2
                    if k % 2 == 0 and 0 <= j < 3:
                        act.wait_ge(pv_mm, SLOTS * l + 2 * j + 2)
                        A(o_sq, bank[O_BANK[j % 2]][:, 0:T], ACT.Square).then_inc(o_squared, 1)
                    j = (k - 5) // 2
                    if k % 2 == 1 and 0 <= j < 3:
                        act.wait_ge(o_ss_mm, 3 * l + j + 1)
                        if 3 * l + j > 0:
                            act.wait_ge(o_normed, 3 * l + j)
                        A(o_rs, bank[O_BANK[j % 2]][:, T:2 * T], ACT.Ln, scale=1.0 / DV, bias=eps_ln[:]
                          ).then_inc(o_ln, 1)
                        act.wait_ge(o_ln, 3 * l + j + 1)
                        A(o_rs, o_rs, ACT.Exp, scale=-0.5).then_inc(o_rs_done, 1)
                    j = (k - 7) // 2
                    if k % 2 == 1 and 0 <= j < 3:
                        act.wait_ge(o_normed, 3 * l + j + 1)
                        A(hT_hi[:, 5 + j, :], o_y, ACT.Copy).then_inc(cat_hi["diff"], 1)
                    j = (k - 4) // 2
                    if k % 2 == 0 and 3 <= j < 6:
                        act.wait_ge(pv_mm, SLOTS * l + 2 * j + 2)
                        A(hT_hi[:, 2 + 5 - j, :], bank[O_BANK[j % 2]][:, 0:T], ACT.Copy).then_inc(cat_hi["mla"], 1)
                    if HEADS <= k - 2 < SLOTS:
                        copy_transposed(k - 2)
                    if 2 <= k <= HEADS:
                        scale(k - 1)
                    if k == 13:
                        mid(15)
                        for c in range(2):
                            A(hT_hi[:, c, :], bank[7][:, c * T:(c + 1) * T], ACT.Identity,
                              bias=vecs[:, V_BPW + 2 * l + c:V_BPW + 2 * l + c + 1]).then_inc(cat_hi["conv"], 1)
                        split(n0 + 11)
                    if k == 5:
                        act.wait_ge(conv_step, CS * l + CS_CENTRED)
                        A(glu_e[:], cv[:, 1], ACT.Square).then_inc(conv_act, 1)
                    if k == 7:
                        mid(14)
                        A(ln_rs[:], bank[7][:, 0:T], ACT.Ln, scale=1.0 / CONV, bias=eps_ln[:]).then_inc(conv_act, 1)
                        act.wait_ge(conv_act, CA * l + 3)
                        A(ln_rs[:], ln_rs[:], ACT.Exp, scale=-0.5).then_inc(conv_act, 1)
                    if k == 9:
                        act.wait_ge(conv_step, CS * l + CS_NORMED)
                        for c in range(2):
                            r = A(glu_e[:, c, :], cv[:, 0, c, :], ACT.Exp,
                                  scale=neg_vecs[:, V_LNG + 2 * l + c:V_LNG + 2 * l + c + 1],
                                  bias=neg_vecs[:, V_LNB + 2 * l + c:V_LNB + 2 * l + c + 1])
                        r.then_inc(conv_act, 1)
                    if k == 10:
                        act.wait_ge(conv_act, CA * (l + 1))
                        sigmoids(1)
                split(n0 + 12)
                f0 = n0 + NIN + NOUT
                for m in range(2):
                    if l == 0:
                        split(f0 + m)
                    else:
                        split_expert(0, m)
                norm_squares(2 * l + 1, 8 * l)
                if l == 0:
                    norm_evac(1, V_FFN)
                    for j, (kind, c) in enumerate(ORDER):
                        if j + 2 < NFF:
                            split(f0 + j + 2)
                        if kind == "U":
                            act.wait_ge(piece_used, dense_done("U", c))
                            for f in range(2):
                                if c >= 2:
                                    act.wait_ge(prod_done, 2 * (c - 2) + f + 1)
                                A(d_sg[:, c % 2, f, :], bank[(c % 2) * 2 + f][:, 0:T], ACT.Silu).then_inc(sg_done, 1)
                            for f in range(2):
                                act.wait_ge(prod_done, 2 * c + f + 1)
                                if c >= 2:
                                    act.wait_ge(piece_used, dense_done("D", c - 2))
                                A(d_hi[:, c % 2, f, :], d_prod[:, c % 2, f, :], ACT.Copy).then_inc(act_hi, 1)
                else:
                    norm_evac(3, V_FFN + KT)

            act.wait_ge(logits_mm, 1)
            A(lg_t[:], bank[4][0:2 * NE, 0:T], ACT.Copy).then_inc(logits_out, 1)
            for t in range(TT):
                act.wait_ge(h_rows, t + 1)
                A(ht_hi[:, t, :], xn[:, t, :], ACT.Copy).then_inc(ht_split, 1)
            act.wait_ge(route_v, RV_GAP)
            A(e2[:], gap[:], ACT.Exp).then_inc(route_a, 1)

            def gather_evac(i):
                for h in range(4):
                    act.wait_ge(gather_mm, 4 * i + h + 1)
                    part, b = (sel_hi, bank[6 + h]) if h < 2 else (sel_lo, bank[h - 2])
                    h0 = 4 * (h % 2)
                    A(part[:, h0:h0 + 4, :], b[:].rearrange("p (k s) -> p k s", k=4), ACT.Copy).then_inc(gathered, 1)

            def item(i, more):
                for j, (kind, c) in enumerate(ORDER):
                    if j + 2 < NFF or more is True:
                        split_expert(i, j + 2)
                    else:
                        with act.If(more):
                            split_expert(i, j + 2)
                    if kind == "U":
                        act.wait_ge(piece_used, expert_done(i, "U", c))
                        act.wait_ge(prod_done, GU0 + c - 1 + i * NCH)
                        A(m_sg[:, c % 2, :], bank[c % 2][:, 0:FC], ACT.Silu).then_inc(sg_done, 1)
                    if kind == "G" and c == 2:
                        act.wait_ge(onehot_tmm, i + 1)
                        A(onehot_t[:], bank[6][:, 0:TT * P].rearrange("p (t s) -> p t s", t=TT),
                          ACT.Copy).then_inc(onehot_tdone, 1)
                    tc = transposed_after(kind, c)
                    if tc is not None:
                        act.wait_ge(act_t, tc + 1 + i * NCH)
                        if tc >= 2:
                            act.wait_ge(piece_used, expert_done(i, "D", tc - 2))
                        A(m_hi[:, tc % 2, :, :], bank[2 + tc % 2][:, 0:2 * P].rearrange("p (f s) -> p f s", f=2),
                          ACT.Copy).then_inc(act_hi, 1)
                gather_evac(i + 1)
                act.wait_ge(piece_used, expert_done(i, "D", NCH - 1))
                for h in range(2):
                    A(y_hi[:, h * 512:(h + 1) * 512], bank[4 + h][:], ACT.Copy).then_inc(yhi_done, 1)

            gather_evac(0)
            item(0, True)
            act.wait_ge(items_ready, 1)
            n_items = act.value_load(it_i[0:1, 0:1], min_val=NE, max_val=ITEMS_MAX)
            with act.Fori(1, n_items) as i:
                item(i, i < n_items - 1)
            norm_squares(2 * LAYERS, n_items * 4 + (XU0 - 4))
            act.wait_ge(xn_ready, TT * (2 * LAYERS + 1))
            act.dma_start(out[0, P:2 * P, :], xn[:, 1, :]).then_inc(out_sent, 16)

        @block.vector
        def _(dve):
            V = nc.vector

            def split(n):
                w = trunk_width.get(n, PIECE)
                dve.wait_ge(hi_ready, n + 1)
                V.tensor_tensor(lo_of(n)[:, 0:w], raw_slot(n)[0][:, 0:w], hi_of(n)[:, 0:w].bitcast(F32),
                                ALU.subtract).then_inc(lo_ready, 1)

            def split_expert(i, j):
                dve.wait_ge(hi_ready, NA + j + 1 + i * NFF)
                V.tensor_tensor(lo_of(NA + j), expert_slot(i, j)[0], hi_of(NA + j).bitcast(F32),
                                ALU.subtract).then_inc(lo_ready, 1)

            def norm_ms(j, t):
                dve.wait_ge(sumsq, TT * j + t + 1)
                V.tensor_scalar(ms[:, t:t + 1], ss[:, t:t + 1], 1.0 / D, RMS_EPS, ALU.mult, ALU.add
                                ).then_inc(ms_ready, 1)

            def norm_rows(j, t):
                dve.wait_ge(rstd_ready, TT * j + t + 1)
                if j < 2 * LAYERS:
                    r = V.tensor_scalar(xn[:, t, :], x[:, t, :], rstd[:, t:t + 1], None, ALU.mult)
                else:
                    r = V.scalar_tensor_tensor(xn[:, t, :], x[:, t, :], rstd[:, t:t + 1], g_bc[:], ALU.mult, ALU.mult)
                r.then_inc(xn_ready, 1)

            def update_and_norm(j, add):
                add(0)
                add(1)
                add(2)
                norm_ms(j, 0)
                add(3)
                norm_rows(j, 0)
                norm_ms(j, 1)
                norm_rows(j, 1)

            def norm_evac(j, g0):
                for k in range(KT):
                    dve.wait_ge(hThi_done, KT * j + 2 * (k // 2) + 2)
                    V.scalar_tensor_tensor(hT_lo[:, k, :], bank[k // 2][:, (k % 2) * T:(k % 2 + 1) * T],
                                           vecs[:, g0 + k:g0 + k + 1], hT_hi[:, k, :].bitcast(F32),
                                           ALU.mult, ALU.subtract).then_inc(hTlo_done, 1)

            def add_to_x(q, done, a, banks):
                t, n = q // 2, q % 2
                if q < 3:
                    dve.wait_ge(acc_part, 3 * a + q + 1)
                else:
                    dve.wait_ge(piece_used, done)
                V.tensor_tensor(x[:, t, n * 512:(n + 1) * 512], x[:, t, n * 512:(n + 1) * 512], banks[q][:],
                                ALU.add).then_inc(x_upd, 1)

            for t in range(TT):
                norm_ms(0, t)
            for t in range(TT):
                norm_rows(0, t)
            split(0)
            dve.wait_ge(setup_a, 1)
            V.tensor_scalar(neg_vecs[:], vecs[:], -1.0, None, ALU.mult).then_inc(setup_v, 1)

            for l in range(LAYERS):
                n0 = LAYER_PIECE0[l]
                norm_evac(2 * l, V_ATTN + KT * l)
                split(n0 + 1)
                split(n0 + 2)

                def setup():
                    dve.wait_ge(params_in, 16 * N_PARAMS)
                    V.tensor_tensor(lam_prod[:], lam_in[:, 0:4:2], lam_in[:, 1:4:2], ALU.mult).then_inc(setup_v, 1)
                    dve.wait_ge(setup_v, 2)
                    V.tensor_reduce(lam_dot[:], lam_prod[:], AX.X, ALU.add).then_inc(setup_v, 1)
                    for h in range(HEADS):
                        slope = 2.0 ** (-8.0 * (h + 1) / HEADS)
                        V.scalar_tensor_tensor(bias[:, h, :], dist, -slope * HD ** 0.5, mask, ALU.mult, ALU.add).then_inc(setup_v, 1)
                    for m in range(LAYERS):
                        li = 0.8 - 0.6 * math.exp(-0.3 * m)
                        V.tensor_scalar(sub_g[:, m:m + 1], vecs[:, V_SUB + m:V_SUB + m + 1], 1.0 - li, None, ALU.mult
                                        ).then_inc(setup_v, 1)

                def setup_lambda():
                    dve.wait_ge(setup_a, 4)
                    V.tensor_tensor(wr_parts[:, :, 1, :], wr[:], wr_parts[:, :, 0, :].bitcast(F32), ALU.subtract
                                    ).then_inc(setup_v, 1)
                    V.tensor_tensor(neg_lam[:], lam_exp[:, 1], lam_exp[:, 0], ALU.subtract).then_inc(setup_v, 1)
                    dve.wait_ge(setup_v, SETUP_V - LAYERS)
                    for m in range(LAYERS):
                        li = 0.8 - 0.6 * math.exp(-0.3 * m)
                        V.tensor_scalar(neg_lam[:, m:m + 1], neg_lam[:, m:m + 1], -li, None, ALU.add).then_inc(setup_v, 1)

                cs = [CS * l]
                ms_ = [DVE_MID_STEPS * l]

                def conv(ins):
                    cs[0] += 1
                    ins.then_inc(conv_step, 1)

                def mids(ins):
                    ms_[0] += 1
                    ins.then_inc(mid_dve, 1)

                tap_list = []
                for w in range(TAPS):
                    tap_list.append((0, w))
                    if w < TAPS - POOL_TAPS:
                        tap_list.append((1, POOL_TAPS + w))
                last_tap = {}

                def taps(count):
                    for c, w in tap_list[:count]:
                        win = u_pad[:, c, w:w + T]
                        wc = dw[:, c, TAPS * l + w:TAPS * l + w + 1]
                        b = V_BDW + 2 * l + c
                        if c in last_tap:
                            dve.wait_ge(conv_step, last_tap[c])
                        if w == 0:
                            conv(V.tensor_scalar(cv[:, 0, c, :], win, wc, vecs[:, b:b + 1], ALU.mult, ALU.add))
                        elif c not in last_tap:
                            conv(V.tensor_scalar(tap1[:, w % 2, :], win, wc, None, ALU.mult))
                        else:
                            out, old = (tap1[:, w % 2, :], tap1[:, (w + 1) % 2, :]) if c else \
                                       (cv[:, w % 2, 0, :], cv[:, (w + 1) % 2, 0, :])
                            conv(V.scalar_tensor_tensor(out, win, wc, old, ALU.mult, ALU.add))
                        last_tap[c] = cs[0]
                    del tap_list[:count]

                def join_taps():
                    dve.wait_ge(pool_taps, POOL_TAPS * (l + 1))
                    dve.wait_ge(conv_step, cs[0])
                    conv(V.tensor_tensor(cv[:, 0, 1, :], cv[:, (POOL_TAPS - 1) % 2, 1, :], tap1[:, (TAPS - 1) % 2, :],
                                         ALU.add))

                def glu():
                    dve.wait_ge(sigmoid, 4 * l + 2)
                    dve.wait_ge(const_set, N_CONST + 3 * (l + 1))
                    for c in range(2):
                        conv(V.tensor_tensor(u_pad[:, c, TAPS - 1:], glu_a[:, c, :], glu_e[:, c, :], ALU.mult))
                    dve.wait_ge(conv_step, cs[0])

                def latents():
                    dve.wait_ge(mid_act, ACT_MID_STEPS * l + 1)
                    for c in range(2):
                        mids(V.scalar_tensor_tensor(cq[:, c, :], cq[:, c, :],
                                                    vecs[:, V_QN + 2 * l + c:V_QN + 2 * l + c + 1], rs[:, 0, :],
                                                    ALU.mult, ALU.mult))
                    mids(V.scalar_tensor_tensor(ckv[:], ckv[:], vecs[:, V_KVN + l:V_KVN + l + 1], rs[:, 1, :],
                                                ALU.mult, ALU.mult))

                def rope_q(pairs):
                    for r3 in pairs:
                        pair = q_m[:, 2 * r3:2 * r3 + 2, :]
                        wide = [QD, 2, T]
                        dve.wait_ge(mid_mm, MID * l + 8 + r3)
                        dve.wait_ge(mid_dve, ms_[0])
                        mids(V.tensor_tensor(pair, pair, cos.unsqueeze(1).broadcast_to(wide), ALU.mult))
                        mids(V.tensor_tensor(rot[:], bank[MID_BANK[7 + r3]][0:QD, :].rearrange("p (h t) -> p h t", h=2),
                                             sin.unsqueeze(1).broadcast_to(wide), ALU.mult))
                        dve.wait_ge(mid_dve, ms_[0])
                        mids(V.tensor_tensor(pair, pair, rot[:], ALU.add))

                cr = [CR * l]

                def coefs(ins):
                    cr[0] += 1
                    ins.then_inc(coef_ready, 1)

                def maxima(k):
                    for u in units_of(k):
                        dve.wait_ge(s_mm, UNITS * l + u + 1)
                        if UNITS * l + u >= 3:
                            dve.wait_ge(exp_done, UNITS * l + u - 2)
                        if u < 2 * HEADS:
                            sc, bi = HD ** -0.5, bias[:, u // 2, :]
                        else:
                            sc, bi = QD ** -0.5, mask
                        if l == 0 and u == 0:
                            dve.wait_ge(setup_v, SETUP_V)
                        for b, (c0, c1) in enumerate(((0, P), (P, 3 * P))):
                            V.tensor_tensor_reduce(s_sb[:, u % 3, c0:c1], bank[S_BANK[u % 3]][:, c0:c1], bi[:, c0:c1],
                                                   -sc, 3e38, ALU.add, ALU.min, neg_max[:, u, b:b + 1]
                                                   ).then_inc(s_max, 1)

                def combine(k):
                    us = units_of(k)
                    dve.wait_ge(exp_done, UNITS * l + us[-1] + 1)
                    if k >= HEADS:
                        coefs(V.reciprocal(coef[:, us[0]], row_sum[:, us[0]]))
                        dve.wait_ge(coef_ready, cr[0])
                        e = e_sb[:, k % 3, 0, :]
                        V.tensor_scalar(e[:, 0:P], e[:, 0:P], coef[:, us[0], 0:1], None, ALU.mult)
                        V.tensor_scalar(e[:, P:3 * P], e[:, P:3 * P], coef[:, us[0], 1:2], None, ALU.mult
                                        ).then_inc(scaled_mla, 1)
                        return
                    coefs(V.reciprocal(coef[:, us[0]:us[1] + 1], row_sum[:, us[0]:us[1] + 1]))
                    dve.wait_ge(coef_ready, cr[0])
                    coefs(V.scalar_tensor_tensor(ratio[:, k], coef[:, us[1]], neg_lam[:, l:l + 1], row_sum[:, us[0]],
                                                 ALU.mult, ALU.mult))
                    dve.wait_ge(coef_ready, cr[0])
                    e = e_sb[:, k % 3]
                    V.scalar_tensor_tensor(e[:, 0, 0:P], e[:, 1, 0:P], ratio[:, k, 0:1], e[:, 0, 0:P],
                                           ALU.mult, ALU.add)
                    V.scalar_tensor_tensor(e[:, 0, P:3 * P], e[:, 1, P:3 * P], ratio[:, k, 1:2], e[:, 0, P:3 * P],
                                           ALU.mult, ALU.add).then_inc(comb_done, 1)

                for p in range(NIN):
                    if p < NIN - 1:
                        split(n0 + 3 + p)
                    if l == 0 and p == 0:
                        setup()
                    if l == 0 and p == 4:
                        setup_lambda()
                    if p == 1:
                        glu()
                    if p == 4:
                        latents()
                    if p == 5:
                        dve.wait_ge(mid_mm, MID * l + 5)
                        mids(V.tensor_tensor(kr[:], kr[:], cos, ALU.mult))
                        mids(V.tensor_tensor(rot[:, 0, :], bank[0][0:QD, 0:T], sin, ALU.mult))
                        dve.wait_ge(mid_dve, ms_[0])
                        mids(V.tensor_tensor(kr[:], kr[:], rot[:, 0, :], ALU.add))
                    if p == 7:
                        maxima(0)
                    if p in ROPE_AT:
                        rope_q(ROPE_AT[p])
                    if p == 8:
                        combine(0)
                    taps(TAPS_AT[p])

                for k in range(SLOTS + 3):
                    if 1 <= k < SLOTS:
                        maxima(k)
                    if 0 <= k - 2 < HEADS:
                        dve.wait_ge(pt_mm, SLOTS * l + k - 1)
                        if SLOTS * l + k - 2 >= 2:
                            dve.wait_ge(pv_mm, SLOTS * l + k - 3)
                        V.tensor_copy(pt_sb[:, k % 2, :], bank[T_BANK[k % 2]][:, 0:3 * P]).then_inc(pt_diff, 1)
                    if 2 <= k <= SLOTS:
                        combine(k - 1)
                    j = (k - 7) // 2
                    if k % 2 == 1 and 0 <= j < 3:
                        dve.wait_ge(cat_hi["diff"], 3 * l + j + 1)
                        V.tensor_tensor(hT_lo[:, 5 + j, :], o_y, hT_hi[:, 5 + j, :].bitcast(F32), ALU.subtract
                                        ).then_inc(cat_lo["diff"], 1)
                    j = (k - 6) // 2
                    if k % 2 == 0 and 0 <= j < 3:
                        dve.wait_ge(o_rs_done, 3 * l + j + 1)
                        if 3 * l + j > 0:
                            dve.wait_ge(cat_lo["diff"], 3 * l + j)
                        V.scalar_tensor_tensor(o_y, bank[O_BANK[j % 2]][:, 0:T], sub_g[:, l:l + 1], o_rs,
                                               ALU.mult, ALU.mult).then_inc(o_normed, 1)
                    j = (k - 4) // 2
                    if k % 2 == 0 and 3 <= j < 6:
                        dve.wait_ge(cat_hi["mla"], 3 * l + j - 2)
                        V.tensor_tensor(hT_lo[:, 2 + 5 - j, :], bank[O_BANK[j % 2]][:, 0:T],
                                        hT_hi[:, 2 + 5 - j, :].bitcast(F32), ALU.subtract).then_inc(cat_lo["mla"], 1)
                    if k == 1:
                        join_taps()
                    if k == 13:
                        for c in range(2):
                            dve.wait_ge(cat_hi["conv"], 2 * l + 2)
                            V.scalar_tensor_tensor(hT_lo[:, c, :], bank[7][:, c * T:(c + 1) * T],
                                                   vecs[:, V_BPW + 2 * l + c:V_BPW + 2 * l + c + 1],
                                                   hT_hi[:, c, :].bitcast(F32), ALU.add, ALU.subtract
                                                   ).then_inc(cat_lo["conv"], 1)
                    if k == 13:
                        split(n0 + 11)
                    if k == 4:
                        dve.wait_ge(mid_mm, MID * l + 14)
                        mean = bank[7][:, 0:T].unsqueeze(1).broadcast_to([P, 2, T])
                        conv(V.scalar_tensor_tensor(cv[:, 1], mean, -1.0 / CONV, cv[:, 0], ALU.mult, ALU.add))
                    if k == 8:
                        dve.wait_ge(conv_act, CA * l + 4)
                        conv(V.tensor_tensor(cv[:, 0], cv[:, 1], ln_rs[:].unsqueeze(1).broadcast_to([P, 2, T]), ALU.mult))
                        dve.wait_ge(conv_step, cs[0])
                        for c in range(2):
                            conv(V.tensor_scalar(glu_a[:, c, :], cv[:, 0, c, :],
                                                 vecs[:, V_LNG + 2 * l + c:V_LNG + 2 * l + c + 1],
                                                 vecs[:, V_LNB + 2 * l + c:V_LNB + 2 * l + c + 1], ALU.mult, ALU.add))
                    if k == 11:
                        dve.wait_ge(sigmoid, 4 * l + 4)
                        dve.wait_ge(conv_step, cs[0])
                        conv(V.tensor_tensor(glu_a[:], glu_a[:], glu_e[:], ALU.mult))
                split(n0 + 12)
                f0 = n0 + NIN + NOUT
                if l == 0:
                    split(f0)
                else:
                    split_expert(0, 0)
                update_and_norm(2 * l + 1, lambda q: add_to_x(q, out_done(l), 2 * l, [bank[b] for b in OUT_BANK]))
                if l == 0:
                    norm_evac(1, V_FFN)
                    split(f0 + 1)
                    for j, (kind, c) in enumerate(ORDER):
                        if j + 2 < NFF:
                            split(f0 + j + 2)
                        if kind == "U":
                            for f in range(2):
                                dve.wait_ge(sg_done, 2 * c + f + 1)
                                if c >= 2:
                                    dve.wait_ge(act_lo, 2 * (c - 2) + f + 1)
                                V.tensor_tensor(d_prod[:, c % 2, f, :], bank[(c % 2) * 2 + f][:, T:2 * T],
                                                d_sg[:, c % 2, f, :], ALU.mult).then_inc(prod_done, 1)
                            for f in range(2):
                                dve.wait_ge(act_hi, 2 * c + f + 1)
                                V.tensor_tensor(d_lo[:, c % 2, f, :], d_prod[:, c % 2, f, :],
                                                d_hi[:, c % 2, f, :].bitcast(F32), ALU.subtract).then_inc(act_lo, 1)
                    split(LAYER_PIECE0[1])
                    update_and_norm(2, lambda q: add_to_x(q, dense_done("D", NCH - 1), 1, bank[4:8]))
                else:
                    norm_evac(3, V_FFN + KT)

            def split_rows(t):
                dve.wait_ge(ht_split, t + 1)
                V.tensor_tensor(ht_lo[:, t, :], xn[:, t, :], ht_hi[:, t, :].bitcast(F32), ALU.subtract
                                ).then_inc(ht_lo_done, 1)

            rv = [0]

            def step(ins, wait=True):
                rv[0] += 1
                ins.then_inc(route_v, 1)
                if wait:
                    dve.wait_ge(route_v, rv[0])

            dve.wait_ge(route_mm, 1)
            parts = bank[4][:, T:T + TT * 2 * NE].rearrange("p (t m e) -> p t m e", t=TT, m=2)
            step(V.tensor_copy(lg[:], parts[:, :, 1]))
            step(V.tensor_tensor(lg[:], lg[:], parts[:, :, 0], ALU.add))
            for t in range(TT):
                step(V.max(m8[:, t, :], lg[:, t, :]), wait=t == TT - 1)
            step(V.tensor_tensor(gap[:], m8[:, :, 1], m8[:, :, 0], ALU.subtract), wait=False)
            assert rv[0] == RV_GAP
            for t in range(TT):
                step(V.max_index(idx[:, t, :], m8[:, t, :], lg[:, t, :]), wait=t == TT - 1)
            step(V.tensor_copy(idf[:], idx[:]))
            for t in range(TT):
                for m in range(2):
                    step(V.tensor_scalar(oh[:, m, t, :], iota[:, 0:NE], idf[:, t, m:m + 1], None, ALU.is_equal),
                         wait=False)
            dve.wait_ge(route_v, rv[0])
            step(V.tensor_tensor(chosen[:], oh[:, 0], oh[:, 1], ALU.add))
            assert rv[0] == RV_CHOSEN
            step(V.tensor_scalar(less1[:], chosen[:].bitcast(F32), -1.0, None, ALU.add), wait=False)
            step(V.memset(pos_item[:], -1.0), wait=False)
            step(V.memset(g_item[:], 0.0))
            dve.wait_ge(route_mm, 2)
            step(V.tensor_tensor(pos[:], bank[5][:, 0:TT * NE].rearrange("p (t e) -> p t e", t=TT), chosen[:].bitcast(F32),
                                 ALU.mult))
            step(V.tensor_tensor(pos_item[:, :, 0:NE], pos[:], less1[:], ALU.add))

            def make_onehot(i):
                V.tensor_copy(p_col[:], pos_item[:, :, bass.ds(i, 1)].rearrange("p t o -> p (t o)")
                              ).then_inc(onehot_done, 1)
                dve.wait_ge(onehot_done, 1 + i * 3)
                for t in range(TT):
                    V.tensor_scalar(onehot[:, t, :], iota, p_col[:, t:t + 1], None, ALU.is_equal
                                    ).then_inc(onehot_done, 1)

            make_onehot(0)
            for t in range(TT):
                split_rows(t)
            split_expert(0, 1)
            dve.wait_ge(route_a, 1)
            step(V.tensor_scalar(w_top[:, 2, :], e2[:], 1.0, None, ALU.add))
            step(V.reciprocal(w_top[:, 0, :], w_top[:, 2, :]))
            step(V.tensor_tensor(w_top[:, 1, :], e2[:], w_top[:, 0, :], ALU.mult))
            for t in range(TT):
                for m in range(2):
                    step(V.tensor_scalar(gw[:, m, t, :], oh[:, m, t, :], w_top[:, m, t:t + 1], None, ALU.mult),
                         wait=False)
            step(V.tensor_copy(cnt[:], bank[5][:, TT * NE:3 * NE]))
            step(V.tensor_tensor(g_item[:, :, 0:NE], gw[:, 0], gw[:, 1], ALU.add), wait=False)
            step(V.tensor_scalar(over[:], cnt[:], float(P), None, ALU.is_gt))
            step(V.tensor_tensor_scan(incl[:], ones[:, 0:NE], over[:], 0.0, ALU.mult, ALU.add))
            step(V.tensor_scalar(pos_hi[:], pos_item[:, :, 0:NE], -float(P), None, ALU.add), wait=False)
            step(V.tensor_tensor(rank[:], incl[:], over[:], ALU.subtract))
            for j in range(3):
                step(V.scalar_tensor_tensor(sel[:, j, :], rank[:], float(j), over[:], ALU.is_equal, ALU.mult),
                     wait=False)
            step(V.tensor_scalar(it_f[:, 0:1], incl[:, NE - 1:NE], float(NE), None, ALU.add))
            m = 0
            for j in range(3):
                for t in range(TT):
                    for src, dst in ((pos_hi, pos_item), (g_item, g_item)):
                        step(V.tensor_tensor_reduce(junk[:, m, :], sel[:, j, :], src[:, t, 0:NE], 1.0, 0.0, ALU.mult,
                                                    ALU.add, dst[:, t, NE + j:NE + j + 1]), wait=False)
                        m += 1
                step(V.tensor_tensor_reduce(junk[:, m, :], sel[:, j, :], iota[:, 0:NE], 1.0, 0.0, ALU.mult, ALU.add,
                                            it_f[:, 1 + j:2 + j]), wait=False)
                m += 1
            dve.wait_ge(route_v, rv[0])
            V.tensor_copy(it_i[:], it_f[:]).then_inc(items_ready, 1)

            def scatter_add(items, q):
                t, n = q // 2, q % 2
                dve.wait_ge(scat_mm[q], items)
                dve.wait_ge(x_upd, XU0 - 7 + q + 4 * items)
                xs = x[:, t, n * 512:(n + 1) * 512]
                V.scalar_tensor_tensor(xs, bank[6 + q % 2][:], g_col[:, t:t + 1], xs, ALU.mult, ALU.add
                                       ).then_inc(x_upd, 1)

            def item(i, more, first=False):
                for j, (kind, c) in enumerate(ORDER):
                    if j + 2 < NFF or more is True:
                        split_expert(i, j + 2)
                    else:
                        with dve.If(more):
                            split_expert(i, j + 2)
                    if kind == "U":
                        dve.wait_ge(sg_done, GU0 + c + 1 + i * NCH)
                        if c >= 2:
                            dve.wait_ge(act_t, c - 1 + i * NCH)
                        V.tensor_tensor(m_prod[:, c % 2, :], bank[c % 2][:, FC:2 * FC], m_sg[:, c % 2, :],
                                        ALU.mult).then_inc(prod_done, 1)
                    tc = transposed_after(kind, c)
                    if tc is not None:
                        dve.wait_ge(act_hi, GU0 + tc + 1 + i * NCH)
                        V.tensor_tensor(m_lo[:, tc % 2, :, :], bank[2 + tc % 2][:, 0:2 * P].rearrange("p (f s) -> p f s", f=2),
                                        m_hi[:, tc % 2, :, :].bitcast(F32), ALU.subtract).then_inc(act_lo, 1)
                    if not first and c <= 1 and kind == ("U", "G")[c]:
                        scatter_add(i, 2 * c)
                        scatter_add(i, 2 * c + 1)
                    if kind == "U" and c == 5:
                        dve.wait_ge(onehot_tmm, i + 1)
                        dve.wait_ge(x_upd, XU0 + 4 * i)
                        V.tensor_copy(g_col[:], g_item[:, :, bass.ds(i, 1)].rearrange("p t o -> p (t o)")
                                      ).then_inc(route_v, 1)
                        dve.wait_ge(gather_mm, 4 + 4 * i)
                        dve.wait_ge(onehot_done, 3 + 3 * i)
                        make_onehot(i + 1)
                        dve.wait_ge(route_v, rv[0] + 1 + i)
                for h in range(2):
                    dve.wait_ge(yhi_done, 2 * i + 1 + h)
                    V.tensor_tensor(y_lo[:, h * 512:(h + 1) * 512], bank[4 + h][:],
                                    y_hi[:, h * 512:(h + 1) * 512].bitcast(F32), ALU.subtract).then_inc(ylo_done[h], 1)

            item(0, True, first=True)
            n_items = dve.value_load(it_i[0:1, 0:1], min_val=NE, max_val=ITEMS_MAX)
            with dve.Fori(1, n_items) as i:
                item(i, i < n_items - 1)
            dve.wait_ge(gfin_in, 32)
            update_and_norm(2 * LAYERS, lambda q: scatter_add(n_items, q))

        @block.tensor
        def _(pe):
            M = nc.tensor.matmul

            def mm3(o, lh, ll, rh, rl, start, stop):
                M(o, lh, rh, start=start, stop=False)
                M(o, lh, rl, start=False, stop=False)
                return M(o, ll, rh, start=False, stop=stop)

            def norm_transposes(j):
                for t in range(TT):
                    pe.wait_ge(xn_ready, TT * j + t + 1)
                    for b in range(4):
                        for kk in range(2):
                            k = 2 * b + kk
                            r = nc.tensor.transpose(bank[b][:, kk * T + t * P:kk * T + (t + 1) * P],
                                                    xn[:, t, k * P:(k + 1) * P], ident)
                        if t == TT - 1:
                            r.then_inc(hT_mm, 1)

            pe.wait_ge(early_in, 16 * N_EARLY)
            pe.wait_ge(const_set, N_CONST)
            for l in range(LAYERS):
                n0 = LAYER_PIECE0[l]
                if l == 0:
                    nc.tensor.transpose(bank[4][:, 0:V_END], vec_rows[:], ident[0:V_END, 0:V_END]).then_inc(setup_t, 1)
                norm_transposes(2 * l)
                if l == 0:
                    pe.wait_ge(taps_in, 16)
                    nt = LAYERS * TAPS
                    for c in range(2):
                        r = nc.tensor.transpose(bank[7][:, c * nt:(c + 1) * nt], dw_rows[:, c * P:(c + 1) * P],
                                                ident[0:nt, 0:nt])
                    r.then_inc(setup_t, 1)

                def mid_start(g):
                    gp = g - 4
                    if gp in MID_ACT:
                        pe.wait_ge(mid_act, ACT_MID_STEPS * l + MID_ACT[gp])
                    else:
                        pe.wait_ge(mid_dve, DVE_MID_STEPS * l + MID_DVE[gp])

                def project(p):
                    n = n0 + p
                    pe.wait_ge(lo_ready, n + 1)
                    if p >= 4:
                        pe.wait_ge(proj_evac, NIN * l + p - 3)
                    elif l == 0 and p in (0, 3):
                        pe.wait_ge(setup_a, 1 if p == 0 else 2)
                    b = bank[4 + p % 4]
                    wh, wl = in_piece_view(hi_of(n), p), in_piece_view(lo_of(n), p)
                    if p < 7:
                        cols = [(0, P), (P, P)] if p != 3 else [(0, P), (KR - NOPE, QD)]
                        for m, (c0, cn) in enumerate(cols):
                            for k in range(KT):
                                if p == 0 and m == 0:
                                    pe.wait_ge(hTlo_done, KT * 2 * l + k + 1)
                                r = mm3(b[0:cn, m * T:(m + 1) * T], wh[:, k, c0:c0 + cn], wl[:, k, c0:c0 + cn],
                                        hT_hi[:, k, :], hT_lo[:, k, :], k == 0, k == KT - 1)
                    else:
                        for t in range(TT):
                            for k in range(KT):
                                tok = slice(t * P, (t + 1) * P)
                                r = mm3(b[:, t * 192:(t + 1) * 192], hT_hi[:, k, tok], hT_lo[:, k, tok],
                                        wh[:, k, :], wl[:, k, :], k == 0, k == KT - 1)
                    r.then_inc(piece_used, 1)

                def scores(k):
                    for u in units_of(k):
                        if u == 0:
                            pe.wait_ge(proj_evac, NIN * l + 7)
                        if u == 2:
                            pe.wait_ge(proj_evac, NIN * (l + 1))
                        if u >= 3:
                            pe.wait_ge(s_max, 2 * (UNITS * l + u - 2))
                        h, _ = head_of(k)
                        if k < HEADS:
                            r0 = (h % 2) * DV + (u % 2) * HD
                            q, kk = dqk[r0:r0 + HD, h // 2, :], dqk[r0:r0 + HD, 3 + h // 2, :]
                        else:
                            q, kk = q_m[:, h, :], k_m[:, h, :]
                        b = bank[S_BANK[u % 3]]
                        M(b[:, 0:P], q[:, 0:P], kk[:, 0:P], start=True, stop=True)
                        M(b[:, P:3 * P], q[:, P:2 * P], kk[:, :], start=True, stop=True).then_inc(s_mm, 1)

                for p in range(NIN):
                    project(p)
                    if p == 7:
                        scores(0)
                    if p == 4:
                        pe.wait_ge(proj_evac, NIN * l + 4)
                        for c in range(2):
                            M(bank[0][:, 0:T], ones[:], sq_q[:, c, :], start=c == 0, stop=c == 1)
                        M(bank[0][:, T:2 * T], ones[:], sq_kv[:], start=True, stop=True).then_inc(mid_mm, 1)
                    if p == 5:
                        pe.wait_ge(small_in, 48 * (l + 1))
                        pe.wait_ge(mid_dve, DVE_MID_STEPS * l + 3)
                        for r3 in range(3):
                            for hh in range(2):
                                h = 2 * r3 + hh
                                for c in range(2):
                                    r = M(bank[1 + r3][0:QD, hh * T:(hh + 1) * T], w_uq[:, c, h * QD:(h + 1) * QD],
                                          cq[:, c, :], start=c == 0, stop=c == 1)
                            r.then_inc(mid_mm, 1)
                        mid_start(4)
                        M(bank[0][0:QD, 0:T], rotate, kr[:], start=True, stop=True).then_inc(mid_mm, 1)
                    if p == 6:
                        for t in range(TT):
                            mid_start(5 + t)
                            wv = w_ukv[:].rearrange("p (h n) -> p h n", h=HEADS)[:, :, NOPE:]
                            M(bank[1 + t][:, 0:HEADS * MV], ckv[:, t * P:(t + 1) * P], wv, start=True, stop=True
                              ).then_inc(mid_mm, 1)
                    if p in ROPE_AT:
                        for r3 in ROPE_AT[p]:
                            mid_start(7 + r3)
                            M(bank[MID_BANK[7 + r3]][0:QD, :], rotate,
                              q_m[:, 2 * r3:2 * r3 + 2, :].rearrange("p h t -> p (h t)"), start=True, stop=True
                              ).then_inc(mid_mm, 1)
                    if p in KEYS_AT:
                        for r3 in KEYS_AT[p]:
                            mid_start(10 + r3)
                            for hh in range(2):
                                h = 2 * r3 + hh
                                r = M(bank[MID_BANK[10 + r3]][0:NOPE, hh * T:(hh + 1) * T],
                                      w_ukv[:, h * KVD:h * KVD + NOPE], ckv[:], start=True, stop=True)
                            r.then_inc(mid_mm, 1)
                def wait_slot(diff, mla, k):
                    if k < HEADS:
                        pe.wait_ge(diff, HEADS * l + k + 1)
                    else:
                        pe.wait_ge(mla, HEADS * l + k - HEADS + 1)

                def transposes(k):
                    wait_slot(scaled_diff, scaled_mla, k)
                    if k == 0:
                        pe.wait_ge(mid_dve, DVE_MID_STEPS * (l + 1))
                        pe.wait_ge(mid_act, ACT_MID_STEPS * (l + 1))
                    if k >= 2:
                        wait_slot(pt_diff, pt_mla, k - 2)
                    for b in range(3):
                        r = nc.tensor.transpose(bank[T_BANK[k % 2]][:, b * P:(b + 1) * P],
                                                e_sb[:, k % 3, 0, b * P:(b + 1) * P], ident)
                    r.then_inc(pt_mm, 1)

                def values(k):
                    _, r3 = head_of(k)
                    j, odd = k // 2, k % 2
                    wait_slot(pt_diff, pt_mla, k)
                    if k == 0:
                        pe.wait_ge(const_set, N_CONST + 3 * (l + 1))
                    if not odd and 2 <= j <= 4:
                        pe.wait_ge(o_normed, 3 * l + j - 1)
                    elif not odd and j == 5:
                        pe.wait_ge(cat_lo["mla"], 3 * l + 1)
                    v = (dv if k < HEADS else v_m)[:, :, r3, odd * DV:odd * DV + P]
                    o, pt = bank[O_BANK[j % 2]], pt_sb[:, k % 2, :]
                    if not odd:
                        M(o[:, 0:T], v[:, 0, :], pt[:, 0:T], start=True, stop=False)
                        r = M(o[:, P:T], v[:, 1, :], pt[:, T:3 * P], start=False, stop=False)
                    else:
                        M(o[:, P:T], v[:, 1, :], pt[:, T:3 * P], start=False, stop=False)
                        r = M(o[:, 0:T], v[:, 0, :], pt[:, 0:T], start=False, stop=True)
                    r.then_inc(pv_mm, 1)

                def output(i):
                    n = n0 + NIN + i
                    pe.wait_ge(lo_ready, n + 1)
                    for g, count in (("diff", 3), ("mla", 1), ("conv", 2), ("mla", 3))[i:i + 1]:
                        pe.wait_ge(cat_lo[g], {"diff": 3, "conv": 2, "mla": 3}[g] * l + count)
                    wh, wl = ff_view(hi_of(n), "D"), ff_view(lo_of(n), "D")
                    last = i == NOUT - 1
                    order = [(kk, q) for q in range(4) for kk in range(2)] if last else \
                            [(kk, q) for kk in range(2) for q in range(4)]
                    for kk, q in order:
                        k, t, nn = 2 * OUT_ORDER[i] + kk, q // 2, q % 2
                        if i == 0 and kk == 0 and q == 2:
                            pe.wait_ge(s_max, 2 * UNITS * (l + 1))
                        if i == 0 and kk == 0 and q == 3:
                            wait_slot(pt_diff, pt_mla, SLOTS - 2)
                        r = mm3(bank[OUT_BANK[q]][:], hT_hi[:, k, t * P:(t + 1) * P], hT_lo[:, k, t * P:(t + 1) * P],
                                wh[:, kk, nn * 512:(nn + 1) * 512], wl[:, kk, nn * 512:(nn + 1) * 512],
                                i == 0 and kk == 0, last and kk == 1)
                        if last and kk == 1 and q < 3:
                            r.then_inc(acc_part, 1)
                    r.then_inc(piece_used, 1)

                scores(1)
                for k in range(SLOTS + 1):
                    if k + 2 < SLOTS:
                        scores(k + 2)
                    if k == SLOTS:
                        pe.wait_ge(conv_step, CS * (l + 1))
                        for m in range(2):
                            for c in range(2):
                                r = M(bank[7][:, m * T:(m + 1) * T], w_pw[:, c, m * P:(m + 1) * P], glu_a[:, c, :],
                                      start=c == 0, stop=c == 1)
                        r.then_inc(mid_mm, 1)
                    if k >= SLOTS - 1:
                        output(k - SLOTS + 1)
                    j = (k - 3) // 2
                    if k % 2 == 1 and 0 <= j < 3:
                        pe.wait_ge(o_squared, 3 * l + j + 1)
                        M(bank[O_BANK[j % 2]][:, T:2 * T], blocks, o_sq, start=True, stop=True).then_inc(o_ss_mm, 1)
                    if k >= 1:
                        values(k - 1)
                    if k < SLOTS:
                        transposes(k)
                    if k == 2:
                        pe.wait_ge(conv_step, CS * l + CS_TAPS)
                        for c in range(2):
                            r = M(bank[7][:, 0:T], ones[:], cv[:, 0, c, :], start=c == 0, stop=c == 1)
                        r.then_inc(mid_mm, 1)
                    if k == 5:
                        pe.wait_ge(conv_act, CA * l + 2)
                        for c in range(2):
                            r = M(bank[7][:, 0:T], ones[:], glu_e[:, c, :], start=c == 0, stop=c == 1)
                        r.then_inc(mid_mm, 1)
                for i in range(2, NOUT):
                    output(i)
                norm_transposes(2 * l + 1)
                if l == 0:
                    f0 = n0 + NIN + NOUT
                    for j, (kind, c) in enumerate(ORDER):
                        n = f0 + j
                        pe.wait_ge(lo_ready, n + 1)
                        wh, wl = ff_view(hi_of(n), kind), ff_view(lo_of(n), kind)
                        if kind == "D":
                            pe.wait_ge(act_lo, 2 * c + 2)
                            last = c == NCH - 1
                            order = [(f, q) for q in range(4) for f in range(2)] if last else \
                                    [(f, q) for f in range(2) for q in range(4)]
                            for f, q in order:
                                t, nn = q // 2, q % 2
                                tok = slice(t * P, (t + 1) * P)
                                r = mm3(bank[4 + q][:], d_hi[:, c % 2, f, tok], d_lo[:, c % 2, f, tok],
                                        wh[:, f, nn * 512:(nn + 1) * 512], wl[:, f, nn * 512:(nn + 1) * 512],
                                        c == 0 and f == 0, last and f == 1)
                                if last and f == 1 and q < 3:
                                    r.then_inc(acc_part, 1)
                            r.then_inc(piece_used, 1)
                        else:
                            if kind == "G" and c >= 2:
                                pe.wait_ge(prod_done, 2 * (c - 1))
                            for f in range(2):
                                o = bank[(c % 2) * 2 + f][:, 0:T] if kind == "G" else bank[(c % 2) * 2 + f][:, T:2 * T]
                                for k in range(KT):
                                    if j == 0 and f == 0:
                                        pe.wait_ge(hTlo_done, KT + max(k + 1, 2))
                                    r = mm3(o, wh[:, k, f * P:(f + 1) * P], wl[:, k, f * P:(f + 1) * P],
                                            hT_hi[:, k, :], hT_lo[:, k, :], k == 0, k == KT - 1)
                            r.then_inc(piece_used, 1)
            pe.wait_ge(setup_v, SETUP_V)
            for k in range(KT):
                pe.wait_ge(hTlo_done, 3 * KT + k + 1)
                w = wr_parts[:, k].rearrange("p m e -> p (m e)")
                M(bank[4][0:2 * NE, 0:T], w, hT_hi[:, k, :], start=k == 0, stop=False)
                r = M(bank[4][0:2 * NE, 0:T], w, hT_lo[:, k, :], start=False, stop=k == KT - 1)
            r.then_inc(logits_mm, 1)
            pe.wait_ge(logits_out, 1)
            for t in range(TT):
                r = nc.tensor.transpose(bank[4][:, T + t * 2 * NE:T + (t + 1) * 2 * NE], lg_t[:, t * P:(t + 1) * P],
                                        ident[0:2 * NE, 0:2 * NE])
            r.then_inc(route_mm, 1)
            pe.wait_ge(route_v, RV_CHOSEN)
            M(bank[5][:, 0:NE], upper_r[:], chosen[:, 0, :], start=True, stop=True)
            M(bank[5][:, NE:2 * NE], ones_r[:], chosen[:, 0, :], start=True, stop=False)
            M(bank[5][:, NE:2 * NE], upper_r[:], chosen[:, 1, :], start=False, stop=True)
            M(bank[5][:, 2 * NE:3 * NE], ones_r[:], chosen[:, 0, :], start=True, stop=False)
            M(bank[5][:, 2 * NE:3 * NE], ones_r[:], chosen[:, 1, :], start=False, stop=True).then_inc(route_mm, 1)

            def gather(i, first=False):
                pe.wait_ge(onehot_done, 3 + 3 * i)
                for src, b0, parts_done in ((ht_hi, 6, ht_split), (ht_lo, 0, ht_lo_done)):
                    if first:
                        pe.wait_ge(parts_done, TT)
                    for h in range(2):
                        for kk in range(4):
                            k = 4 * h + kk
                            for t in range(TT):
                                r = M(bank[b0 + h][:, kk * P:(kk + 1) * P], src[:, t, k * P:(k + 1) * P],
                                      onehot[:, t, :], start=t == 0, stop=t == TT - 1)
                        r.then_inc(gather_mm, 1)

            def scatter(items, q):
                t, n = q // 2, q % 2
                if q < 2:
                    pe.wait_ge(ylo_done[n], items)
                else:
                    pe.wait_ge(x_upd, XU0 + q - 5 + 4 * items)
                b = bank[6 + q % 2]
                M(b[:], onehot_t[:, t, :], y_hi[:, n * 512:(n + 1) * 512], start=True, stop=False)
                M(b[:], onehot_t[:, t, :], y_lo[:, n * 512:(n + 1) * 512], start=False, stop=True
                  ).then_inc(scat_mm[q], 1)

            def transpose_act(i, c):
                pe.wait_ge(prod_done, GU0 + c + 1 + i * NCH)
                pe.wait_ge(act_lo, GU0 + c - 1 + i * NCH)
                for f in range(2):
                    r = nc.tensor.transpose(bank[2 + c % 2][:, f * P:(f + 1) * P], m_prod[:, c % 2, f * P:(f + 1) * P],
                                            ident)
                r.then_inc(act_t, 1)

            def item(i, first=False):
                for j, (kind, c) in enumerate(ORDER):
                    pe.wait_ge(lo_ready, NA + j + 1 + i * NFF)
                    wh, wl = ff_view(hi_of(NA + j), kind), ff_view(lo_of(NA + j), kind)
                    if kind == "D":
                        if c == NCH - 1:
                            transpose_act(i, c)
                            pe.wait_ge(onehot_tdone, i + 1)
                            gather(i + 1)
                        pe.wait_ge(act_lo, GU0 + c + 1 + i * NCH)
                        for f in range(2):
                            for n in range(2):
                                r = mm3(bank[4 + n][:], m_hi[:, c % 2, f, :], m_lo[:, c % 2, f, :],
                                        wh[:, f, n * 512:(n + 1) * 512], wl[:, f, n * 512:(n + 1) * 512],
                                        c == 0 and f == 0, c == NCH - 1 and f == 1)
                    else:
                        if kind == "G" and c >= 2:
                            pe.wait_ge(prod_done, GU0 + c - 1 + i * NCH)
                        o = bank[c % 2][:, 0:FC] if kind == "G" else bank[c % 2][:, FC:2 * FC]
                        for k in range(KT):
                            if kind == "G" and c == 0 and k % 4 == 0:
                                pe.wait_ge(gathered, 3 + k // 4 + 4 * i)
                            r = mm3(o, sel_hi[:, k, :], sel_lo[:, k, :], wh[:, k, :], wl[:, k, :], k == 0, k == KT - 1)
                    r.then_inc(piece_used, 1)
                    if kind == "G" and c >= 1:
                        transpose_act(i, c - 1)
                    if not first and c <= 1 and kind == ("U", "G")[c]:
                        scatter(i, 2 * c)
                        scatter(i, 2 * c + 1)
                    if kind == "G" and c == 2:
                        pe.wait_ge(x_upd, XU0 + 4 * i)
                        for t in range(TT):
                            r = nc.tensor.transpose(bank[6][:, t * P:(t + 1) * P], onehot[:, t, :].bitcast(F32), ident)
                        r.then_inc(onehot_tmm, 1)

            gather(0, first=True)
            item(0, first=True)
            pe.wait_ge(items_ready, 1)
            n_items = pe.value_load(it_i[0:1, 0:1], min_val=NE, max_val=ITEMS_MAX)
            with pe.Fori(1, n_items) as i:
                item(i)
            for q in range(4):
                scatter(n_items, q)


_INS = ["x", "attn_norm", "w_in", "b_glu", "w_dw", "b_dw", "conv_ln_g", "conv_ln_b", "w_pw", "b_pw", "q_norm", "w_uq",
        "kv_norm", "w_ukv", "lambda_q1", "lambda_k1", "lambda_q2", "lambda_k2", "diff_subln", "w_out", "ffn_norm",
        "w_gate_dense", "w_up_dense", "w_down_dense", "w_router", "w_gate_exp", "w_up_exp", "w_down_exp", "final_norm"]


def kernel(**inputs):
    import concourse.bacc as bacc
    from concourse.bass_utils import run_bass_kernel_spmd as run

    nc = bacc.Bacc("TRN2", target_bir_lowering=False, num_devices=1)
    arrays = {name: np.ascontiguousarray(inputs[name]) for name in _INS}
    arrays["table1"], arrays["table2"] = tables()
    a = {name: nc.dram_tensor(f"in_{name}", v.shape, F32, kind="ExternalInput").ap() for name, v in arrays.items()}
    out = nc.dram_tensor("out", (1, T, D), F32, kind="ExternalOutput").ap()
    build(nc, a, out)
    r = run(nc, [{f"in_{name}": v for name, v in arrays.items()}], core_ids=[0])
    return r.results[0]["out"]
```
